# Optimizing a Trainium2 kernel written in Bass

```python
import math
import jax
import jax.numpy as jnp
from jax import lax
import numpy as np

D_MODEL = 1024
BATCH = 1
SEQ = 512
DEPTH = 1

HEAD_DIM = 64
NSA_HEADS = 8
NSA_KV_HEADS = 2
NSA_REP = NSA_HEADS // NSA_KV_HEADS
CMP_LEN = 32
CMP_STRIDE = 16
CMP_HID = 256
SEL_LEN = 64
SEL_TOPN = 16
WINDOW = 512
SEL_FORCE = 1e4

MLA_HEADS = 8
Q_LORA = 256
KV_LORA = 128
QK_NOPE = 64
QK_ROPE = 32
V_DIM = 64
ROPE_THETA = 10000.0

N_BUCKETS = 32
MAX_DISTANCE = 2048

PEER_HEADS = 8
PEER_NKEYS = 128
PEER_EXPERTS = PEER_NKEYS * PEER_NKEYS
PEER_QDIM = 256
PEER_TOPK = 16
PEER_CHUNK = 128

Q_BLOCK = 128
EPS = 1e-6
NEG = -1e30

NSA_WIDTH = NSA_HEADS * HEAD_DIM
MLA_WIDTH = MLA_HEADS * V_DIM
KV_WIDTH = NSA_KV_HEADS * HEAD_DIM
IN_SIZES = (NSA_WIDTH,) + (KV_WIDTH,) * 6 + (3 * NSA_HEADS, Q_LORA, KV_LORA, QK_ROPE)
IN_TOTAL = NSA_WIDTH + 6 * KV_WIDTH + 3 * NSA_HEADS + Q_LORA + KV_LORA + QK_ROPE

kernel_name = "hymba_nsa_mla_peer_block"

def rmsnorm(x, g):
    xf = x.astype(jnp.float32)
    y = xf * lax.rsqrt(jnp.mean(xf * xf, axis=-1, keepdims=True) + EPS)
    return (y * g.astype(jnp.float32)).astype(x.dtype)

def split_columns(z):
    out, start = [], 0
    for size in IN_SIZES:
        out.append(z[..., start:start + size])
        start += size
    return out

def t5_bucket(dist):
    dist = jnp.maximum(dist, 0)
    max_exact = N_BUCKETS // 2
    d = jnp.maximum(dist, 1).astype(jnp.float32)
    large = max_exact + (jnp.log(d / max_exact) / math.log(MAX_DISTANCE / max_exact)
                         * (N_BUCKETS - max_exact)).astype(jnp.int32)
    return jnp.where(dist < max_exact, dist, jnp.minimum(large, N_BUCKETS - 1))

def rope(x, positions):
    half = QK_ROPE // 2
    inv = ROPE_THETA ** (-jnp.arange(half, dtype=jnp.float32) / half)
    ang = positions.astype(jnp.float32)[..., None] * inv
    if x.ndim == 4:
        ang = ang[:, :, None, :]
    cos, sin = jnp.cos(ang), jnp.sin(ang)
    xf = x.astype(jnp.float32)
    x1, x2 = xf[..., :half], xf[..., half:]
    return jnp.concatenate([x1 * cos - x2 * sin, x1 * sin + x2 * cos], axis=-1).astype(x.dtype)

def nsa_mixer(q, kc, vc, ks, vs, kw, vw, gates, cmp_pos, cmp_k_w1, cmp_k_w2, cmp_v_w1, cmp_v_w2, t5_bias):
    B, S = q.shape[0], q.shape[1]
    G, R, dh = NSA_KV_HEADS, NSA_REP, HEAD_DIM
    n_cmp = (S - CMP_LEN) // CMP_STRIDE + 1
    n_sel = S // SEL_LEN
    n_top = min(SEL_TOPN, n_sel)
    n_qb = S // Q_BLOCK
    wk = WINDOW + Q_BLOCK
    scale = dh ** -0.5

    cmp_start = jnp.arange(n_cmp) * CMP_STRIDE
    cmp_end = cmp_start + CMP_LEN - 1
    cidx = cmp_start[:, None] + jnp.arange(CMP_LEN)[None, :]

    def compress(raw, w1, w2):
        blk = raw[:, cidx] + cmp_pos[None, None, :, None, :]
        blk = jnp.moveaxis(blk, 3, 2).reshape(B, n_cmp, G, CMP_LEN * dh)
        return jax.nn.gelu(blk @ w1, approximate=False) @ w2

    k_cmp = compress(kc, cmp_k_w1, cmp_k_w2)
    v_cmp = compress(vc, cmp_v_w1, cmp_v_w2)

    sel_start = jnp.arange(n_sel) * SEL_LEN
    overlap = ((cmp_start[:, None] < sel_start[None, :] + SEL_LEN)
               & (cmp_end[:, None] >= sel_start[None, :])).astype(jnp.float32)
    ks_blk = ks.reshape(B, n_sel, SEL_LEN, G, dh).transpose(0, 3, 1, 2, 4)
    vs_blk = vs.reshape(B, n_sel, SEL_LEN, G, dh).transpose(0, 3, 1, 2, 4)
    gather_blocks = jax.vmap(jax.vmap(lambda blocks, idx: blocks[idx]))

    kw_pad = jnp.pad(kw, ((0, 0), (WINDOW, 0), (0, 0), (0, 0)))
    vw_pad = jnp.pad(vw, ((0, 0), (WINDOW, 0), (0, 0), (0, 0)))
    w_dist = WINDOW + jnp.arange(Q_BLOCK)[:, None] - jnp.arange(wk)[None, :]
    w_rel_ok = (w_dist >= 0) & (w_dist < WINDOW)
    w_bias = jnp.moveaxis(t5_bias[t5_bucket(w_dist)], -1, 0).reshape(G, R, Q_BLOCK, wk).astype(jnp.float32)

    bias_tbl = t5_bias.reshape(N_BUCKETS, G, R).astype(jnp.float32)
    g_ix = jnp.arange(G)[None, :, None, None]

    q_b = q.reshape(B, n_qb, Q_BLOCK, G, R, dh).transpose(1, 0, 3, 4, 2, 5)
    g_b = gates.reshape(B, n_qb, Q_BLOCK, G, R, 3).transpose(1, 0, 3, 4, 2, 5)

    def block(args):
        i, qi, gi = args
        t = i * Q_BLOCK + jnp.arange(Q_BLOCK)
        dist_c = t[:, None] - cmp_end[None, :]
        ok_c = dist_c >= 0
        bias_c = jnp.moveaxis(t5_bias[t5_bucket(dist_c)], -1, 0).reshape(G, R, Q_BLOCK, n_cmp).astype(jnp.float32)
        s_c = jnp.einsum('bgrqd,bkgd->bgrqk', qi, k_cmp).astype(jnp.float32) * scale + bias_c
        p_c = jax.nn.softmax(jnp.where(ok_c, s_c, NEG), axis=-1) * jnp.any(ok_c, axis=-1)[:, None]
        o_c = jnp.einsum('bgrqk,bkgd->bgrqd', p_c.astype(qi.dtype), v_cmp)
        imp = jnp.einsum('bgrqk,ks->bgqs', p_c, overlap)
        cur = t // SEL_LEN
        sid = jnp.arange(n_sel)[None, :]
        forced = (sid == 0) | (sid == cur[:, None]) | (sid == cur[:, None] - 1)
        imp = jnp.where(sid <= cur[:, None], imp + jnp.where(forced, SEL_FORCE, 0.0), NEG)
        _, sel = lax.top_k(imp, n_top)
        k_g = gather_blocks(ks_blk, sel).reshape(B, G, Q_BLOCK, n_top * SEL_LEN, dh)
        v_g = gather_blocks(vs_blk, sel).reshape(B, G, Q_BLOCK, n_top * SEL_LEN, dh)
        pos_g = (sel[..., None] * SEL_LEN + jnp.arange(SEL_LEN)).reshape(B, G, Q_BLOCK, n_top * SEL_LEN)
        dist_s = t[:, None] - pos_g
        bias_s = jnp.moveaxis(bias_tbl[t5_bucket(dist_s), g_ix], -1, 2)
        s_s = jnp.einsum('bgrqd,bgqkd->bgrqk', qi, k_g).astype(jnp.float32) * scale + bias_s
        p_s = jax.nn.softmax(jnp.where((dist_s >= 0)[:, :, None], s_s, NEG), axis=-1)
        o_s = jnp.einsum('bgrqk,bgqkd->bgrqd', p_s.astype(qi.dtype), v_g)
        k_w = lax.dynamic_slice_in_dim(kw_pad, i * Q_BLOCK, wk, axis=1)
        v_w = lax.dynamic_slice_in_dim(vw_pad, i * Q_BLOCK, wk, axis=1)
        ok_w = w_rel_ok & ((i * Q_BLOCK - WINDOW + jnp.arange(wk)) >= 0)[None, :]
        s_w = jnp.einsum('bgrqd,bkgd->bgrqk', qi, k_w).astype(jnp.float32) * scale + w_bias
        p_w = jax.nn.softmax(jnp.where(ok_w, s_w, NEG), axis=-1)
        o_w = jnp.einsum('bgrqk,bkgd->bgrqd', p_w.astype(qi.dtype), v_w)
        return gi[..., 0:1] * o_c + gi[..., 1:2] * o_s + gi[..., 2:3] * o_w

    out = lax.map(block, (jnp.arange(n_qb), q_b, g_b))
    return out.transpose(1, 0, 4, 2, 3, 5).reshape(B, S, NSA_WIDTH)

def mla_mixer(c_q, c_kv, k_rope_raw, positions, q_norm_g, w_q_up, kv_norm_g, w_kv_up):
    B, S = c_q.shape[0], c_q.shape[1]
    H = MLA_HEADS
    qh = (rmsnorm(c_q, q_norm_g) @ w_q_up).reshape(B, S, H, QK_NOPE + QK_ROPE)
    q_nope, q_rope = qh[..., :QK_NOPE], rope(qh[..., QK_NOPE:], positions)
    kv = (rmsnorm(c_kv, kv_norm_g) @ w_kv_up).reshape(B, S, H, QK_NOPE + V_DIM)
    k_nope, v = kv[..., :QK_NOPE], kv[..., QK_NOPE:]
    k_rope = rope(k_rope_raw, positions)
    scale = (QK_NOPE + QK_ROPE) ** -0.5
    n_qb = S // Q_BLOCK
    qn_b = q_nope.reshape(B, n_qb, Q_BLOCK, H, QK_NOPE).transpose(1, 0, 2, 3, 4)
    qr_b = q_rope.reshape(B, n_qb, Q_BLOCK, H, QK_ROPE).transpose(1, 0, 2, 3, 4)
    kpos = jnp.arange(S)

    def block(args):
        i, qn, qr = args
        s = (jnp.einsum('bqhd,bkhd->bhqk', qn, k_nope)
             + jnp.einsum('bqhd,bkd->bhqk', qr, k_rope)).astype(jnp.float32) * scale
        t = i * Q_BLOCK + jnp.arange(Q_BLOCK)
        p = jax.nn.softmax(jnp.where(kpos[None, :] <= t[:, None], s, NEG), axis=-1)
        return jnp.einsum('bhqk,bkhd->bqhd', p.astype(v.dtype), v)

    out = lax.map(block, (jnp.arange(n_qb), qn_b, qr_b))
    return out.transpose(1, 0, 2, 3, 4).reshape(B, S, MLA_WIDTH)

def peer_ffn(h, w_q, keys1, keys2, u, v):
    B, S, D = h.shape
    K = PEER_TOPK
    q = (h @ w_q).reshape(B, S, PEER_HEADS, 2, PEER_QDIM // 2)
    s1 = jnp.einsum('bshd,nd->bshn', q[..., 0, :], keys1).astype(jnp.float32)
    s2 = jnp.einsum('bshd,nd->bshn', q[..., 1, :], keys2).astype(jnp.float32)
    v1, i1 = lax.top_k(s1, K)
    v2, i2 = lax.top_k(s2, K)
    cand = (v1[..., :, None] + v2[..., None, :]).reshape(B, S, PEER_HEADS, K * K)
    cid = (i1[..., :, None] * PEER_NKEYS + i2[..., None, :]).reshape(B, S, PEER_HEADS, K * K)
    top, pos = lax.top_k(cand, K)
    eid = jnp.take_along_axis(cid, pos, axis=-1)
    gate = jax.nn.softmax(top, axis=-1).astype(h.dtype)
    n_ch = (B * S) // PEER_CHUNK
    h_c = h.reshape(n_ch, PEER_CHUNK, D)
    e_c = eid.reshape(n_ch, PEER_CHUNK, PEER_HEADS * K)
    g_c = gate.reshape(n_ch, PEER_CHUNK, PEER_HEADS * K)

    def chunk(args):
        hx, e, g = args
        act = jax.nn.gelu(jnp.einsum('cd,ced->ce', hx, u[e]), approximate=False)
        return jnp.einsum('ce,ced->cd', g * act, v[e])

    return lax.map(chunk, (h_c, e_c, g_c)).reshape(B, S, D)

def setup_inputs(seed: int = 0) -> dict:
    key = jax.random.key(seed)
    k = jax.random.split(key, 26)
    L = DEPTH

    def nrm(kk, shape, scale):
        return jax.random.normal(kk, shape, jnp.float32) * scale

    def gain(kk, shape):
        return 1.0 + 0.05 * jax.random.normal(kk, shape, jnp.float32)

    positions = (jnp.arange(SEQ, dtype=jnp.int32)[None, :]
                 + jax.random.randint(k[1], (BATCH, 1), 0, 4096, dtype=jnp.int32))
    return {
        "x": nrm(k[0], (BATCH, SEQ, D_MODEL), 1.0),
        "positions": positions,
        "norm1_g": gain(k[2], (L, D_MODEL)),
        "w_in": nrm(k[3], (L, D_MODEL, IN_TOTAL), D_MODEL ** -0.5),
        "cmp_pos": nrm(k[4], (L, CMP_LEN, HEAD_DIM), 0.1),
        "cmp_k_w1": nrm(k[5], (L, CMP_LEN * HEAD_DIM, CMP_HID), (CMP_LEN * HEAD_DIM) ** -0.5),
        "cmp_k_w2": nrm(k[6], (L, CMP_HID, HEAD_DIM), CMP_HID ** -0.5),
        "cmp_v_w1": nrm(k[7], (L, CMP_LEN * HEAD_DIM, CMP_HID), (CMP_LEN * HEAD_DIM) ** -0.5),
        "cmp_v_w2": nrm(k[8], (L, CMP_HID, HEAD_DIM), CMP_HID ** -0.5),
        "t5_bias": nrm(k[9], (N_BUCKETS, NSA_HEADS), 0.5),
        "q_norm_g": gain(k[10], (L, Q_LORA)),
        "w_q_up": nrm(k[11], (L, Q_LORA, MLA_HEADS * (QK_NOPE + QK_ROPE)), Q_LORA ** -0.5),
        "kv_norm_g": gain(k[12], (L, KV_LORA)),
        "w_kv_up": nrm(k[13], (L, KV_LORA, MLA_HEADS * (QK_NOPE + V_DIM)), KV_LORA ** -0.5),
        "grp_norm_nsa": gain(k[14], (L, NSA_WIDTH)),
        "grp_norm_mla": gain(k[15], (L, MLA_WIDTH)),
        "w_out": nrm(k[16], (L, NSA_WIDTH + MLA_WIDTH, D_MODEL), (NSA_WIDTH + MLA_WIDTH) ** -0.5),
        "norm2_g": gain(k[17], (L, D_MODEL)),
        "peer_wq": nrm(k[18], (L, D_MODEL, PEER_HEADS * PEER_QDIM), D_MODEL ** -0.5),
        "peer_keys1": nrm(k[19], (L, PEER_NKEYS, PEER_QDIM // 2), (PEER_QDIM // 2) ** -0.5),
        "peer_keys2": nrm(k[20], (L, PEER_NKEYS, PEER_QDIM // 2), (PEER_QDIM // 2) ** -0.5),
        "peer_u": nrm(k[21], (L, PEER_EXPERTS, D_MODEL), D_MODEL ** -0.5),
        "peer_v": nrm(k[22], (L, PEER_EXPERTS, D_MODEL), PEER_HEADS ** -0.5),
        "final_g": gain(k[23], (D_MODEL,)),
    }

def reference(x, positions, norm1_g, w_in, cmp_pos, cmp_k_w1, cmp_k_w2, cmp_v_w1, cmp_v_w2, t5_bias,
              q_norm_g, w_q_up, kv_norm_g, w_kv_up, grp_norm_nsa, grp_norm_mla, w_out, norm2_g,
              peer_wq, peer_keys1, peer_keys2, peer_u, peer_v, final_g):
    B, S, _ = x.shape
    for l in range(DEPTH):
        h = rmsnorm(x, norm1_g[l])
        cols = split_columns(h @ w_in[l])
        q, kc, vc, ks, vs, kw, vw = [c.reshape(B, S, -1, HEAD_DIM) for c in cols[:7]]
        gates = jax.nn.sigmoid(cols[7].astype(jnp.float32)).astype(x.dtype).reshape(B, S, NSA_HEADS, 3)
        c_q, c_kv, k_rope = cols[8], cols[9], cols[10]
        o_nsa = nsa_mixer(q, kc, vc, ks, vs, kw, vw, gates, cmp_pos[l], cmp_k_w1[l], cmp_k_w2[l],
                          cmp_v_w1[l], cmp_v_w2[l], t5_bias)
        o_mla = mla_mixer(c_q, c_kv, k_rope, positions, q_norm_g[l], w_q_up[l], kv_norm_g[l], w_kv_up[l])
        mixed = jnp.concatenate([rmsnorm(o_nsa, grp_norm_nsa[l]), rmsnorm(o_mla, grp_norm_mla[l])], axis=-1)
        x = x + mixed @ w_out[l]
        x = x + peer_ffn(rmsnorm(x, norm2_g[l]), peer_wq[l], peer_keys1[l], peer_keys2[l], peer_u[l], peer_v[l])
    return rmsnorm(x, final_g)


_drawn_inputs = setup_inputs


def setup_inputs(seed=0):
    import zlib

    import numpy as np

    out = dict(_drawn_inputs(seed))
    spreads = {}
    factors = {}
    for name, (base, spread) in spreads.items():
        noise = np.random.default_rng([zlib.crc32(name.encode()), seed]).standard_normal(out[name].shape)
        drawn = base * np.exp(spread * noise) if base else spread * noise
        out[name] = jnp.asarray(drawn.astype(out[name].dtype))
    for name, factor in factors.items():
        out[name] = (out[name] * factor).astype(out[name].dtype)
    return out
```

```python
from contextlib import ExitStack

import numpy as np

import concourse.bass as bass
from concourse import mybir

F32 = mybir.dt.float32
F32R = mybir.dt.float32r
BF16 = mybir.dt.bfloat16
I32 = mybir.dt.int32
U32 = mybir.dt.uint32
ALU = mybir.AluOpType
ACT = mybir.ActivationFunctionType
X = mybir.AxisListType.X

P = 128
D = 1024
S = 512
QT = S // P
KD = D // P
DH = 64
HEADS = 8
GROUPS = 2
NSA_W = HEADS * DH
CMP_LEN, CMP_STRIDE, CMP_HID = 32, 16, 256
N_CMP = (S - CMP_LEN) // CMP_STRIDE + 1
LP = CMP_LEN * DH // P
HT = CMP_HID // P
Q_LORA, KV_LORA, NOPE, ROPE = 256, 128, 64, 32
HALF = ROPE // 2
QK = NOPE + ROPE
MLA_SCALE = QK ** -0.5
NSA_SCALE = DH ** -0.5
EPS = 1e-6
NEG = -1e30
BUCKETS = 32
R_CQ, R_CKV, R_VS, R_VW, R_KR, R_G = 0, 256, 384, 512, 640, 672
ROW_W = 696
C_KC, C_VC, C_KS, C_KW, C_Q = 0, 1, 2, 3, 4
N_COLS = 8
BIAS_L = 1024
BIAS_W = 896
NKEYS = 128
TOPK = 16
PH = 8
EXP_BUF = 2
TWO_PI_HI = 6.28125
TWO_PI_MID = float(np.float32(0.0019350051879882812))
TWO_PI_LO = float(2 * np.pi - 6.28125 - 0.0019350051879882812)
ROUND = 12582912.0
PI_IN = 3.1415925


class Memory:
    pass


class Region:

    def __init__(self, nc, start, end):
        self.nc, self.at, self.end = nc, start, end

    def take(self, name, shape, dt=F32):
        size = int(np.prod(shape[1:])) * (2 if dt == BF16 else 4)
        tensor = self.nc.alloc_sbuf_tensor_at(name, shape, dt, offset=self.at)
        self.at += (size + 31) // 32 * 32
        assert self.at <= self.end, (name, self.at, self.end)
        return tensor


def project(nc, io, m, psum):
    with ExitStack() as ctx:
        sb = m.scratch().take

        def sem(name):
            return ctx.enter_context(nc.semaphore(name))

        xn = m.late().take("xn", [P, QT, D])
        early = m.early()
        hT = early.take("hT", [P, KD, S])
        w_rows = sb("w_rows", [P, KD, ROW_W])
        w_col = sb("w_col", [P, 2, KD, P])
        cT = sb("cT", [P, 2, S])
        pairs = m.mla_values().take("pairs", [P, 2, GROUPS, S])
        blk = sb("blk", [P, 2, LP, GROUPS, N_CMP])
        w1 = w_rows[:, :, :].rearrange("p k n -> p (k n)")[:, 0:LP * CMP_HID].rearrange(
            "p (l c) -> p l c", l=LP)
        w1v = early.take("w1v", [P, LP, CMP_HID])
        w2 = sb("w2", [P, 2, HT, DH])
        hid = sb("hid", [P, 2, HT, GROUPS * N_CMP])
        posT = sb("posT", [P, LP])
        g1 = sb("g1", [P, KD])
        qkvg = sb("qkvg", [P, 3])
        t5x = sb("t5x", [BUCKETS + 1, HEADS])
        onehot = sb("onehot", [BUCKETS + 1, BIAS_L])
        brow = sb("brow", [HEADS, BIAS_L])
        stat = sb("stat", [P, 4, 4])
        lat = sb("lat", [P, QT, 384])
        junk = sb("junk", [P, D])

        x_in = [sem(f"x_in{t}") for t in range(QT)]
        wr_in, small_in, w2_in, t5_in, up_in = sem("wr_in"), sem("small_in"), sem("w2_in"), sem("t5_in"), sem("up_in")
        wc_in = [sem("wc_in0"), sem("wc_in1")]
        w1_in, w1v_in = sem("w1_in"), sem("w1v_in")
        x_sq, x_var, x_std, x_rs, xn_ok = sem("x_sq"), sem("x_var"), sem("x_std"), sem("x_rs"), sem("xn_ok")
        xT_ok, h_ok = sem("xT_ok"), sem("h_ok")
        rows_mm, rows_a, rows_v = sem("rows_mm"), sem("rows_a"), sem("rows_v")
        cols_mm, cols_a, cols_v = sem("cols_mm"), sem("cols_a"), sem("cols_v")
        pair_ok, blk_ok, hid_mm, hid_ok, cmp_mm, cmp_ok = (
            sem("pair_ok"), sem("blk_ok"), sem("hid_mm"), sem("hid_ok"), sem("cmp_mm"), sem("cmp_ok"))
        lat_sq, lat_var, lat_std, lat_rs, lat_ok, latT_mm, latT_ok = (
            sem("lat_sq"), sem("lat_var"), sem("lat_std"), sem("lat_rs"), sem("lat_ok"), sem("latT_mm"), sem("latT_ok"))
        b_mm, b_row, b_out, b_rep, b_tile = sem("b_mm"), sem("b_row"), sem("b_out"), sem("b_rep"), sem("b_tile")
        neg_ok, eye_ok, ones_ok = sem("neg_ok"), sem("eye_ok"), sem("ones_ok")

        block = ctx.enter_context(nc.Block())

        @block.sync
        def _(sp):
            for t in range(QT):
                sp.dma_start(m.x[:, t, :], io.x.rearrange("(t p) d -> t p d", p=P)[t]).then_inc(x_in[t], 16)
            sp.dma_start(g1[:, :], io.g1).then_inc(small_in, 16)
            sp.dma_start(qkvg[:, :], io.qkvg).then_inc(small_in, 16)
            sp.dma_start(posT[:, :], io.cmp_posT).then_inc(small_in, 16)
            sp.dma_start(w_rows[:, :, :], io.w_rows).then_inc(wr_in, 16)
            for j in range(N_COLS):
                if j >= 2:
                    sp.wait_ge(cols_mm, j - 1)
                sp.dma_start(w_col[:, j % 2], io.w_cols[j]).then_inc(wc_in[j % 2], 16)
                if j == 1:
                    sp.dma_start(w1v[:, :, :], io.w1v).then_inc(w1v_in, 16)
                if j == 2:
                    sp.wait_ge(rows_mm, QT)
                    sp.dma_start(w1, io.w1k).then_inc(w1_in, 16)

        @block.gpsimd
        def _(pool):
            pool.memset(m.eye[:, :], 0.0).then_inc(eye_ok, 1)
            pool.wait_ge(eye_ok, 1)
            pool.affine_select(out=m.eye[:, :], in_=m.eye[:, :], compare_op=ALU.not_equal, fill=1.0,
                               base=0, pattern=[[-1, P]], channel_multiplier=1).then_inc(eye_ok, 1)
            pool.memset(m.mask[:, :], 0.0).then_inc(ones_ok, 1)
            pool.memset(m.seen[:, :], 1.0).then_inc(ones_ok, 1)
            pool.wait_ge(ones_ok, 2)
            pool.affine_select(out=m.mask[:, S - P:S], in_=m.mask[:, S - P:S], compare_op=ALU.is_ge, fill=NEG,
                               base=0, pattern=[[-1, P]], channel_multiplier=1)
            pool.affine_select(out=m.seen[:, :], in_=m.seen[:, :], compare_op=ALU.is_ge, fill=0.0,
                               base=-(CMP_LEN - 1), pattern=[[0, 1]], channel_multiplier=1).then_inc(ones_ok, 1)
            for c in range(2):
                pool.wait_ge(cols_a if c == 0 else cols_v, 1)
                for g in range(GROUPS):
                    src = cT[g * DH:(g + 1) * DH, c, :]
                    pool.dma_start(pairs[0:DH, c, g, :], src).then_inc(pair_ok, 16)
                    pool.dma_start(pairs[DH:P, c, g, 0:S - 1], src[:, 1:S]).then_inc(pair_ok, 16)
            pool.wait_ge(b_row, 1)
            pool.dma_start(io.bias_rows, brow[:, :]).then_inc(b_out, 16)
            pool.wait_ge(b_out, 16)
            pool.dma_start(io.bias_rep.rearrange("p (h n) -> p h n", h=HEADS),
                           io.bias_rows.partition_broadcast(P)).then_inc(b_rep, 16)
            pool.wait_ge(b_rep, 16)
            skew = bass.AP(tensor=io.bias_rep.tensor, offset=P - 1,
                           ap=[[HEADS * BIAS_L - 1, P], [BIAS_L, HEADS], [1, BIAS_W]])
            pool.dma_start(m.bias[:, :, :], skew).then_inc(b_tile, 16)
            pool.wait_ge(b_tile, 16)
            pool.wait_ge(pair_ok, 128)
            pool.wait_ge(ones_ok, 3)

        @block.scalar
        def _(act):
            act.dma_start(t5x[0:BUCKETS, :], io.t5).then_inc(t5_in, 16)
            act.dma_start(onehot[:, :], io.bucket_onehot).then_inc(t5_in, 16)
            act.dma_start(w2[:, :, :, :], io.w2).then_inc(w2_in, 16)
            act.dma_start(m.wq_up[:, :, :], io.wq_up).then_inc(up_in, 16)
            act.dma_start(m.wkv_up[:, :], io.wkv_up).then_inc(up_in, 16)
            act.dma_start(m.inv[:, :], io.inv_freq.partition_broadcast(P)).then_inc(up_in, 16)
            act.dma_start(m.pos[:, :], io.positions).then_inc(up_in, 16)
            for t in range(QT):
                act.wait_ge(x_in[t], 16)
                act.activation(xn[:, t, :], m.x[:, t, :], ACT.Square, accum_out=stat[:, 0, t:t + 1]).then_inc(x_sq, 1)
            act.wait_ge(x_var, 1)
            act.activation(stat[:, 2, :], stat[:, 1, :], ACT.Sqrt).then_inc(x_std, 1)
            act.wait_ge(small_in, 48)
            for k in range(0, KD, 2):
                act.wait_ge(xT_ok, 1)
                act.activation(hT[:, k, :], psum[:, k, :], ACT.Copy, scale=g1[:, k:k + 1]).then_inc(h_ok, 1)
            for t in range(QT):
                act.wait_ge(rows_mm, t + 1)
                act.activation(m.rows[:, t, 0:S], psum[:, 2 * t, :], ACT.Copy).then_inc(rows_a, 1)
            for j in (C_KC, C_KS):
                act.wait_ge(cols_mm, j + 1)
                dst = cT[:, 0, :] if j == C_KC else m.kT[:, 0, :]
                act.activation(dst, psum[:, j, :], ACT.Copy).then_inc(cols_a, 1)
            for c in (0, 1):
                for t in range(QT):
                    act.wait_ge(rows_a, t + 1)
                    lo, hi = (R_CQ, R_CKV) if c == 0 else (R_CKV, R_VS)
                    if c + t:
                        act.wait_ge(lat_sq, c * QT + t)
                    act.activation(junk[:, 0:hi - lo], m.rows[:, t, lo:hi], ACT.Square,
                                   accum_out=stat[:, 3, t:t + 1] if c == 0 else m.lsum[:, t:t + 1]).then_inc(lat_sq, 1)
            for j in (C_Q, C_Q + 2):
                act.wait_ge(cols_mm, j + 1)
                act.activation(m.qT[:, j - C_Q, :], psum[:, j, :], ACT.Copy, scale=NSA_SCALE).then_inc(cols_a, 1)
            act.wait_ge(lat_var, 2)
            act.activation(m.lstat[:, 1, :], m.lstat[:, 0, :], ACT.Sqrt).then_inc(lat_std, 1)
            for c in range(3):
                act.wait_ge(latT_mm, c + 1)
                act.activation(m.latT[:, c, :], psum[:, c, :], ACT.Copy, scale=qkvg[:, c:c + 1]).then_inc(latT_ok, 1)
            for c in range(2):
                act.wait_ge(hid_mm, c + 1)
                act.activation(hid[:, c, :, :], psum[:, 4 + c, 0:HT * GROUPS * N_CMP].rearrange(
                    "p (h n) -> p h n", h=HT), ACT.Gelu).then_inc(hid_ok, 1)
            act.wait_ge(w1_in, 16)

        @block.vector
        def _(dve):
            dve.memset(t5x[BUCKETS:BUCKETS + 1, :], NEG).then_inc(neg_ok, 1)
            dve.wait_ge(x_sq, QT)
            dve.tensor_scalar(stat[:, 1, :], stat[:, 0, :], 1.0 / D, EPS, ALU.mult, ALU.add).then_inc(x_var, 1)
            dve.wait_ge(x_std, 1)
            dve.reciprocal(stat[:, 0, :], stat[:, 2, :]).then_inc(x_rs, 1)
            dve.wait_ge(x_rs, 1)
            for t in range(QT):
                dve.tensor_scalar(xn[:, t, :], m.x[:, t, :], stat[:, 0, t:t + 1], None, ALU.mult).then_inc(xn_ok, 1)
            dve.wait_ge(small_in, 48)
            for k in range(1, KD, 2):
                dve.wait_ge(xT_ok, 1)
                dve.tensor_scalar(hT[:, k, :], psum[:, k, :], g1[:, k:k + 1], None, ALU.mult).then_inc(h_ok, 1)
            for t in range(QT):
                dve.wait_ge(rows_mm, t + 1)
                dve.tensor_copy(m.rows[:, t, S:ROW_W], psum[:, 2 * t + 1, 0:ROW_W - S]).then_inc(rows_v, 1)
            for j in (C_VC, C_KW):
                dve.wait_ge(cols_mm, j + 1)
                dst = cT[:, 1, :] if j == C_VC else m.kT[:, 1, :]
                dve.tensor_copy(dst, psum[:, j, :]).then_inc(cols_v, 1)
            dve.wait_ge(lat_sq, 2 * QT)
            dve.tensor_scalar(m.lstat[:, 0, 0:QT], stat[:, 3, :], 1.0 / Q_LORA, EPS, ALU.mult, ALU.add).then_inc(lat_var, 1)
            dve.tensor_scalar(m.lstat[:, 0, QT:], m.lsum[:, :], 1.0 / KV_LORA, EPS, ALU.mult, ALU.add).then_inc(lat_var, 1)
            for j in (C_Q + 1, C_Q + 3):
                dve.wait_ge(cols_mm, j + 1)
                dve.tensor_scalar(m.qT[:, j - C_Q, :], psum[:, j, :], NSA_SCALE, None, ALU.mult).then_inc(cols_v, 1)
            dve.wait_ge(lat_std, 1)
            dve.reciprocal(m.lstat[:, 2, :], m.lstat[:, 1, :]).then_inc(lat_rs, 1)
            dve.wait_ge(lat_rs, 1)
            for t in range(QT):
                dve.tensor_scalar(lat[:, t, 0:256], m.rows[:, t, R_CQ:R_CKV], m.lstat[:, 2, t:t + 1], None, ALU.mult)
                dve.tensor_scalar(lat[:, t, 256:384], m.rows[:, t, R_CKV:R_VS], m.lstat[:, 2, QT + t:QT + t + 1], None,
                                  ALU.mult).then_inc(lat_ok, 1)
            dve.wait_ge(pair_ok, 128)
            for c in range(2):
                for g in range(GROUPS):
                    raw = pairs[:, c, g, :]
                    raw = bass.AP(tensor=raw.tensor, offset=raw.offset,
                                  ap=[raw.ap[0], [2, LP], [CMP_STRIDE, N_CMP]])
                    dve.tensor_tensor(blk[:, c, :, g, :], raw, posT[:, :].unsqueeze(2).to_broadcast([P, LP, N_CMP]),
                                      ALU.add).then_inc(blk_ok, 1)
            dve.wait_ge(b_mm, 1)
            dve.tensor_copy(brow[:, :].rearrange("h (b n) -> h b n", b=2), psum[0:HEADS, 6:8, :]).then_inc(b_row, 1)
            dve.wait_ge(cmp_mm, 1)
            dve.tensor_copy(m.kcT[0:DH, :], psum[0:DH, 3, 0:N_CMP]).then_inc(cmp_ok, 1)
            dve.tensor_copy(m.kcT[DH:P, :], psum[DH:P, 3, 0:N_CMP]).then_inc(cmp_ok, 1)
            dve.wait_ge(cmp_mm, 2)
            dve.tensor_copy(m.vc[:, :], psum[0:N_CMP, 4, 0:GROUPS * DH]).then_inc(cmp_ok, 1)
            dve.wait_ge(b_rep, 16)

        @block.tensor
        def _(pe):
            pe.wait_ge(eye_ok, 2)
            for t in range(QT):
                pe.wait_ge(xn_ok, t + 1)
                for k in range(KD):
                    mm = pe.transpose(psum[:, k, t * P:(t + 1) * P], xn[:, t, k * P:(k + 1) * P], m.eye[:, :])
            mm.then_inc(xT_ok, 1)
            pe.wait_ge(h_ok, KD)
            pe.wait_ge(wr_in, 16)
            for t in range(QT):
                for b, (lo, hi) in enumerate(((0, S), (S, ROW_W))):
                    for k in range(KD):
                        mm = pe.matmul(psum[:, 2 * t + b, 0:hi - lo], hT[:, k, t * P:(t + 1) * P],
                                       w_rows[:, k, lo:hi], start=(k == 0), stop=(k == KD - 1))
                mm.then_inc(rows_mm, 1)
            for j in range(N_COLS):
                pe.wait_ge(wc_in[j % 2], 16 * (j // 2 + 1))
                pe.wait_ge(rows_a, j // 2 + 1)
                pe.wait_ge(rows_v, j // 2 + 1)
                for k in range(KD):
                    mm = pe.matmul(psum[:, j, :], w_col[:, j % 2, k, :], hT[:, k, :],
                                   start=(k == 0), stop=(k == KD - 1))
                mm.then_inc(cols_mm, 1)
            pe.wait_ge(t5_in, 32)
            pe.wait_ge(neg_ok, 1)
            pe.wait_ge(cols_a, 4)
            pe.wait_ge(cols_v, 4)
            for b in range(2):
                mm = pe.matmul(psum[0:HEADS, 6 + b, :], t5x[:, :], onehot[:, b * S:(b + 1) * S], start=True, stop=True)
            mm.then_inc(b_mm, 1)
            pe.wait_ge(w1_in, 16)
            pe.wait_ge(w1v_in, 16)
            for c in range(2):
                pe.wait_ge(blk_ok, GROUPS * (c + 1))
                for h in range(HT):
                    for l in range(LP):
                        mm = pe.matmul(psum[:, 4 + c, h * GROUPS * N_CMP:(h + 1) * GROUPS * N_CMP],
                                       (w1 if c == 0 else w1v)[:, l, h * P:(h + 1) * P],
                                       blk[:, c, l, :, :].rearrange("p g n -> p (g n)"),
                                       start=(l == 0), stop=(l == LP - 1))
                mm.then_inc(hid_mm, 1)
            pe.wait_ge(lat_ok, QT)
            for c in range(3):
                for t in range(QT):
                    mm = pe.transpose(psum[:, c, t * P:(t + 1) * P], lat[:, t, c * P:(c + 1) * P], m.eye[:, :])
                mm.then_inc(latT_mm, 1)
            pe.wait_ge(w2_in, 16)
            pe.wait_ge(hid_ok, 1)
            for g in range(GROUPS):
                for h in range(HT):
                    mm = pe.matmul(psum[g * DH:(g + 1) * DH, 3, 0:N_CMP], w2[:, 0, h, :],
                                   hid[:, 0, h, g * N_CMP:(g + 1) * N_CMP], start=(h == 0), stop=(h == HT - 1))
            mm.then_inc(cmp_mm, 1)
            pe.wait_ge(hid_ok, 2)
            for g in range(GROUPS):
                for h in range(HT):
                    mm = pe.matmul(psum[0:N_CMP, 4, g * DH:(g + 1) * DH], hid[:, 1, h, g * N_CMP:(g + 1) * N_CMP],
                                   w2[:, 1, h, :], start=(h == 0), stop=(h == HT - 1))
            mm.then_inc(cmp_mm, 1)
            pe.wait_ge(up_in, 64)
            pe.wait_ge(latT_ok, 3)


def latents(nc, io, m, psum):
    with ExitStack() as ctx:
        sb = m.scratch().take

        def sem(name):
            return ctx.enter_context(nc.semaphore(name))

        posf = sb("posf", [P, QT])
        ang = sb("ang", [P, QT, HALF])
        turns = sb("turns", [P, 2, QT * HALF])
        red = sb("red", [P, 2, QT * HALF])
        trig = sb("trig", [P, 2, QT, HALF])
        qf = sb("qf", [P, QT, HEADS, QK])
        kf = sb("kf", [P, QT, HEADS, QK])
        part = sb("part", [P, 4, QT, HEADS, HALF])
        kpart = sb("kpart", [P, 4, QT, HALF])
        krot = sb("krot", [P, QT, ROPE])

        step, red_ok, trig_ok = sem("rope_step"), sem("red_ok"), sem("trig_ok")
        up_mm, upq_ok, upk_ok = sem("up_mm"), sem("upq_ok"), sem("upk_ok")
        q_rot, k_rot, qkT_mm, qkT_a, qkT_v = sem("q_rot"), sem("k_rot"), sem("qkT_mm"), sem("qkT_a"), sem("qkT_v")
        gate_e = sem("gate_e")
        block = ctx.enter_context(nc.Block())

        @block.scalar
        def _(act):
            for t in range(QT):
                act.wait_ge(up_mm, t + 1)
                for b in range(2):
                    act.activation(qf[:, t, 4 * b:4 * b + 4, :].rearrange("p h d -> p (h d)"),
                                   psum[:, 4 * (t % 2) + b, 0:4 * QK], ACT.Copy).then_inc(upq_ok, 1)
            act.activation(m.gate[:, :, :], m.rows[:, :, R_G:ROW_W], ACT.Exp, scale=-1.0).then_inc(gate_e, 1)
            act.wait_ge(red_ok, 1)
            act.activation(trig[:, :, :, :].rearrange("p c t d -> p (c t d)"),
                           red[:, :, :].rearrange("p c n -> p (c n)"), ACT.Sin).then_inc(trig_ok, 1)
            for u in range(0, 2 * HEADS, 2):
                act.wait_ge(qkT_mm, u + 1)
                act.activation(m.qmT[:, u // 2, :], psum[0:QK, u % 8, :], ACT.Copy).then_inc(qkT_a, 1)

        @block.vector
        def _(dve):
            chain = [0]

            def link(ins):
                chain[0] += 1
                ins.then_inc(step, 1)
                dve.wait_ge(step, chain[0])

            link(dve.tensor_copy(posf[:, :], m.pos[:, :]))
            link(dve.tensor_tensor(ang[:, :, :], posf[:, :].unsqueeze(2).to_broadcast([P, QT, HALF]),
                                   m.inv[:, :].unsqueeze(1).to_broadcast([P, QT, HALF]), ALU.mult))
            a = ang[:, :, :].rearrange("p t d -> p (t d)")
            dve.tensor_scalar(turns[:, 0, :], a, 1 / (2 * np.pi), None, ALU.mult).then_inc(step, 1)
            chain[0] += 1
            link(dve.tensor_scalar(turns[:, 1, :], a, 1 / (2 * np.pi), 0.25, ALU.mult, ALU.add))
            link(dve.tensor_scalar(turns[:, :, :], turns[:, :, :], ROUND, None, ALU.add))
            link(dve.tensor_scalar(turns[:, :, :], turns[:, :, :], ROUND, None, ALU.subtract))
            src = ang[:, :, :].rearrange("p t d -> p (t d)").unsqueeze(1).to_broadcast([P, 2, QT * HALF])
            for c in (TWO_PI_HI, TWO_PI_MID, TWO_PI_LO):
                link(dve.scalar_tensor_tensor(out=red[:, :, :], in0=turns[:, :, :], scalar=-c, in1=src,
                                              op0=ALU.mult, op1=ALU.add))
                src = red[:, :, :]
            link(dve.tensor_scalar(red[:, 1, :], red[:, 1, :], float(np.pi / 2), None, ALU.add))
            dve.tensor_scalar(red[:, :, :], red[:, :, :], PI_IN, -PI_IN, ALU.min, ALU.max).then_inc(red_ok, 1)
            for t in range(QT):
                dve.wait_ge(up_mm, t + 1)
                dve.tensor_copy(kf[:, t, :, 0:NOPE], psum[:, 4 * (t % 2) + 2, :].rearrange("p (h d) -> p h d", h=HEADS)
                                ).then_inc(upk_ok, 1)
                dve.tensor_copy(m.vm[:, t, :], psum[:, 4 * (t % 2) + 3, :]).then_inc(upk_ok, 1)
            dve.wait_ge(gate_e, 1)
            link(dve.tensor_scalar(m.gate[:, :, :], m.gate[:, :, :], 1.0, None, ALU.add))
            dve.reciprocal(m.gate[:, :, :], m.gate[:, :, :])
            dve.wait_ge(trig_ok, 1)
            k1, k2 = m.rows[:, :, R_KR:R_KR + HALF], m.rows[:, :, R_KR + HALF:R_G]
            sin, cos = trig[:, 0], trig[:, 1]
            for n, (xx, tt) in enumerate(((k1, cos), (k2, sin), (k1, sin), (k2, cos))):
                dve.tensor_tensor(kpart[:, n], xx, tt, ALU.mult).then_inc(step, 1)
                chain[0] += 1
            dve.wait_ge(step, chain[0])
            dve.tensor_tensor(krot[:, :, 0:HALF], kpart[:, 0], kpart[:, 1], ALU.subtract)
            link(dve.tensor_tensor(krot[:, :, HALF:ROPE], kpart[:, 2], kpart[:, 3], ALU.add))
            for t in range(QT):
                dve.tensor_copy(kf[:, t, :, NOPE:QK], krot[:, t, :].unsqueeze(1).to_broadcast([P, HEADS, ROPE])
                                ).then_inc(k_rot, 1)
            dve.wait_ge(upq_ok, 2 * QT)
            for t in range(QT):
                q1, q2 = qf[:, t, :, NOPE:NOPE + HALF], qf[:, t, :, NOPE + HALF:QK]
                sin_t = trig[:, 0, t, :].unsqueeze(1).to_broadcast([P, HEADS, HALF])
                cos_t = trig[:, 1, t, :].unsqueeze(1).to_broadcast([P, HEADS, HALF])
                for n, (xx, tt) in enumerate(((q1, cos_t), (q2, sin_t), (q1, sin_t), (q2, cos_t))):
                    dve.tensor_tensor(part[:, n, t], xx, tt, ALU.mult).then_inc(step, 1)
                    chain[0] += 1
            dve.wait_ge(step, chain[0])
            for t in range(QT):
                dve.tensor_tensor(qf[:, t, :, NOPE:NOPE + HALF], part[:, 0, t], part[:, 1, t], ALU.subtract
                                  ).then_inc(q_rot, 1)
                dve.tensor_tensor(qf[:, t, :, NOPE + HALF:QK], part[:, 2, t], part[:, 3, t], ALU.add).then_inc(q_rot, 1)
            for u in range(1, 2 * HEADS, 2):
                dve.wait_ge(qkT_mm, u + 1)
                dve.tensor_copy(m.kmT[:, u // 2, :], psum[0:QK, u % 8, :]).then_inc(qkT_v, 1)

        @block.tensor
        def _(pe):
            for t in range(QT):
                if t >= 2:
                    pe.wait_ge(upq_ok, 2 * (t - 1))
                    pe.wait_ge(upk_ok, 2 * (t - 1))
                for b in range(2):
                    for c in range(2):
                        pe.matmul(psum[:, 4 * (t % 2) + b, 0:4 * QK], m.latT[:, c, t * P:(t + 1) * P],
                                  m.wq_up[:, c, b * 4 * QK:(b + 1) * 4 * QK], start=(c == 0), stop=(c == 1))
                for b in range(2):
                    mm = pe.matmul(psum[:, 4 * (t % 2) + 2 + b, :], m.latT[:, 2, t * P:(t + 1) * P],
                                   m.wkv_up[:, b * 512:(b + 1) * 512], start=True, stop=True)
                mm.then_inc(up_mm, 1)
            pe.wait_ge(upq_ok, 2 * QT)
            pe.wait_ge(upk_ok, 2 * QT)
            pe.wait_ge(k_rot, QT)
            pe.wait_ge(q_rot, 2 * QT)
            for u in range(2 * HEADS):
                if u >= 8:
                    pe.wait_ge(qkT_a if u % 2 == 0 else qkT_v, (u - 8) // 2 + 1)
                for t in range(QT):
                    mm = pe.transpose(psum[0:QK, u % 8, t * P:(t + 1) * P], (qf if u % 2 == 0 else kf)[:, t, u // 2, :],
                                      m.eye[:, :])
                mm.then_inc(qkT_mm, 1)


def attend(nc, io, m, psum):
    units = []
    for i in range(QT):
        units += [(i, 0, g) for g in range(GROUPS)]
        units += [(i, b, (n % 2) * 4 + n // 2) for b in (1, 2) for n in range(HEADS)]
        units += [(i, 3, h) for h in range(HEADS)]
    last = {}
    for u, (i, b, _) in enumerate(units):
        last[(i, b)] = u
    branches = [(i, b) for i in range(QT) for b in range(4)]
    n_units = len(units)
    with ExitStack() as ctx:
        sb = m.scratch().take

        def sem(name):
            return ctx.enter_context(nc.semaphore(name))

        sc = sb("sc", [P, 3, S])
        pr = sb("pr", [P, 3, S])
        prT = sb("prT", [P, 3, S])
        top = sb("top", [P, n_units, 4])
        sums = sb("sums", [P, QT, 4, HEADS])
        fac = sb("fac", [P, QT, 4, HEADS])
        tmp = sb("tmp", [P, NSA_W])

        s_mm, s_in, e_ok, c_step = sem("s_mm"), sem("s_in"), sem("e_ok"), sem("c_step")
        t_mm, t_v, t_a, o_mm, o_in = sem("t_mm"), sem("t_v"), sem("t_a"), sem("o_mm"), sem("o_in")
        block = ctx.enter_context(nc.Block())
        S_BANK, T_BANK, O_BANK = 0, 3, 5
        S_N, T_N, O_N = 3, 2, 2

        def copied(eng, u):
            eng.wait_ge(t_v if u % 2 == 0 else t_a, u // 2 + 1)

        def copy_out(eng, u):
            i, b, _ = units[u]
            eng.wait_ge(t_mm, u + 1)
            if u >= 3:
                eng.wait_ge(o_mm, u - 2)
            rows, w = (N_CMP, S) if b == 0 else (P, (i + 1) * P)
            src, dst = psum[0:rows, T_BANK + u % T_N, 0:w], prT[0:rows, u % 3, 0:w]
            if u % 2 == 0:
                nc.vector.tensor_copy(dst, src).then_inc(t_v, 1)
            else:
                nc.scalar.activation(dst, src, ACT.Copy).then_inc(t_a, 1)

        @block.tensor
        def _(pe):
            def scores(u):
                i, b, h = units[u]
                if u >= S_N:
                    pe.wait_ge(s_in, u - S_N + 1)
                bank, q = psum[:, S_BANK + u % S_N, :], slice(i * P, (i + 1) * P)
                if b == 0:
                    r = slice(h * DH, (h + 1) * DH)
                    for n in range(4):
                        mm = pe.matmul(bank[:, n * N_CMP:(n + 1) * N_CMP], m.qT[r, n, q], m.kcT[r, :],
                                       start=True, stop=True)
                elif b < 3:
                    r = slice(h // 4 * DH, (h // 4 + 1) * DH)
                    mm = pe.matmul(bank[:, 0:(i + 1) * P], m.qT[r, h % 4, q], m.kT[r, b - 1, 0:(i + 1) * P],
                                   start=True, stop=True)
                else:
                    mm = pe.matmul(bank[:, 0:(i + 1) * P], m.qmT[:, h, q], m.kmT[:, h, 0:(i + 1) * P],
                                   start=True, stop=True)
                mm.then_inc(s_mm, 1)

            def turn(u):
                i, b, _ = units[u]
                pe.wait_ge(e_ok, u + 1)
                if u >= T_N:
                    copied(pe, u - T_N)
                for n in range(4 if b == 0 else i + 1):
                    if b == 0:
                        mm = pe.transpose(psum[0:N_CMP, T_BANK + u % T_N, n * P:(n + 1) * P],
                                          pr[:, u % 3, n * N_CMP:(n + 1) * N_CMP], m.eye[:, :])
                    else:
                        mm = pe.transpose(psum[:, T_BANK + u % T_N, n * P:(n + 1) * P],
                                          pr[:, u % 3, n * P:(n + 1) * P], m.eye[:, :])
                mm.then_inc(t_mm, 1)

            def values(u):
                i, b, h = units[u]
                copied(pe, u)
                bi = branches.index((i, b))
                if bi >= O_N:
                    pe.wait_ge(o_in, bi - O_N + 1)
                bank = psum[:, O_BANK + bi % O_N, :]
                if b == 0:
                    for n in range(4):
                        hh = h * 4 + n
                        mm = pe.matmul(bank[:, hh * DH:(hh + 1) * DH], prT[0:N_CMP, u % 3, n * P:(n + 1) * P],
                                       m.vc[:, h * DH:(h + 1) * DH], start=True, stop=True)
                else:
                    for n in range(i + 1):
                        if b < 3:
                            lo = (R_VS, R_VW)[b - 1] + h // 4 * DH
                            v = m.rows[:, n, lo:lo + DH]
                        else:
                            v = m.vm[:, n, h * DH:(h + 1) * DH]
                        mm = pe.matmul(bank[:, h * DH:(h + 1) * DH], prT[:, u % 3, n * P:(n + 1) * P], v,
                                       start=(n == 0), stop=(n == i))
                mm.then_inc(o_mm, 1)

            for s in range(n_units + 3):
                if s < n_units:
                    scores(s)
                if 2 <= s < n_units + 2:
                    turn(s - 2)
                if s >= 3:
                    values(s - 3)

        @block.scalar
        def _(act):
            for s in range(n_units + 3):
                if s < n_units:
                    i, b, h = units[s]
                    act.wait_ge(s_in, s + 1)
                    if s >= 3:
                        act.wait_ge(t_mm, s - 2)
                    if b == 0:
                        act.activation(pr[:, s % 3, 0:4 * N_CMP], sc[:, s % 3, 0:4 * N_CMP], ACT.Exp).then_inc(e_ok, 1)
                    else:
                        w = (i + 1) * P
                        act.activation(pr[:, s % 3, 0:w], sc[:, s % 3, 0:w], ACT.Exp, bias=top[:, s, 0:1], scale=-1.0,
                                       accum_out=sums[:, i, b, h:h + 1]).then_inc(e_ok, 1)
                if s >= 2 and s % 2 == 1 and s - 2 < n_units:
                    copy_out(act, s - 2)

        @block.vector
        def _(dve):
            chain = [0]

            def link(ins):
                chain[0] += 1
                ins.then_inc(c_step, 1)
                dve.wait_ge(c_step, chain[0])

            def combine(bi):
                i, b = branches[bi]
                dve.wait_ge(e_ok, last[(i, b)] + 1)
                f = fac[:, i, b, :]
                link(dve.reciprocal(f, sums[:, i, b, :]))
                if b < 3:
                    link(dve.tensor_tensor(f, f, m.gate[:, i, :].rearrange("p (h b) -> p b h", b=3)[:, b, :], ALU.mult))
                if b == 0 and i == 0:
                    link(dve.tensor_scalar(f, f, m.seen[:, 0:1], None, ALU.mult))
                dve.wait_ge(o_mm, last[(i, b)] + 1)
                src = psum[:, O_BANK + bi % O_N, :].rearrange("p (h d) -> p h d", h=HEADS)
                fb = f.unsqueeze(2).to_broadcast([P, HEADS, DH])
                out = m.o[:, i, 1 if b == 3 else 0, :]
                if b in (0, 3):
                    dve.tensor_tensor(out.rearrange("p (h d) -> p h d", h=HEADS), src, fb, ALU.mult).then_inc(o_in, 1)
                else:
                    dve.tensor_tensor(tmp[:, :].rearrange("p (h d) -> p h d", h=HEADS), src, fb, ALU.mult
                                      ).then_inc(o_in, 1)
                    dve.wait_ge(o_in, bi + 1)
                    link(dve.tensor_tensor(out, out, tmp[:, :], ALU.add))

            for s in range(n_units + 4):
                if s < n_units:
                    i, b, h = units[s]
                    dve.wait_ge(s_mm, s + 1)
                    if s >= 3:
                        dve.wait_ge(e_ok, s - 2)
                    bank, w = psum[:, S_BANK + s % S_N, :], (i + 1) * P
                    j0 = S - w
                    if b == 0:
                        out = sc[:, s % 3, 0:4 * N_CMP].rearrange("p (h n) -> p h n", h=4)
                        c0 = S - P + CMP_LEN - 1 - i * P
                        bias = m.bias[:, 4 * h:4 * h + 4, c0:c0 + (N_CMP - 1) * CMP_STRIDE + 1:CMP_STRIDE]
                        link(dve.tensor_tensor(out, bank[:, 0:4 * N_CMP].rearrange("p (h n) -> p h n", h=4), bias,
                                               ALU.add))
                        link(dve.tensor_reduce(top[:, s, :], out, X, ALU.max))
                        dve.tensor_tensor(out, out, top[:, s, :].unsqueeze(2).to_broadcast([P, 4, N_CMP]),
                                          ALU.subtract).then_inc(s_in, 1)
                    elif b < 3:
                        dve.tensor_tensor_reduce(sc[:, s % 3, 0:w], bank[:, 0:w], m.bias[:, h, j0:S], -1.0, 3.0e38,
                                                 ALU.add, ALU.min, top[:, s, 0:1]).then_inc(s_in, 1)
                    else:
                        dve.tensor_tensor_reduce(sc[:, s % 3, 0:w], bank[:, 0:w], m.mask[:, j0:S], -MLA_SCALE, 3.0e38,
                                                 ALU.add, ALU.min, top[:, s, 0:1]).then_inc(s_in, 1)
                if s >= 2 and s % 2 == 0 and s - 2 < n_units:
                    copy_out(dve, s - 2)
                if s >= 1 and s - 1 < n_units and units[s - 1][1] == 0:
                    i, b, g = units[s - 1]
                    dve.wait_ge(e_ok, s)
                    link(dve.tensor_reduce(sums[:, i, 0, 4 * g:4 * g + 4],
                                           pr[:, (s - 1) % 3, 0:4 * N_CMP].rearrange("p (h n) -> p h n", h=4),
                                           X, ALU.add))
                if s >= 4 and last[units[s - 4][0:2]] == s - 4:
                    combine(branches.index(units[s - 4][0:2]))


def output(nc, io, m, psum):
    with ExitStack() as ctx:
        sb = m.scratch().take

        def sem(name):
            return ctx.enter_context(nc.semaphore(name))

        w_out = sb("w_out", [P, KD, D])
        oT = sb("oT", [P, KD, S])
        h2T = sb("h2T", [P, KD, S])
        gain = sb("gain", [P, 2, KD])
        stat = sb("ostat", [P, 4, 2 * QT])
        stat2 = sb("ostat2", [P, 4, QT])
        junk = sb("ojunk", [P, 2, D])
        xn = m.o

        wo_in, gain_in = sem("wo_in"), sem("gain_in")
        g_sq, g_var, g_std, g_rs, on_ok, oT_mm, oT_a, oT_v = (
            sem("g_sq"), sem("g_var"), sem("g_std"), sem("g_rs"), sem("on_ok"), sem("oT_mm"), sem("oT_a"), sem("oT_v"))
        y_mm, y_ok, x2_out = sem("y_mm"), sem("y_ok"), sem("x2_out")
        y_sq, y_var, y_std, y_rs, yn_ok, yT_mm, h2_a, h2_v, hi_ok, lo_ok = (
            sem("y_sq"), sem("y_var"), sem("y_std"), sem("y_rs"), sem("yn_ok"), sem("yT_mm"), sem("h2_a"), sem("h2_v"),
            sem("hi_ok"), sem("lo_ok"))
        block = ctx.enter_context(nc.Block())

        @block.sync
        def _(sp):
            sp.dma_start(w_out[:, :, :], io.w_out).then_inc(wo_in, 16)
            sp.dma_start(gain[:, 0, :], io.grp_gain).then_inc(gain_in, 16)
            sp.dma_start(gain[:, 1, :], io.g2).then_inc(gain_in, 16)
            sp.wait_ge(y_ok, 2 * QT)
            sp.dma_start(io.x2.rearrange("(t p) d -> p t d", p=P), m.x[:, :, :]).then_inc(x2_out, 16)
            sp.wait_ge(x2_out, 16)

        @block.scalar
        def _(act):
            for t in range(QT):
                for b in range(2):
                    if t + b:
                        act.wait_ge(g_sq, 2 * t + b)
                    act.activation(junk[:, 0, 0:NSA_W], m.o[:, t, b, :], ACT.Square,
                                   accum_out=stat[:, 0, 2 * t + b:2 * t + b + 1]).then_inc(g_sq, 1)
            act.wait_ge(g_var, 1)
            act.activation(stat[:, 2, :], stat[:, 1, :], ACT.Sqrt).then_inc(g_std, 1)
            act.wait_ge(gain_in, 32)
            act.wait_ge(oT_mm, 1)
            for k in range(0, KD, 2):
                act.activation(oT[:, k, :], psum[:, k, :], ACT.Copy, scale=gain[:, 0, k:k + 1]).then_inc(oT_a, 1)
            for t in range(QT):
                act.wait_ge(y_ok, 2 * t + 2)
                if t:
                    act.wait_ge(y_sq, t)
                act.activation(junk[:, 1, :], m.x[:, t, :], ACT.Square, accum_out=stat2[:, 0, t:t + 1]).then_inc(y_sq, 1)
            act.wait_ge(y_var, 1)
            act.activation(stat2[:, 2, :], stat2[:, 1, :], ACT.Sqrt).then_inc(y_std, 1)
            act.wait_ge(yT_mm, 1)
            for k in range(0, KD, 2):
                act.activation(h2T[:, k, :], psum[:, k, :], ACT.Copy, scale=gain[:, 1, k:k + 1]).then_inc(h2_a, 1)
            for k in range(KD):
                act.wait_ge(h2_a if k % 2 == 0 else h2_v, k // 2 + 1)
                act.activation(m.h_hi[:, k, :], h2T[:, k, :], ACT.Copy).then_inc(hi_ok, 1)

        @block.vector
        def _(dve):
            dve.wait_ge(g_sq, 2 * QT)
            dve.tensor_scalar(stat[:, 1, :], stat[:, 0, :], 1.0 / NSA_W, EPS, ALU.mult, ALU.add).then_inc(g_var, 1)
            dve.wait_ge(g_std, 1)
            dve.reciprocal(stat[:, 3, :], stat[:, 2, :]).then_inc(g_rs, 1)
            dve.wait_ge(g_rs, 1)
            for t in range(QT):
                for b in range(2):
                    dve.tensor_scalar(m.o[:, t, b, :], m.o[:, t, b, :], stat[:, 3, 2 * t + b:2 * t + b + 1], None,
                                      ALU.mult).then_inc(on_ok, 1)
            dve.wait_ge(gain_in, 32)
            dve.wait_ge(oT_mm, 1)
            for k in range(1, KD, 2):
                dve.tensor_scalar(oT[:, k, :], psum[:, k, :], gain[:, 0, k:k + 1], None, ALU.mult).then_inc(oT_v, 1)
            for t in range(QT):
                for b in range(2):
                    dve.wait_ge(y_mm, 2 * t + b + 1)
                    xs = m.x[:, t, b * S:(b + 1) * S]
                    dve.tensor_tensor(xs, psum[:, 2 * t + b, :], xs, ALU.add).then_inc(y_ok, 1)
            dve.wait_ge(y_sq, QT)
            dve.tensor_scalar(stat2[:, 1, :], stat2[:, 0, :], 1.0 / D, EPS, ALU.mult, ALU.add).then_inc(y_var, 1)
            dve.wait_ge(y_std, 1)
            dve.reciprocal(stat2[:, 3, :], stat2[:, 2, :]).then_inc(y_rs, 1)
            dve.wait_ge(y_rs, 1)
            for t in range(QT):
                dve.tensor_scalar(xn[:, t, :, :].rearrange("p b n -> p (b n)"), m.x[:, t, :], stat2[:, 3, t:t + 1],
                                  None, ALU.mult).then_inc(yn_ok, 1)
            dve.wait_ge(yT_mm, 1)
            for k in range(1, KD, 2):
                dve.tensor_scalar(h2T[:, k, :], psum[:, k, :], gain[:, 1, k:k + 1], None, ALU.mult).then_inc(h2_v, 1)
            for k in range(KD):
                dve.wait_ge(hi_ok, k + 1)
                dve.wait_ge(h2_a if k % 2 == 0 else h2_v, k // 2 + 1)
                dve.tensor_tensor(m.h_lo[:, k, :], h2T[:, k, :], m.h_hi[:, k, :].bitcast(F32), ALU.subtract
                                  ).then_inc(lo_ok, 1)

        @block.tensor
        def _(pe):
            for t in range(QT):
                pe.wait_ge(on_ok, 2 * t + 2)
                for k in range(KD):
                    mm = pe.transpose(psum[:, k, t * P:(t + 1) * P], m.o[:, t, k // 4, k % 4 * P:(k % 4 + 1) * P],
                                      m.eye[:, :])
            mm.then_inc(oT_mm, 1)
            pe.wait_ge(oT_a, KD // 2)
            pe.wait_ge(oT_v, KD // 2)
            pe.wait_ge(wo_in, 16)
            for t in range(QT):
                for b in range(2):
                    for k in range(KD):
                        mm = pe.matmul(psum[:, 2 * t + b, :], oT[:, k, t * P:(t + 1) * P],
                                       w_out[:, k, b * S:(b + 1) * S], start=(k == 0), stop=(k == KD - 1))
                    mm.then_inc(y_mm, 1)
            pe.wait_ge(y_ok, 2 * QT)
            for t in range(QT):
                pe.wait_ge(yn_ok, t + 1)
                for k in range(KD):
                    mm = pe.transpose(psum[:, k, t * P:(t + 1) * P], xn[:, t, k // 4, k % 4 * P:(k % 4 + 1) * P],
                                      m.eye[:, :])
            mm.then_inc(yT_mm, 1)


def product3(pe, bank, w_hi, w_lo, x_hi, x_lo):
    n = 3 * KD
    i = 0
    for k in range(KD):
        for w, x in ((w_hi, x_hi), (w_hi, x_lo), (w_lo, x_hi)):
            mm = pe.matmul(bank, w[:, k, :], x[:, k, :], start=(i == 0), stop=(i == n - 1))
            i += 1
    return mm


def peer_scores(nc, io, m, psum):
    with ExitStack() as ctx:
        sb = m.scratch().take

        def sem(name):
            return ctx.enter_context(nc.semaphore(name))

        raw = sb("wq_raw", [P, 2, KD, P])
        hi = sb("wq_hi", [P, 2, KD, P], F32R)
        lo = sb("wq_lo", [P, 2, KD, P], F32R)
        qp = sb("qp", [P, 2, S])
        keys = sb("keysT", [P, 2, NKEYS])
        keys_in = sem("keys_in")
        raw_in = [sem("wq_in0"), sem("wq_in1")]
        hi_ok, lo_ok, q_mm, q_ok, s_mm, s_ok = (
            sem("wqhi_ok"), sem("wqlo_ok"), sem("pq_mm"), sem("pq_ok"), sem("ps_mm"), sem("ps_ok"))
        block = ctx.enter_context(nc.Block())
        rounds = PH

        @block.sync
        def _(sp):
            sp.dma_start(keys[:, :, :], io.keysT).then_inc(keys_in, 16)
            for c in range(2):
                sp.dma_start(raw[:, c], io.wq[c]).then_inc(raw_in[c], 16)
            with sp.Fori(1, rounds) as h:
                for c in range(2):
                    sp.wait_ge(lo_ok, 2 * h - 1 + c)
                    sp.dma_start(raw[:, c], io.wq[bass.ds(2 * h + c, 1)].rearrange("o p k n -> p (o k) n")
                                 ).then_inc(raw_in[c], 16)

        @block.scalar
        def _(act):
            def split(h, c):
                act.wait_ge(raw_in[c], 16 * h + 16)
                act.activation(hi[:, c].rearrange("p k n -> p (k n)"), raw[:, c].rearrange("p k n -> p (k n)"),
                               ACT.Copy).then_inc(hi_ok, 1)

            split(0, 0)
            split(0, 1)

            def queries(h, c):
                act.wait_ge(q_mm, 2 * h + 1 + c)
                act.activation(qp[:, c, :], psum[:, c, :], ACT.Copy).then_inc(q_ok, 1)

            with act.Fori(1, rounds) as h:
                for c in range(2):
                    queries(h - 1, c)
                    split(h, c)
            for c in range(2):
                queries(rounds - 1, c)

        @block.vector
        def _(dve):
            def split(h, c):
                dve.wait_ge(hi_ok, 2 * h + 1 + c)
                dve.tensor_tensor(lo[:, c].rearrange("p k n -> p (k n)"), raw[:, c].rearrange("p k n -> p (k n)"),
                                  hi[:, c].rearrange("p k n -> p (k n)").bitcast(F32), ALU.subtract).then_inc(lo_ok, 1)

            def scores(h, c):
                dve.wait_ge(s_mm, 2 * h + 1 + c)
                for t in range(QT):
                    ins = dve.tensor_copy(m.ps[:, bass.ds(t * 2 * PH + 2 * h + c, 1), :].rearrange("p a n -> p (a n)"),
                                          psum[:, 2 + c, t * P:(t + 1) * P])
                ins.then_inc(s_ok, 1)

            split(0, 0)
            split(0, 1)
            with dve.Fori(1, rounds) as h:
                for c in range(2):
                    split(h, c)
                for c in range(2):
                    scores(h - 1, c)
            for c in range(2):
                scores(rounds - 1, c)

        @block.tensor
        def _(pe):
            def turn(h, first):
                for c in range(2):
                    pe.wait_ge(lo_ok, 2 * h + 1 + c)
                    if not first:
                        pe.wait_ge(q_ok, 2 * h - 1 + c)
                    product3(pe, psum[:, c, :], hi[:, c], lo[:, c], m.h_hi, m.h_lo).then_inc(q_mm, 1)
                for c in range(2):
                    pe.wait_ge(q_ok, 2 * h + 1 + c)
                    if not first:
                        pe.wait_ge(s_ok, 2 * h - 1 + c)
                    for t in range(QT):
                        mm = pe.matmul(psum[:, 2 + c, t * P:(t + 1) * P], qp[:, c, t * P:(t + 1) * P], keys[:, c, :],
                                       start=True, stop=True)
                    mm.then_inc(s_mm, 1)

            pe.wait_ge(keys_in, 16)
            turn(0, True)
            with pe.Fori(1, rounds) as h:
                turn(h, False)


N_TILES = NKEYS
ROUNDS = N_TILES // 2
R_ROUNDS = QT * PH
TOK = S // (ROUNDS - R_ROUNDS)
QUAD = 4
CHUNK = P
C_ROUNDS = CHUNK // TOK


def experts(nc, io, m, psum):
    with ExitStack() as ctx:
        sb = m.scratch().take

        def sem(name):
            return ctx.enter_context(nc.semaphore(name))

        raw = sb("u_raw", [P, 2, KD, P])
        hi = sb("u_hi", [P, 2, KD, P], F32R)
        lo = sb("u_lo", [P, 2, KD, P], F32R)
        act_out = sb("act_out", [P, 2, S])
        routed = m.routed
        raw_in = [sem("u_in0"), sem("u_in1")]
        hi_ok, lo_ok, a_mm, a_ok = sem("uhi_ok"), sem("ulo_ok"), sem("a_mm"), sem("a_ok")
        a_out = [sem("a_out0"), sem("a_out1")]
        r_step, routed_ok, g_exp, g_norm, slot_mm, slot_ok = (
            sem("r_step"), sem("routed_ok"), sem("g_exp"), sem("g_norm"), sem("slot_mm"), sem("slot_ok"))
        hot_ok, is1_ok, w_mm, w_ok, w_out = sem("hot_ok"), sem("is1_ok"), sem("w_mm"), sem("w_ok"), [sem("w_out0"), sem("w_out1")]
        iota_ok = sem("iota_ok")
        block = ctx.enter_context(nc.Block())

        def load(sp, r, c):
            sp.wait_ge(lo_ok, 2 * r - 1 + c)
            sp.dma_start(raw[:, c], io.uT[bass.ds(2 * r + c, 1)].rearrange("o p k n -> p (o k) n")
                         ).then_inc(raw_in[c], 16)

        def store(sp, r, c):
            sp.wait_ge(a_ok, 2 * r + 1 + c)
            sp.dma_start(io.acts[bass.ds(2 * r + c, 1)].rearrange("o p n -> p (o n)"), act_out[:, c, :]
                         ).then_inc(a_out[c], 16)

        @block.sync
        def _(sp):
            for c in range(2):
                sp.dma_start(raw[:, c], io.uT[c]).then_inc(raw_in[c], 16)

            def turn(r, last=False):
                if not last:
                    for c in range(2):
                        load(sp, r + 1, c)
                for c in range(2):
                    store(sp, r, c)

            slice_keys = NKEYS // C_ROUNDS

            def store_gates(ch, k):
                cols = slice(ch * CHUNK, (ch + 1) * CHUNK)
                sp.dma_start(io.gates[bass.ds(k, slice_keys), :, cols].rearrange("a b t -> b a t"),
                             m.dense[:, ch % 2, bass.ds(k, slice_keys), :]).then_inc(w_out[ch % 2], 16)

            with sp.Fori(0, R_ROUNDS) as r:
                turn(r)
            for ch in range(QT):
                first = R_ROUNDS + ch * C_ROUNDS
                if ch:
                    sp.wait_ge(w_ok, ch * CHUNK // QUAD)
                with sp.Fori(first, first + C_ROUNDS - (ch == QT - 1)) as r:
                    turn(r)
                    if ch:
                        store_gates(ch - 1, (r - first) * slice_keys)
                if ch == QT - 1:
                    turn(ROUNDS - 1, last=True)
                    store_gates(ch - 1, NKEYS - slice_keys)
            sp.wait_ge(w_out[0], 16 * C_ROUNDS * QT // 2)
            for c in range(2):
                sp.dma_start(m.v_raw[:, c, :], io.v[c]).then_inc(m.v_in[c], 16)
            sp.dma_start(m.x2_back[:, :, :], io.x2.rearrange("(t p) d -> p t d", p=P)).then_inc(m.x2_in, 16)
            sp.dma_start(m.final_gain[:, :], io.final_g.partition_broadcast(P)).then_inc(m.x2_in, 16)
            sp.wait_ge(w_ok, QT * CHUNK // QUAD)
            for c in range(2):
                sp.wait_ge(a_out[c], 16 * ROUNDS)
            sp.wait_ge(w_out[1], 16 * C_ROUNDS * (QT // 2 - 1))

        @block.gpsimd
        def _(pool):
            pool.iota(m.iota[:, :], pattern=[[1, P]], base=0, channel_multiplier=0,
                      allow_small_or_imprecise_dtypes=True).then_inc(iota_ok, 1)
            pool.iota(m.iota4[:, :, :], pattern=[[1, P], [0, QUAD]], base=0, channel_multiplier=0,
                      allow_small_or_imprecise_dtypes=True).then_inc(iota_ok, 1)

        @block.scalar
        def _(act):
            def split(r, c):
                act.wait_ge(raw_in[c], 16 * r + 16)
                act.activation(hi[:, c].rearrange("p k n -> p (k n)"), raw[:, c].rearrange("p k n -> p (k n)"),
                               ACT.Copy).then_inc(hi_ok, 1)

            def gelu(r, c, first=False):
                act.wait_ge(a_mm, 2 * r + 1 + c)
                if not first:
                    act.wait_ge(a_out[c], 16 * r)
                act.activation(act_out[:, c, :], psum[:, c, :], ACT.Gelu).then_inc(a_ok, 1)

            split(0, 0)
            split(0, 1)
            for c in range(2):
                gelu(0, c, True)
                split(1, c)
            with act.Fori(1, R_ROUNDS) as r:
                for c in range(2):
                    gelu(r, c)
                    split(r + 1, c)
            act.wait_ge(routed_ok, R_ROUNDS)
            act.activation(routed[:, 2], routed[:, 2], ACT.Exp).then_inc(g_exp, 1)

            def turn(r, r0, ch, last=False, between=False):
                if between:
                    for c in range(2):
                        gelu(r, c)
                        split(r + 1, c)
                for c in range(2):
                    if not between:
                        gelu(r, c)
                        if not last:
                            split(r + 1, c)
                    for b in range(2):
                        n = 2 * c + b
                        q = (r - R_ROUNDS) * (TOK // QUAD) + n
                        act.wait_ge(w_mm, q + 1)
                        off = (r - r0) * TOK + n * QUAD
                        act.activation(m.dense[:, ch % 2, :, bass.ds(off, QUAD)].rearrange("p a t -> p t a"),
                                       psum[:, 2 + n % 2, :].rearrange("p (t a) -> p t a", t=QUAD),
                                       ACT.Copy).then_inc(w_ok, 1)

            for ch in range(QT):
                r0 = R_ROUNDS + ch * C_ROUNDS
                if ch >= 2:
                    act.wait_ge(w_out[ch % 2], 16 * C_ROUNDS)
                if ch == 0:
                    turn(r0, r0, ch, between=True)
                with act.Fori(r0 + (ch == 0), r0 + C_ROUNDS - (ch == QT - 1)) as r:
                    turn(r, r0, ch)
                if ch == QT - 1:
                    turn(ROUNDS - 1, r0, ch, last=True)

        @block.vector
        def _(dve):
            def split(r, c):
                dve.wait_ge(hi_ok, 2 * r + 1 + c)
                dve.tensor_tensor(lo[:, c].rearrange("p k n -> p (k n)"), raw[:, c].rearrange("p k n -> p (k n)"),
                                  hi[:, c].rearrange("p k n -> p (k n)").bitcast(F32), ALU.subtract).then_inc(lo_ok, 1)

            STEPS = 14
            low = -3.0e38

            def route(r):
                n = [0]

                def link(ins, before_max=False):
                    n[0] += 1
                    ins.then_inc(r_step, 1)
                    dve.wait_ge(r_step, r * STEPS + n[0])
                    if before_max:
                        dve.memset(m.pause[:, :], 0.0)

                link(dve.tensor_copy(m.cur[:, :, :], m.ps[:, bass.ds(2 * r, 2), :]), True)
                dve.max(m.best[:, 0, 0:8], m.cur[:, 0, :])
                link(dve.max(m.best[:, 1, 0:8], m.cur[:, 1, :]), True)
                for c in range(2):
                    dve.max_index(m.where[:, c, 0:8], m.best[:, c, 0:8], m.cur[:, c, :])
                    ins = dve.match_replace(m.cur2[:, c, :], m.best[:, c, 0:8], m.cur[:, c, :], low)
                link(ins, True)
                dve.max(m.best[:, 0, 8:16], m.cur2[:, 0, :])
                link(dve.max(m.best[:, 1, 8:16], m.cur2[:, 1, :]), True)
                for c in range(2):
                    dve.max_index(m.where[:, c, 8:16], m.best[:, c, 8:16], m.cur2[:, c, :])
                link(dve.tensor_tensor(m.cand[:, :].rearrange("p (a b) -> p a b", a=TOPK),
                                       m.best[:, 0, :].unsqueeze(2).to_broadcast([P, TOPK, TOPK]),
                                       m.best[:, 1, :].unsqueeze(1).to_broadcast([P, TOPK, TOPK]), ALU.add))
                dve.tensor_copy(m.wheref[:, :, :], m.where[:, :, :])
                link(dve.max(m.ctop[:, 0:8], m.cand[:, :]), True)
                dve.max_index(m.cpos[:, 0:8], m.ctop[:, 0:8], m.cand[:, :])
                link(dve.match_replace(m.cand2[:, :], m.ctop[:, 0:8], m.cand[:, :], low), True)
                link(dve.max(m.ctop[:, 8:16], m.cand2[:, :]), True)
                link(dve.max_index(m.cpos[:, 8:16], m.ctop[:, 8:16], m.cand2[:, :]))
                split(r + 1, 0)
                dve.tensor_scalar(m.rc[:, 0, :], m.cpos[:, :], 4, None, ALU.logical_shift_right)
                link(dve.tensor_scalar(m.rc[:, 1, :], m.cpos[:, :], 15, None, ALU.bitwise_and))
                link(dve.tensor_copy(m.rcf[:, :, :], m.rc[:, :, :]))
                for c in range(2):
                    ins = dve.tensor_tensor(m.pick[:, c], m.rcf[:, c, :].unsqueeze(2).to_broadcast([P, TOPK, TOPK]),
                                            m.iota[:, 0:TOPK].unsqueeze(1).to_broadcast([P, TOPK, TOPK]), ALU.is_equal)
                link(ins)
                for c in range(2):
                    ins = dve.tensor_tensor(m.pick[:, c], m.pick[:, c],
                                            m.wheref[:, c, :].unsqueeze(1).to_broadcast([P, TOPK, TOPK]), ALU.mult)
                link(ins)
                for c in range(2):
                    dve.tensor_reduce(routed[:, c, bass.ds(r * TOPK, TOPK)], m.pick[:, c], X, ALU.add)
                dve.tensor_scalar(routed[:, 2, bass.ds(r * TOPK, TOPK)], m.ctop[:, :], m.ctop[:, 0:1], None,
                                  ALU.subtract).then_inc(routed_ok, 1)
                link(dve.tensor_copy(m.cur2[:, 0, 0:1], m.ctop[:, 0:1]))
                return n[0]

            dve.wait_ge(iota_ok, 2)
            split(0, 0)
            split(0, 1)
            with dve.Fori(0, R_ROUNDS) as r:
                steps = route(r)
                split(r + 1, 1)
            assert steps == STEPS, steps
            dve.wait_ge(g_exp, 1)
            dve.tensor_reduce(m.gsum[:, 0, :], routed[:, 2].rearrange("p (u k) -> p u k", k=TOPK), X, ALU.add
                              ).then_inc(g_norm, 1)
            dve.wait_ge(g_norm, 1)
            dve.reciprocal(m.gsum[:, 1, :], m.gsum[:, 0, :]).then_inc(g_norm, 1)
            dve.wait_ge(g_norm, 2)
            g3 = routed[:, 2].rearrange("p (u k) -> p u k", k=TOPK)
            dve.tensor_tensor(g3, g3, m.gsum[:, 1, :].unsqueeze(2).to_broadcast([P, QT * PH, TOPK]), ALU.mult
                              ).then_inc(g_norm, 1)
            for n in range(3):
                dve.wait_ge(slot_mm, n + 1)
                dve.tensor_copy((m.slot_key[:, 0], m.slot_key[:, 1], m.slot_gate[:, 0])[n], psum[:, 4 + n, :]
                                ).then_inc(slot_ok, 1)
            n_slot = 3
            src = psum[:, 6, :]
            for n in range(1, 3):
                dve.wait_ge(slot_ok, n_slot)
                dve.tensor_tensor(m.slot_rest[:, :], src, m.slot_gate[:, n - 1], ALU.subtract).then_inc(slot_ok, 1)
                dve.wait_ge(slot_ok, n_slot + 1)
                dve.tensor_copy(m.slot_gate[:, n], m.slot_rest[:, :]).then_inc(slot_ok, 1)
                n_slot += 2
                src = m.slot_rest[:, :]
            dve.wait_ge(slot_ok, n_slot)

            def hots(r, n, first=False):
                q = (r - R_ROUNDS) * (TOK // QUAD) + n
                if not first:
                    dve.wait_ge(w_mm, q - 1)

                def row(x):
                    return x[:, bass.ds(q * QUAD, QUAD)].unsqueeze(1).to_broadcast([P, NKEYS, QUAD])

                dve.tensor_tensor(m.is1[:, n % 2], m.iota4[:, :, :], row(m.slot_key[:, 0]), ALU.is_equal
                                  ).then_inc(is1_ok, 1)
                dve.tensor_tensor(m.hot2[:, n % 2], m.iota4[:, :, :], row(m.slot_key[:, 1]), ALU.is_equal)
                dve.wait_ge(is1_ok, q + 1)
                for g in range(3):
                    ins = dve.tensor_tensor(m.hot1[:, n % 2, g], m.is1[:, n % 2], row(m.slot_gate[:, g]), ALU.mult)
                ins.then_inc(hot_ok, 1)

            def turn(r, first=False, last=False):
                for n in range(TOK // QUAD):
                    if not last and n == 2:
                        split(r + 1, 0)
                    hots(r, n, first and n < 2)
                if not last:
                    split(r + 1, 1)

            turn(R_ROUNDS, first=True)
            with dve.Fori(R_ROUNDS + 1, ROUNDS - 1) as r:
                turn(r)
            turn(ROUNDS - 1, last=True)

        @block.tensor
        def _(pe):
            def tile(r, c, first=False):
                pe.wait_ge(lo_ok, 2 * r + 1 + c)
                if not first:
                    pe.wait_ge(a_ok, 2 * r - 1 + c)
                product3(pe, psum[:, c, :], hi[:, c], lo[:, c], m.h_hi, m.h_lo).then_inc(a_mm, 1)

            def gates(r, n, first):
                q = (r - R_ROUNDS) * (TOK // QUAD) + n
                if not (first and n < 2):
                    pe.wait_ge(w_ok, q - 1)
                pe.wait_ge(hot_ok, q + 1)
                for j in range(QUAD):
                    for g in range(3):
                        mm = pe.matmul(psum[:, 2 + n % 2, j * P:(j + 1) * P], m.hot2[:, n % 2, :, j],
                                       m.hot1[:, n % 2, g, :, j], start=(g == 0), stop=(g == 2))
                mm.then_inc(w_mm, 1)

            tile(0, 0, True)
            tile(0, 1, True)
            with pe.Fori(1, R_ROUNDS) as r:
                for c in range(2):
                    tile(r, c)

            def turn(r):
                for c in range(2):
                    tile(r, c)
                    gates(r, 2 * c, False)
                    gates(r, 2 * c + 1, False)

            tile(R_ROUNDS, 0)
            pe.wait_ge(g_norm, 3)
            for n in range(3):
                for t in range(QT):
                    mm = pe.transpose(psum[:, 4 + n, t * P:(t + 1) * P], routed[:, n, t * P:(t + 1) * P], m.eye[:, :])
                mm.then_inc(slot_mm, 1)
            tile(R_ROUNDS, 1)
            for n in range(TOK // QUAD):
                gates(R_ROUNDS, n, n < 2)
            with pe.Fori(R_ROUNDS + 1, ROUNDS) as r:
                turn(r)


def combine(nc, io, m, psum):
    with ExitStack() as ctx:
        sb = m.scratch().take

        def sem(name):
            return ctx.enter_context(nc.semaphore(name))

        raw, x2, fg = m.v_raw, m.x2_back, m.final_gain
        hi = sb("v_hi", [P, 2, D], F32R)
        lo = sb("v_lo", [P, 2, D], F32R)
        acts = sb("acts_in", [P, 2, S])
        gates = sb("gates_in", [P, 2, S])
        wa = sb("wa", [P, 2, S])
        wa_hi = sb("wa_hi", [P, 2, S], F32R)
        wa_lo = sb("wa_lo", [P, 2, S], F32R)
        early = m.early()
        junk = early.take("fjunk", [P, D])
        stat = early.take("fstat", [P, 4, QT])
        v_in, x2_in = m.v_in, m.x2_in
        gates_first, gates_rest = sem("gates_first"), sem("gates_rest")
        ag_in = [sem("ag_in0"), sem("ag_in1")]
        vhi_ok, vlo_ok, wa_ok, wahi_ok, walo_ok, o_mm = (
            sem("vhi_ok"), sem("vlo_ok"), sem("wa_ok"), sem("wahi_ok"), sem("walo_ok"), sem("o2_mm"))
        f_add, f_sq, f_var, f_std, f_rs, f_sc, f_ok, f_out = (
            sem("f_add"), sem("f_sq"), sem("f_var"), sem("f_std"), sem("f_rs"), sem("f_sc"), sem("f_ok"), sem("f_out"))
        block = ctx.enter_context(nc.Block())

        @block.sync
        def _(sp):
            def load(r, c):
                sp.dma_start(raw[:, c, :], io.v[bass.ds(2 * r + c, 1)].rearrange("o p n -> p (o n)")
                             ).then_inc(v_in[c], 16)

            slices = CHUNK // TOK
            n_keys = NKEYS // slices

            def store_gates(k):
                cols = slice((QT - 1) * CHUNK, QT * CHUNK)
                keys = slice(k * n_keys, (k + 1) * n_keys)
                sp.dma_start(io.gates[keys, :, cols].rearrange("a b t -> b a t"), m.dense[:, (QT - 1) % 2, keys, :]
                             ).then_inc(gates_rest if k else gates_first, 16)

            store_gates(0)

            def turn(r):
                for c in range(2):
                    sp.wait_ge(vlo_ok, 2 * r - 1 + c)
                    load(r, c)

            for r in range(1, slices):
                turn(r)
                store_gates(r)
            with sp.Fori(slices, ROUNDS) as r:
                turn(r)
            sp.wait_ge(gates_rest, 16 * (slices - 1))
            for t in range(QT):
                sp.wait_ge(f_ok, t + 1)
                sp.dma_start(io.out.rearrange("(t p) d -> t p d", p=P)[t], x2[:, t, :]).then_inc(f_out, 16)
            sp.wait_ge(f_out, 16 * QT)

        @block.gpsimd
        def _(pool):
            for c in range(2):
                pool.dma_start(acts[:, c, :], io.acts[c]).then_inc(ag_in[c], 16)
            pool.wait_ge(gates_first, 16)
            for c in range(2):
                pool.dma_start(gates[:, c, :], io.gates[c]).then_inc(ag_in[c], 16)

            def turn(r):
                for c in range(2):
                    pool.wait_ge(wa_ok, 2 * r - 1 + c)
                    pool.dma_start(acts[:, c, :], io.acts[bass.ds(2 * r + c, 1)].rearrange("o p n -> p (o n)")
                                   ).then_inc(ag_in[c], 16)
                    pool.dma_start(gates[:, c, :], io.gates[bass.ds(2 * r + c, 1)].rearrange("o p n -> p (o n)")
                                   ).then_inc(ag_in[c], 16)

            rounds = NKEYS // (CHUNK // TOK) // 2
            with pool.Fori(1, rounds) as r:
                turn(r)
            pool.wait_ge(gates_rest, 16 * (CHUNK // TOK - 1))
            with pool.Fori(rounds, ROUNDS) as r:
                turn(r)

        @block.scalar
        def _(act):
            def split(r, c, first=False):
                act.wait_ge(v_in[c], 16 * r + 16)
                if not first:
                    act.wait_ge(o_mm, 2 * r - 1 + c)
                act.activation(hi[:, c, :], raw[:, c, :], ACT.Copy).then_inc(vhi_ok, 1)
                act.wait_ge(wa_ok, 2 * r + 1 + c)
                act.activation(wa_hi[:, c, :], wa[:, c, :], ACT.Copy).then_inc(wahi_ok, 1)

            split(0, 0, True)
            split(0, 1, True)
            with act.Fori(1, ROUNDS) as r:
                for c in range(2):
                    split(r, c)
            for t in range(QT):
                act.wait_ge(f_add, t + 1)
                if t:
                    act.wait_ge(f_sq, t)
                act.activation(junk[:, :], x2[:, t, :], ACT.Square, accum_out=stat[:, 0, t:t + 1]).then_inc(f_sq, 1)
                act.wait_ge(f_var, t + 1)
                act.activation(stat[:, 2, t:t + 1], stat[:, 1, t:t + 1], ACT.Sqrt).then_inc(f_std, 1)

        @block.vector
        def _(dve):
            def split(r, c, first=False):
                dve.wait_ge(ag_in[c], 32 * r + 32)
                if not first:
                    dve.wait_ge(walo_ok, 2 * r - 1 + c)
                    dve.wait_ge(wahi_ok, 2 * r - 1 + c)
                dve.tensor_tensor(wa[:, c, :], acts[:, c, :], gates[:, c, :], ALU.mult).then_inc(wa_ok, 1)
                dve.wait_ge(vhi_ok, 2 * r + 1 + c)
                dve.tensor_tensor(lo[:, c, :], raw[:, c, :], hi[:, c, :].bitcast(F32), ALU.subtract).then_inc(vlo_ok, 1)
                dve.wait_ge(wahi_ok, 2 * r + 1 + c)
                dve.tensor_tensor(wa_lo[:, c, :], wa[:, c, :], wa_hi[:, c, :].bitcast(F32), ALU.subtract
                                  ).then_inc(walo_ok, 1)

            split(0, 0, True)
            split(0, 1, True)
            with dve.Fori(1, ROUNDS) as r:
                for c in range(2):
                    split(r, c)
            dve.wait_ge(x2_in, 32)
            dve.wait_ge(o_mm, N_TILES)
            for t in range(QT):
                xt = x2[:, t, :].rearrange("p (b n) -> p b n", b=2)
                dve.tensor_tensor(xt, psum[:, 2 * t:2 * t + 2, :], xt, ALU.add).then_inc(f_add, 1)
            for t in range(QT):
                dve.wait_ge(f_sq, t + 1)
                dve.tensor_scalar(stat[:, 1, t:t + 1], stat[:, 0, t:t + 1], 1.0 / D, EPS, ALU.mult, ALU.add
                                  ).then_inc(f_var, 1)
                dve.wait_ge(f_std, t + 1)
                dve.reciprocal(stat[:, 3, t:t + 1], stat[:, 2, t:t + 1]).then_inc(f_rs, 1)
                dve.wait_ge(f_rs, t + 1)
                dve.scalar_tensor_tensor(out=x2[:, t, :], in0=x2[:, t, :], scalar=stat[:, 3, t:t + 1], in1=fg[:, :],
                                         op0=ALU.mult, op1=ALU.mult).then_inc(f_ok, 1)

        @block.tensor
        def _(pe):
            def tile(r, c, first=False, last=False):
                pe.wait_ge(vlo_ok, 2 * r + 1 + c)
                pe.wait_ge(walo_ok, 2 * r + 1 + c)
                for t in range(QT):
                    ts = slice(t * P, (t + 1) * P)
                    for b in range(2):
                        bs = slice(b * S, (b + 1) * S)
                        for n, (w, v) in enumerate(((wa_hi, hi), (wa_hi, lo), (wa_lo, hi))):
                            mm = pe.matmul(psum[:, 2 * t + b, :], w[:, c, ts], v[:, c, bs],
                                           start=(first and n == 0), stop=(last and n == 2), skip_group_check=True)
                mm.then_inc(o_mm, 1)

            tile(0, 0, first=True)
            tile(0, 1)
            with pe.Fori(1, ROUNDS - 1) as r:
                for c in range(2):
                    tile(r, c)
            tile(ROUNDS - 1, 0)
            tile(ROUNDS - 1, 1, last=True)



def hymba_peer_layer(nc, io, until=6):
    KB = 1024
    m = Memory()
    base = (nc.sbuf_base + 63) // 64 * 64
    end = nc.sbuf_usable_end
    shared = base + 1 * KB
    late = shared + 32 * KB
    rows = late + 16 * KB
    rest = rows + 16 * KB

    top = Region(nc, base, shared)
    m.eye = top.take("eye", [P, P])
    m.iota = top.take("iota", [P, P])
    m.early = lambda: Region(nc, shared, late)
    m.late = lambda: Region(nc, late, rows)
    m.x = Region(nc, rows, rest).take("x_rows", [P, QT, D])
    kept = Region(nc, rest, end)
    m.mask = kept.take("mask", [P, S])
    m.seen = kept.take("seen", [P, 1])
    m.bias = kept.take("bias", [P, HEADS, BIAS_W])
    m.rows = kept.take("rows", [P, QT, ROW_W])
    m.kT = kept.take("kT", [P, 2, S])
    m.qT = kept.take("qT", [P, 4, S])
    m.kcT = kept.take("kcT", [P, N_CMP])
    m.vc = kept.take("vc", [N_CMP, GROUPS * DH])
    m.gate = kept.take("gate", [P, QT, 3 * HEADS])
    m.lstat = kept.take("lstat", [P, 3, 2 * QT])
    m.lsum = kept.take("lsum", [P, QT])
    m.inv = kept.take("inv", [P, HALF])
    m.pos = kept.take("pos", [P, QT], I32)
    values_at = kept.at
    m.mla_values = lambda: Region(nc, values_at, values_at + 8 * KB)
    m.vm = kept.take("vm", [P, QT, HEADS * DH])
    attend_free = kept.at
    m.wq_up = kept.take("wq_up", [P, 2, HEADS * QK])
    m.wkv_up = kept.take("wkv_up", [P, HEADS * (NOPE + DH)])
    m.latT = kept.take("latT", [P, 3, S])

    with ExitStack() as own:
        psum = own.enter_context(nc.psum_tensor("psum", [P, 8, S], F32))
        m.scratch = lambda: Region(nc, kept.at, end)
        project(nc, io, m, psum)
        if until < 2:
            return m
        early = m.early()
        m.qmT = early.take("qmT", [QK, HEADS, S])
        m.kmT = early.take("kmT", [QK, HEADS, S])
        latents(nc, io, m, psum)
        m.scratch = lambda: Region(nc, attend_free, end)
        m.o = m.late().take("o", [P, QT, 2, NSA_W])
        attend(nc, io, m, psum)
        if until < 3:
            return m
        parts = m.early()
        m.h_hi = parts.take("h_hi", [P, KD, S], F32R)
        m.h_lo = parts.take("h_lo", [P, KD, S], F32R)
        m.scratch = lambda: Region(nc, rest, end)
        output(nc, io, m, psum)
        if until < 4:
            return m
        m.dense = Region(nc, late, end).take("dense", [P, 2, NKEYS, CHUNK])
        after = late + 2 * NKEYS * CHUNK * 4
        before = Region(nc, late, after)
        m.ps = before.take("peer_s", [P, QT * PH * 2, NKEYS])
        m.cur = before.take("cur", [P, 2, NKEYS])
        m.cur2 = before.take("cur2", [P, 2, NKEYS])
        m.best = before.take("best", [P, 2, TOPK])
        m.where = before.take("where", [P, 2, TOPK], U32)
        m.wheref = before.take("wheref", [P, 2, TOPK])
        m.cand = before.take("cand", [P, TOPK * TOPK])
        m.cand2 = before.take("cand2", [P, TOPK * TOPK])
        m.ctop = before.take("ctop", [P, TOPK])
        m.cpos = before.take("cpos", [P, TOPK], U32)
        m.rc = before.take("rc", [P, 2, TOPK], U32)
        m.rcf = before.take("rcf", [P, 2, TOPK])
        m.pause = before.take("pause", [P, 1])
        m.pick = before.take("pick", [P, 2, TOPK, TOPK])
        m.gsum = before.take("gsum", [P, 2, QT * PH])
        m.scratch = lambda: Region(nc, after, end)
        peer_scores(nc, io, m, psum)
        if until < 5:
            return m
        slots = Region(nc, after, end)
        m.slot_key = slots.take("slot_key", [P, 2, S], BF16)
        m.slot_gate = slots.take("slot_gate", [P, 3, S], BF16)
        m.iota4 = slots.take("iota4", [P, NKEYS, QUAD], BF16)
        turned = Region(nc, slots.at, end)
        m.routed = turned.take("routed", [P, 3, S])
        m.slot_rest = turned.take("slot_rest", [P, S])
        m.is1 = slots.take("is1", [P, 2, NKEYS, QUAD], BF16)
        m.hot2 = slots.take("hot2", [P, 2, NKEYS, QUAD], BF16)
        m.hot1 = slots.take("hot1", [P, 2, 3, NKEYS, QUAD], BF16)
        ahead = Region(nc, late, after)
        m.v_raw = ahead.take("v_raw", [P, 2, D])
        m.x2_back = ahead.take("x2_back", [P, QT, D])
        m.final_gain = ahead.take("final_gain", [P, D])
        m.v_in = [own.enter_context(nc.semaphore("v_in0")), own.enter_context(nc.semaphore("v_in1"))]
        m.x2_in = own.enter_context(nc.semaphore("x2_in"))
        m.scratch = lambda: Region(nc, slots.at, end)
        experts(nc, io, m, psum)
        if until < 6:
            return m
        m.scratch = lambda: Region(nc, ahead.at, late + NKEYS * CHUNK * 4)
        combine(nc, io, m, psum)
    return m


def bucket_onehot():
    dist = S - 1 - np.arange(BIAS_L)
    d = np.maximum(dist, 1).astype(np.float32)
    exact = BUCKETS // 2
    large = exact + (np.log(d / exact) / np.float32(np.log(2048 / exact)) * (BUCKETS - exact)).astype(np.int32)
    bucket = np.where(dist < exact, np.maximum(dist, 0), np.minimum(large, BUCKETS - 1))
    bucket = np.where(dist < 0, BUCKETS, bucket)
    return (np.arange(BUCKETS + 1)[:, None] == bucket[None, :]).astype(np.float32)


def layout(inputs):
    c = np.ascontiguousarray
    a = {k: np.asarray(v) for k, v in inputs.items()}

    def tiles(w):
        return c(w.reshape(-1, P, w.shape[1]).transpose(1, 0, 2))

    def column_tiles(w):
        return c(w.reshape(-1, P, w.shape[1] // P, P).transpose(2, 1, 0, 3))

    sizes = [NSA_W] + [GROUPS * DH] * 6 + [3 * HEADS, Q_LORA, KV_LORA, ROPE]
    cuts = np.split(a["w_in"][0], np.cumsum(sizes)[:-1], axis=1)
    q, kc, vc, ks, vs, kw, vw, gates, cq, ckv, kr = cuts
    q = q.reshape(D, GROUPS, HEADS // GROUPS, DH).transpose(0, 2, 1, 3).reshape(D, NSA_W)
    kv_up = a["w_kv_up"][0].reshape(KV_LORA, HEADS, 2, NOPE).transpose(0, 2, 1, 3).reshape(KV_LORA, -1)
    pairs = a["cmp_pos"][0].reshape(LP, P).T
    return {
        "x": c(a["x"].reshape(S, D)),
        "positions": c(a["positions"].reshape(QT, P).T),
        "g1": c(a["norm1_g"][0].reshape(KD, P).T),
        "qkvg": c(np.concatenate([a["q_norm_g"][0], a["kv_norm_g"][0]]).reshape(3, P).T),
        "cmp_posT": c(pairs),
        "w_rows": tiles(np.concatenate([cq, ckv, vs, vw, kr, gates], axis=1)),
        "w_cols": column_tiles(np.concatenate([kc, vc, ks, kw, q], axis=1)),
        "w1k": tiles(a["cmp_k_w1"][0]),
        "w1v": tiles(a["cmp_v_w1"][0]),
        "w2": c(np.stack([tiles(a["cmp_k_w2"][0]), tiles(a["cmp_v_w2"][0])], axis=1)),
        "t5": c(a["t5_bias"]),
        "bucket_onehot": bucket_onehot(),
        "inv_freq": (10000.0 ** (-np.arange(HALF, dtype=np.float32) / HALF)).astype(np.float32),
        "wq_up": tiles(a["w_q_up"][0]),
        "wkv_up": c(kv_up),
        "grp_gain": c(np.concatenate([a["grp_norm_nsa"][0], a["grp_norm_mla"][0]]).reshape(KD, P).T),
        "w_out": tiles(a["w_out"][0]),
        "g2": c(a["norm2_g"][0].reshape(KD, P).T),
        "wq": column_tiles(a["peer_wq"][0]),
        "keysT": c(np.stack([a["peer_keys1"][0].T, a["peer_keys2"][0].T], axis=1)),
        "uT": c(a["peer_u"][0].reshape(NKEYS, P, KD, P).transpose(0, 3, 2, 1)),
        "v": c(a["peer_v"][0].reshape(NKEYS, P, D)),
        "final_g": c(a["final_g"]),
    }


class Dram:

    def __init__(self, nc, arrays):
        def given(name):
            a = arrays[name]
            return nc.dram_tensor(name, a.shape, mybir.dt.from_np(a.dtype), kind="ExternalInput").ap()

        def scratch(name, shape):
            return nc.dram_tensor(name, shape, F32, kind="Internal").ap()

        self.x = given("x")
        self.positions = given("positions")
        self.g1 = given("g1")
        self.qkvg = given("qkvg")
        self.cmp_posT = given("cmp_posT")
        self.w_rows = given("w_rows")
        self.w_cols = given("w_cols")
        self.w1k = given("w1k")
        self.w1v = given("w1v")
        self.w2 = given("w2")
        self.t5 = given("t5")
        self.bucket_onehot = given("bucket_onehot")
        self.inv_freq = given("inv_freq")
        self.wq_up = given("wq_up")
        self.wkv_up = given("wkv_up")
        self.grp_gain = given("grp_gain")
        self.w_out = given("w_out")
        self.g2 = given("g2")
        self.wq = given("wq")
        self.keysT = given("keysT")
        self.uT = given("uT")
        self.v = given("v")
        self.final_g = given("final_g")
        self.bias_rows = scratch("bias_rows", (HEADS, BIAS_L))
        self.bias_rep = scratch("bias_rep", (P, HEADS * BIAS_L))
        self.x2 = scratch("x2", (S, D))
        self.acts = scratch("acts", (NKEYS, P, S))
        self.gates = scratch("gates", (NKEYS, P, S))
        self.out = nc.dram_tensor("out", (S, D), F32, kind="ExternalOutput").ap()


def kernel(**inputs):
    import concourse.bacc as bacc
    from concourse.bass_utils import run_bass_kernel_spmd

    arrays = layout(inputs)
    nc = bacc.Bacc("TRN2", target_bir_lowering=False, num_devices=1)
    hymba_peer_layer(nc, Dram(nc, arrays))
    result = run_bass_kernel_spmd(nc, [arrays], core_ids=[0])
    return result.results[0]["out"].reshape(1, S, D)
```

```python
from contextlib import ExitStack

import numpy as np

import concourse.bass as bass
from concourse import mybir

F32 = mybir.dt.float32
F32R = mybir.dt.float32r
BF16 = mybir.dt.bfloat16
I32 = mybir.dt.int32
U32 = mybir.dt.uint32
ALU = mybir.AluOpType
ACT = mybir.ActivationFunctionType
X = mybir.AxisListType.X

P = 128
D = 1024
S = 512
QT = S // P
KD = D // P
DH = 64
HEADS = 8
GROUPS = 2
NSA_W = HEADS * DH
CMP_LEN, CMP_STRIDE, CMP_HID = 32, 16, 256
N_CMP = (S - CMP_LEN) // CMP_STRIDE + 1
LP = CMP_LEN * DH // P
HT = CMP_HID // P
Q_LORA, KV_LORA, NOPE, ROPE = 256, 128, 64, 32
HALF = ROPE // 2
QK = NOPE + ROPE
MLA_SCALE = QK ** -0.5
NSA_SCALE = DH ** -0.5
EPS = 1e-6
NEG = -1e30
BUCKETS = 32
R_CQ, R_CKV, R_VS, R_VW, R_KR, R_G = 0, 256, 384, 512, 640, 672
ROW_W = 696
C_KC, C_VC, C_KS, C_KW, C_Q = 0, 1, 2, 3, 4
N_COLS = 8
BIAS_L = 1024
BIAS_W = 896
NKEYS = 128
TOPK = 16
PH = 8
EXP_BUF = 2
TWO_PI_HI = 6.28125
TWO_PI_MID = float(np.float32(0.0019350051879882812))
TWO_PI_LO = float(2 * np.pi - 6.28125 - 0.0019350051879882812)
ROUND = 12582912.0
PI_IN = 3.1415925


class Memory:
    pass


class Region:

    def __init__(self, nc, start, end):
        self.nc, self.at, self.end = nc, start, end

    def take(self, name, shape, dt=F32):
        size = int(np.prod(shape[1:])) * (2 if dt == BF16 else 4)
        tensor = self.nc.alloc_sbuf_tensor_at(name, shape, dt, offset=self.at)
        self.at += (size + 31) // 32 * 32
        assert self.at <= self.end, (name, self.at, self.end)
        return tensor


def project(nc, io, m, psum):
    with ExitStack() as ctx:
        sb = m.scratch().take

        def sem(name):
            return ctx.enter_context(nc.semaphore(name))

        xn = m.late().take("xn", [P, QT, D])
        early = m.early()
        hT = early.take("hT", [P, KD, S])
        w_rows = sb("w_rows", [P, KD, ROW_W])
        w_col = sb("w_col", [P, 2, KD, P])
        cT = sb("cT", [P, 2, S])
        pairs = m.mla_values().take("pairs", [P, 2, GROUPS, S])
        blk = sb("blk", [P, 2, LP, GROUPS, N_CMP])
        w1 = w_rows[:, :, :].rearrange("p k n -> p (k n)")[:, 0:LP * CMP_HID].rearrange(
            "p (l c) -> p l c", l=LP)
        w1v = early.take("w1v", [P, LP, CMP_HID])
        w2 = sb("w2", [P, 2, HT, DH])
        hid = sb("hid", [P, 2, HT, GROUPS * N_CMP])
        posT = sb("posT", [P, LP])
        g1 = sb("g1", [P, KD])
        qkvg = sb("qkvg", [P, 3])
        t5x = sb("t5x", [BUCKETS + 1, HEADS])
        onehot = sb("onehot", [BUCKETS + 1, BIAS_L])
        brow = sb("brow", [HEADS, BIAS_L])
        stat = sb("stat", [P, 4, 4])
        lat = sb("lat", [P, QT, 384])
        junk = sb("junk", [P, D])

        x_in = [sem(f"x_in{t}") for t in range(QT)]
        wr_in, small_in, w2_in, t5_in, up_in = sem("wr_in"), sem("small_in"), sem("w2_in"), sem("t5_in"), sem("up_in")
        wc_in = [sem("wc_in0"), sem("wc_in1")]
        w1_in, w1v_in = sem("w1_in"), sem("w1v_in")
        x_sq, x_var, x_std, x_rs, xn_ok = sem("x_sq"), sem("x_var"), sem("x_std"), sem("x_rs"), sem("xn_ok")
        xT_ok, h_ok = sem("xT_ok"), sem("h_ok")
        rows_mm, rows_a, rows_v = sem("rows_mm"), sem("rows_a"), sem("rows_v")
        cols_mm, cols_a, cols_v = sem("cols_mm"), sem("cols_a"), sem("cols_v")
        pair_ok, blk_ok, hid_mm, hid_ok, cmp_mm, cmp_ok = (
            sem("pair_ok"), sem("blk_ok"), sem("hid_mm"), sem("hid_ok"), sem("cmp_mm"), sem("cmp_ok"))
        lat_sq, lat_var, lat_std, lat_rs, lat_ok, latT_mm, latT_ok = (
            sem("lat_sq"), sem("lat_var"), sem("lat_std"), sem("lat_rs"), sem("lat_ok"), sem("latT_mm"), sem("latT_ok"))
        b_mm, b_row, b_out, b_rep, b_tile = sem("b_mm"), sem("b_row"), sem("b_out"), sem("b_rep"), sem("b_tile")
        neg_ok, eye_ok, ones_ok = sem("neg_ok"), sem("eye_ok"), sem("ones_ok")

        block = ctx.enter_context(nc.Block())

        @block.sync
        def _(sp):
            for t in range(QT):
                sp.dma_start(m.x[:, t, :], io.x.rearrange("(t p) d -> t p d", p=P)[t]).then_inc(x_in[t], 16)
            sp.dma_start(g1[:, :], io.g1).then_inc(small_in, 16)
            sp.dma_start(qkvg[:, :], io.qkvg).then_inc(small_in, 16)
            sp.dma_start(posT[:, :], io.cmp_posT).then_inc(small_in, 16)
            sp.dma_start(w_rows[:, :, :], io.w_rows).then_inc(wr_in, 16)
            for j in range(N_COLS):
                if j >= 2:
                    sp.wait_ge(cols_mm, j - 1)
                sp.dma_start(w_col[:, j % 2], io.w_cols[j]).then_inc(wc_in[j % 2], 16)
                if j == 1:
                    sp.dma_start(w1v[:, :, :], io.w1v).then_inc(w1v_in, 16)
                if j == 2:
                    sp.wait_ge(rows_mm, QT)
                    sp.dma_start(w1, io.w1k).then_inc(w1_in, 16)

        @block.gpsimd
        def _(pool):
            pool.memset(m.eye[:, :], 0.0).then_inc(eye_ok, 1)
            pool.wait_ge(eye_ok, 1)
            pool.affine_select(out=m.eye[:, :], in_=m.eye[:, :], compare_op=ALU.not_equal, fill=1.0,
                               base=0, pattern=[[-1, P]], channel_multiplier=1).then_inc(eye_ok, 1)
            pool.memset(m.mask[:, :], 0.0).then_inc(ones_ok, 1)
            pool.memset(m.seen[:, :], 1.0).then_inc(ones_ok, 1)
            pool.wait_ge(ones_ok, 2)
            pool.affine_select(out=m.mask[:, S - P:S], in_=m.mask[:, S - P:S], compare_op=ALU.is_ge, fill=NEG,
                               base=0, pattern=[[-1, P]], channel_multiplier=1)
            pool.affine_select(out=m.seen[:, :], in_=m.seen[:, :], compare_op=ALU.is_ge, fill=0.0,
                               base=-(CMP_LEN - 1), pattern=[[0, 1]], channel_multiplier=1).then_inc(ones_ok, 1)
            for c in range(2):
                pool.wait_ge(cols_a if c == 0 else cols_v, 1)
                for g in range(GROUPS):
                    src = cT[g * DH:(g + 1) * DH, c, :]
                    pool.dma_start(pairs[0:DH, c, g, :], src).then_inc(pair_ok, 16)
                    pool.dma_start(pairs[DH:P, c, g, 0:S - 1], src[:, 1:S]).then_inc(pair_ok, 16)
            pool.wait_ge(b_row, 1)
            pool.dma_start(io.bias_rows, brow[:, :]).then_inc(b_out, 16)
            pool.wait_ge(b_out, 16)
            pool.dma_start(io.bias_rep.rearrange("p (h n) -> p h n", h=HEADS),
                           io.bias_rows.partition_broadcast(P)).then_inc(b_rep, 16)
            pool.wait_ge(b_rep, 16)
            skew = bass.AP(tensor=io.bias_rep.tensor, offset=P - 1,
                           ap=[[HEADS * BIAS_L - 1, P], [BIAS_L, HEADS], [1, BIAS_W]])
            pool.dma_start(m.bias[:, :, :], skew).then_inc(b_tile, 16)
            pool.wait_ge(b_tile, 16)
            pool.wait_ge(pair_ok, 128)
            pool.wait_ge(ones_ok, 3)

        @block.scalar
        def _(act):
            act.dma_start(t5x[0:BUCKETS, :], io.t5).then_inc(t5_in, 16)
            act.dma_start(onehot[:, :], io.bucket_onehot).then_inc(t5_in, 16)
            act.dma_start(w2[:, :, :, :], io.w2).then_inc(w2_in, 16)
            act.dma_start(m.wq_up[:, :, :], io.wq_up).then_inc(up_in, 16)
            act.dma_start(m.wkv_up[:, :], io.wkv_up).then_inc(up_in, 16)
            act.dma_start(m.inv[:, :], io.inv_freq.partition_broadcast(P)).then_inc(up_in, 16)
            act.dma_start(m.pos[:, :], io.positions).then_inc(up_in, 16)
            for t in range(QT):
                act.wait_ge(x_in[t], 16)
                act.activation(xn[:, t, :], m.x[:, t, :], ACT.Square, accum_out=stat[:, 0, t:t + 1]).then_inc(x_sq, 1)
            act.wait_ge(x_var, 1)
            act.activation(stat[:, 2, :], stat[:, 1, :], ACT.Sqrt).then_inc(x_std, 1)
            act.wait_ge(small_in, 48)
            for k in range(0, KD, 2):
                act.wait_ge(xT_ok, 1)
                act.activation(hT[:, k, :], psum[:, k, :], ACT.Copy, scale=g1[:, k:k + 1]).then_inc(h_ok, 1)
            for t in range(QT):
                act.wait_ge(rows_mm, t + 1)
                act.activation(m.rows[:, t, 0:S], psum[:, 2 * t, :], ACT.Copy).then_inc(rows_a, 1)
            for j in (C_KC, C_KS):
                act.wait_ge(cols_mm, j + 1)
                dst = cT[:, 0, :] if j == C_KC else m.kT[:, 0, :]
                act.activation(dst, psum[:, j, :], ACT.Copy).then_inc(cols_a, 1)
            for c in (0, 1):
                for t in range(QT):
                    act.wait_ge(rows_a, t + 1)
                    lo, hi = (R_CQ, R_CKV) if c == 0 else (R_CKV, R_VS)
                    if c + t:
                        act.wait_ge(lat_sq, c * QT + t)
                    act.activation(junk[:, 0:hi - lo], m.rows[:, t, lo:hi], ACT.Square,
                                   accum_out=stat[:, 3, t:t + 1] if c == 0 else m.lsum[:, t:t + 1]).then_inc(lat_sq, 1)
            for j in (C_Q, C_Q + 2):
                act.wait_ge(cols_mm, j + 1)
                act.activation(m.qT[:, j - C_Q, :], psum[:, j, :], ACT.Copy, scale=NSA_SCALE).then_inc(cols_a, 1)
            act.wait_ge(lat_var, 2)
            act.activation(m.lstat[:, 1, :], m.lstat[:, 0, :], ACT.Sqrt).then_inc(lat_std, 1)
            for c in range(3):
                act.wait_ge(latT_mm, c + 1)
                act.activation(m.latT[:, c, :], psum[:, c, :], ACT.Copy, scale=qkvg[:, c:c + 1]).then_inc(latT_ok, 1)
            for c in range(2):
                act.wait_ge(hid_mm, c + 1)
                act.activation(hid[:, c, :, :], psum[:, 4 + c, 0:HT * GROUPS * N_CMP].rearrange(
                    "p (h n) -> p h n", h=HT), ACT.Gelu).then_inc(hid_ok, 1)
            act.wait_ge(w1_in, 16)

        @block.vector
        def _(dve):
            dve.memset(t5x[BUCKETS:BUCKETS + 1, :], NEG).then_inc(neg_ok, 1)
            dve.wait_ge(x_sq, QT)
            dve.tensor_scalar(stat[:, 1, :], stat[:, 0, :], 1.0 / D, EPS, ALU.mult, ALU.add).then_inc(x_var, 1)
            dve.wait_ge(x_std, 1)
            dve.reciprocal(stat[:, 0, :], stat[:, 2, :]).then_inc(x_rs, 1)
            dve.wait_ge(x_rs, 1)
            for t in range(QT):
                dve.tensor_scalar(xn[:, t, :], m.x[:, t, :], stat[:, 0, t:t + 1], None, ALU.mult).then_inc(xn_ok, 1)
            dve.wait_ge(small_in, 48)
            for k in range(1, KD, 2):
                dve.wait_ge(xT_ok, 1)
                dve.tensor_scalar(hT[:, k, :], psum[:, k, :], g1[:, k:k + 1], None, ALU.mult).then_inc(h_ok, 1)
            for t in range(QT):
                dve.wait_ge(rows_mm, t + 1)
                dve.tensor_copy(m.rows[:, t, S:ROW_W], psum[:, 2 * t + 1, 0:ROW_W - S]).then_inc(rows_v, 1)
            for j in (C_VC, C_KW):
                dve.wait_ge(cols_mm, j + 1)
                dst = cT[:, 1, :] if j == C_VC else m.kT[:, 1, :]
                dve.tensor_copy(dst, psum[:, j, :]).then_inc(cols_v, 1)
            dve.wait_ge(lat_sq, 2 * QT)
            dve.tensor_scalar(m.lstat[:, 0, 0:QT], stat[:, 3, :], 1.0 / Q_LORA, EPS, ALU.mult, ALU.add).then_inc(lat_var, 1)
            dve.tensor_scalar(m.lstat[:, 0, QT:], m.lsum[:, :], 1.0 / KV_LORA, EPS, ALU.mult, ALU.add).then_inc(lat_var, 1)
            for j in (C_Q + 1, C_Q + 3):
                dve.wait_ge(cols_mm, j + 1)
                dve.tensor_scalar(m.qT[:, j - C_Q, :], psum[:, j, :], NSA_SCALE, None, ALU.mult).then_inc(cols_v, 1)
            dve.wait_ge(lat_std, 1)
            dve.reciprocal(m.lstat[:, 2, :], m.lstat[:, 1, :]).then_inc(lat_rs, 1)
            dve.wait_ge(lat_rs, 1)
            for t in range(QT):
                dve.tensor_scalar(lat[:, t, 0:256], m.rows[:, t, R_CQ:R_CKV], m.lstat[:, 2, t:t + 1], None, ALU.mult)
                dve.tensor_scalar(lat[:, t, 256:384], m.rows[:, t, R_CKV:R_VS], m.lstat[:, 2, QT + t:QT + t + 1], None,
                                  ALU.mult).then_inc(lat_ok, 1)
            dve.wait_ge(pair_ok, 128)
            for c in range(2):
                for g in range(GROUPS):
                    raw = pairs[:, c, g, :]
                    raw = bass.AP(tensor=raw.tensor, offset=raw.offset,
                                  ap=[raw.ap[0], [2, LP], [CMP_STRIDE, N_CMP]])
                    dve.tensor_tensor(blk[:, c, :, g, :], raw, posT[:, :].unsqueeze(2).to_broadcast([P, LP, N_CMP]),
                                      ALU.add).then_inc(blk_ok, 1)
            dve.wait_ge(b_mm, 1)
            dve.tensor_copy(brow[:, :].rearrange("h (b n) -> h b n", b=2), psum[0:HEADS, 6:8, :]).then_inc(b_row, 1)
            dve.wait_ge(cmp_mm, 1)
            dve.tensor_copy(m.kcT[0:DH, :], psum[0:DH, 3, 0:N_CMP]).then_inc(cmp_ok, 1)
            dve.tensor_copy(m.kcT[DH:P, :], psum[DH:P, 3, 0:N_CMP]).then_inc(cmp_ok, 1)
            dve.wait_ge(cmp_mm, 2)
            dve.tensor_copy(m.vc[:, :], psum[0:N_CMP, 4, 0:GROUPS * DH]).then_inc(cmp_ok, 1)
            dve.wait_ge(b_rep, 16)

        @block.tensor
        def _(pe):
            pe.wait_ge(eye_ok, 2)
            for t in range(QT):
                pe.wait_ge(xn_ok, t + 1)
                for k in range(KD):
                    mm = pe.transpose(psum[:, k, t * P:(t + 1) * P], xn[:, t, k * P:(k + 1) * P], m.eye[:, :])
            mm.then_inc(xT_ok, 1)
            pe.wait_ge(h_ok, KD)
            pe.wait_ge(wr_in, 16)
            for t in range(QT):
                for b, (lo, hi) in enumerate(((0, S), (S, ROW_W))):
                    for k in range(KD):
                        mm = pe.matmul(psum[:, 2 * t + b, 0:hi - lo], hT[:, k, t * P:(t + 1) * P],
                                       w_rows[:, k, lo:hi], start=(k == 0), stop=(k == KD - 1))
                mm.then_inc(rows_mm, 1)
            for j in range(N_COLS):
                pe.wait_ge(wc_in[j % 2], 16 * (j // 2 + 1))
                pe.wait_ge(rows_a, j // 2 + 1)
                pe.wait_ge(rows_v, j // 2 + 1)
                for k in range(KD):
                    mm = pe.matmul(psum[:, j, :], w_col[:, j % 2, k, :], hT[:, k, :],
                                   start=(k == 0), stop=(k == KD - 1))
                mm.then_inc(cols_mm, 1)
            pe.wait_ge(t5_in, 32)
            pe.wait_ge(neg_ok, 1)
            pe.wait_ge(cols_a, 4)
            pe.wait_ge(cols_v, 4)
            for b in range(2):
                mm = pe.matmul(psum[0:HEADS, 6 + b, :], t5x[:, :], onehot[:, b * S:(b + 1) * S], start=True, stop=True)
            mm.then_inc(b_mm, 1)
            pe.wait_ge(w1_in, 16)
            pe.wait_ge(w1v_in, 16)
            for c in range(2):
                pe.wait_ge(blk_ok, GROUPS * (c + 1))
                for h in range(HT):
                    for l in range(LP):
                        mm = pe.matmul(psum[:, 4 + c, h * GROUPS * N_CMP:(h + 1) * GROUPS * N_CMP],
                                       (w1 if c == 0 else w1v)[:, l, h * P:(h + 1) * P],
                                       blk[:, c, l, :, :].rearrange("p g n -> p (g n)"),
                                       start=(l == 0), stop=(l == LP - 1))
                mm.then_inc(hid_mm, 1)
            pe.wait_ge(lat_ok, QT)
            for c in range(3):
                for t in range(QT):
                    mm = pe.transpose(psum[:, c, t * P:(t + 1) * P], lat[:, t, c * P:(c + 1) * P], m.eye[:, :])
                mm.then_inc(latT_mm, 1)
            pe.wait_ge(w2_in, 16)
            pe.wait_ge(hid_ok, 1)
            for g in range(GROUPS):
                for h in range(HT):
                    mm = pe.matmul(psum[g * DH:(g + 1) * DH, 3, 0:N_CMP], w2[:, 0, h, :],
                                   hid[:, 0, h, g * N_CMP:(g + 1) * N_CMP], start=(h == 0), stop=(h == HT - 1))
            mm.then_inc(cmp_mm, 1)
            pe.wait_ge(hid_ok, 2)
            for g in range(GROUPS):
                for h in range(HT):
                    mm = pe.matmul(psum[0:N_CMP, 4, g * DH:(g + 1) * DH], hid[:, 1, h, g * N_CMP:(g + 1) * N_CMP],
                                   w2[:, 1, h, :], start=(h == 0), stop=(h == HT - 1))
            mm.then_inc(cmp_mm, 1)
            pe.wait_ge(up_in, 64)
            pe.wait_ge(latT_ok, 3)


def latents(nc, io, m, psum):
    with ExitStack() as ctx:
        sb = m.scratch().take

        def sem(name):
            return ctx.enter_context(nc.semaphore(name))

        posf = sb("posf", [P, QT])
        ang = sb("ang", [P, QT, HALF])
        turns = sb("turns", [P, 2, QT * HALF])
        red = sb("red", [P, 2, QT * HALF])
        trig = sb("trig", [P, 2, QT, HALF])
        qf = sb("qf", [P, QT, HEADS, QK])
        kf = sb("kf", [P, QT, HEADS, QK])
        part = sb("part", [P, 4, QT, HEADS, HALF])
        kpart = sb("kpart", [P, 4, QT, HALF])
        krot = sb("krot", [P, QT, ROPE])

        step, red_ok, trig_ok = sem("rope_step"), sem("red_ok"), sem("trig_ok")
        up_mm, upq_ok, upk_ok = sem("up_mm"), sem("upq_ok"), sem("upk_ok")
        q_rot, k_rot, qkT_mm, qkT_a, qkT_v = sem("q_rot"), sem("k_rot"), sem("qkT_mm"), sem("qkT_a"), sem("qkT_v")
        gate_e = sem("gate_e")
        block = ctx.enter_context(nc.Block())

        @block.scalar
        def _(act):
            for t in range(QT):
                act.wait_ge(up_mm, t + 1)
                for b in range(2):
                    act.activation(qf[:, t, 4 * b:4 * b + 4, :].rearrange("p h d -> p (h d)"),
                                   psum[:, 4 * (t % 2) + b, 0:4 * QK], ACT.Copy).then_inc(upq_ok, 1)
            act.activation(m.gate[:, :, :], m.rows[:, :, R_G:ROW_W], ACT.Exp, scale=-1.0).then_inc(gate_e, 1)
            act.wait_ge(red_ok, 1)
            act.activation(trig[:, :, :, :].rearrange("p c t d -> p (c t d)"),
                           red[:, :, :].rearrange("p c n -> p (c n)"), ACT.Sin).then_inc(trig_ok, 1)
            for u in range(0, 2 * HEADS, 2):
                act.wait_ge(qkT_mm, u + 1)
                act.activation(m.qmT[:, u // 2, :], psum[0:QK, u % 8, :], ACT.Copy).then_inc(qkT_a, 1)

        @block.vector
        def _(dve):
            chain = [0]

            def link(ins):
                chain[0] += 1
                ins.then_inc(step, 1)
                dve.wait_ge(step, chain[0])

            link(dve.tensor_copy(posf[:, :], m.pos[:, :]))
            link(dve.tensor_tensor(ang[:, :, :], posf[:, :].unsqueeze(2).to_broadcast([P, QT, HALF]),
                                   m.inv[:, :].unsqueeze(1).to_broadcast([P, QT, HALF]), ALU.mult))
            a = ang[:, :, :].rearrange("p t d -> p (t d)")
            dve.tensor_scalar(turns[:, 0, :], a, 1 / (2 * np.pi), None, ALU.mult).then_inc(step, 1)
            chain[0] += 1
            link(dve.tensor_scalar(turns[:, 1, :], a, 1 / (2 * np.pi), 0.25, ALU.mult, ALU.add))
            link(dve.tensor_scalar(turns[:, :, :], turns[:, :, :], ROUND, None, ALU.add))
            link(dve.tensor_scalar(turns[:, :, :], turns[:, :, :], ROUND, None, ALU.subtract))
            src = ang[:, :, :].rearrange("p t d -> p (t d)").unsqueeze(1).to_broadcast([P, 2, QT * HALF])
            for c in (TWO_PI_HI, TWO_PI_MID, TWO_PI_LO):
                link(dve.scalar_tensor_tensor(out=red[:, :, :], in0=turns[:, :, :], scalar=-c, in1=src,
                                              op0=ALU.mult, op1=ALU.add))
                src = red[:, :, :]
            link(dve.tensor_scalar(red[:, 1, :], red[:, 1, :], float(np.pi / 2), None, ALU.add))
            dve.tensor_scalar(red[:, :, :], red[:, :, :], PI_IN, -PI_IN, ALU.min, ALU.max).then_inc(red_ok, 1)
            for t in range(QT):
                dve.wait_ge(up_mm, t + 1)
                dve.tensor_copy(kf[:, t, :, 0:NOPE], psum[:, 4 * (t % 2) + 2, :].rearrange("p (h d) -> p h d", h=HEADS)
                                ).then_inc(upk_ok, 1)
                dve.tensor_copy(m.vm[:, t, :], psum[:, 4 * (t % 2) + 3, :]).then_inc(upk_ok, 1)
            dve.wait_ge(gate_e, 1)
            link(dve.tensor_scalar(m.gate[:, :, :], m.gate[:, :, :], 1.0, None, ALU.add))
            dve.reciprocal(m.gate[:, :, :], m.gate[:, :, :])
            dve.wait_ge(trig_ok, 1)
            k1, k2 = m.rows[:, :, R_KR:R_KR + HALF], m.rows[:, :, R_KR + HALF:R_G]
            sin, cos = trig[:, 0], trig[:, 1]
            for n, (xx, tt) in enumerate(((k1, cos), (k2, sin), (k1, sin), (k2, cos))):
                dve.tensor_tensor(kpart[:, n], xx, tt, ALU.mult).then_inc(step, 1)
                chain[0] += 1
            dve.wait_ge(step, chain[0])
            dve.tensor_tensor(krot[:, :, 0:HALF], kpart[:, 0], kpart[:, 1], ALU.subtract)
            link(dve.tensor_tensor(krot[:, :, HALF:ROPE], kpart[:, 2], kpart[:, 3], ALU.add))
            for t in range(QT):
                dve.tensor_copy(kf[:, t, :, NOPE:QK], krot[:, t, :].unsqueeze(1).to_broadcast([P, HEADS, ROPE])
                                ).then_inc(k_rot, 1)
            dve.wait_ge(upq_ok, 2 * QT)
            for t in range(QT):
                q1, q2 = qf[:, t, :, NOPE:NOPE + HALF], qf[:, t, :, NOPE + HALF:QK]
                sin_t = trig[:, 0, t, :].unsqueeze(1).to_broadcast([P, HEADS, HALF])
                cos_t = trig[:, 1, t, :].unsqueeze(1).to_broadcast([P, HEADS, HALF])
                for n, (xx, tt) in enumerate(((q1, cos_t), (q2, sin_t), (q1, sin_t), (q2, cos_t))):
                    dve.tensor_tensor(part[:, n, t], xx, tt, ALU.mult).then_inc(step, 1)
                    chain[0] += 1
            dve.wait_ge(step, chain[0])
            for t in range(QT):
                dve.tensor_tensor(qf[:, t, :, NOPE:NOPE + HALF], part[:, 0, t], part[:, 1, t], ALU.subtract
                                  ).then_inc(q_rot, 1)
                dve.tensor_tensor(qf[:, t, :, NOPE + HALF:QK], part[:, 2, t], part[:, 3, t], ALU.add).then_inc(q_rot, 1)
            for u in range(1, 2 * HEADS, 2):
                dve.wait_ge(qkT_mm, u + 1)
                dve.tensor_copy(m.kmT[:, u // 2, :], psum[0:QK, u % 8, :]).then_inc(qkT_v, 1)

        @block.tensor
        def _(pe):
            for t in range(QT):
                if t >= 2:
                    pe.wait_ge(upq_ok, 2 * (t - 1))
                    pe.wait_ge(upk_ok, 2 * (t - 1))
                for b in range(2):
                    for c in range(2):
                        pe.matmul(psum[:, 4 * (t % 2) + b, 0:4 * QK], m.latT[:, c, t * P:(t + 1) * P],
                                  m.wq_up[:, c, b * 4 * QK:(b + 1) * 4 * QK], start=(c == 0), stop=(c == 1))
                for b in range(2):
                    mm = pe.matmul(psum[:, 4 * (t % 2) + 2 + b, :], m.latT[:, 2, t * P:(t + 1) * P],
                                   m.wkv_up[:, b * 512:(b + 1) * 512], start=True, stop=True)
                mm.then_inc(up_mm, 1)
            pe.wait_ge(upq_ok, 2 * QT)
            pe.wait_ge(upk_ok, 2 * QT)
            pe.wait_ge(k_rot, QT)
            pe.wait_ge(q_rot, 2 * QT)
            for u in range(2 * HEADS):
                if u >= 8:
                    pe.wait_ge(qkT_a if u % 2 == 0 else qkT_v, (u - 8) // 2 + 1)
                for t in range(QT):
                    mm = pe.transpose(psum[0:QK, u % 8, t * P:(t + 1) * P], (qf if u % 2 == 0 else kf)[:, t, u // 2, :],
                                      m.eye[:, :])
                mm.then_inc(qkT_mm, 1)


def attend(nc, io, m, psum):
    kinds = [(0, g) for g in range(GROUPS)]
    kinds += [(b, h) for h in range(HEADS) for b in (1, 2)]
    kinds += [(3, h) for h in range(HEADS)]
    pairs = [(i, QT - 1 - i) for i in range(QT // 2)]
    units = [(i, b, h) for pair in pairs for b, h in kinds for i in pair]
    n_units = len(units)
    RING = 4
    outs = [(i, c) for pair in pairs for c in range(2) for i in pair]
    finish = [max(u for u, (ui, b, _) in enumerate(units) if ui == i and (b == 3) == (c == 1)) for i, c in outs]
    with ExitStack() as ctx:
        sb = m.scratch().take

        def sem(name):
            return ctx.enter_context(nc.semaphore(name))

        sc = sb("sc", [P, RING, S])
        pr = sb("pr", [P, RING, S])
        prT = sb("prT", [P, RING, S])
        cprT = sb("cprT", [N_CMP, 2, GROUPS, S])
        top = sb("top", [P, n_units, 4])
        sums = sb("sums", [P, n_units, 4])
        fac = sb("fac", [P, n_units, 4])
        scale = sb("scale", [P, RING, P])
        og = sb("og", [P, 2, S])
        sq = sb("sq", [P, 2, S])
        sq2 = sb("sq2", [P, S // 2])

        s_mm, s_in, e_ok, c_step, d_ok = sem("s_mm"), sem("s_in"), sem("e_ok"), sem("c_step"), sem("d_ok")
        t_mm, t_v, t_a, v_mm = sem("t_mm"), sem("t_v"), sem("t_a"), sem("v_mm")
        og_ok, sq_ok, half_ok, ssq_ok, ohi_ok, olo_ok = (
            sem("og_ok"), sem("sq_ok"), sem("half_ok"), sem("ssq_ok"), sem("ohi_ok"), sem("olo_ok"))
        seen_ok = sem("seen_ok")
        block = ctx.enter_context(nc.Block())
        S_BANK, T_BANK, O_BANK = 0, 3, 5
        S_N, T_N, O_N = 3, 2, 3
        FACTOR, TURN, VALUES, DRAIN = 1, 2, 4, 5

        def valued(u):
            return sum(b != 0 for _, b, _ in units[:u + 1])

        def by_vector(u):
            return u % 4 in (0, 3)

        def copied(eng, u):
            n = sum(by_vector(v) == by_vector(u) for v in range(u + 1))
            eng.wait_ge(t_v if by_vector(u) else t_a, n)

        def copy_out(eng, u):
            i, b, g = units[u]
            eng.wait_ge(t_mm, u + 1)
            if b == 0:
                rows, w, dst = N_CMP, S, cprT[:, u % 2, g, :]
                if u >= n_units // 2:
                    eng.wait_ge(v_mm, valued(finish[1]))
            else:
                rows, w = P, (i + 1) * P
                dst = prT[:, u % RING, 0:w]
                if u >= RING and units[u - RING][1]:
                    eng.wait_ge(v_mm, valued(u - RING))
            src = psum[0:rows, T_BANK + u % T_N, 0:w]
            if by_vector(u):
                nc.vector.tensor_copy(dst, src).then_inc(t_v, 1)
            else:
                nc.scalar.activation(dst, src, ACT.Copy).then_inc(t_a, 1)

        @block.sync
        def _(sp):
            sp.dma_start(m.gain[:, 0, :], io.grp_gain).then_inc(m.gain_in, 16)
            sp.dma_start(m.gain[:, 1, :], io.g2).then_inc(m.gain_in, 16)
            for k in range(2):
                sp.dma_start(m.wo_raw[:, k, :], io.w_out[:, k, :]).then_inc(m.wo_in[k], 16)

        @block.tensor
        def _(pe):
            def scores(u):
                i, b, h = units[u]
                if u >= S_N:
                    pe.wait_ge(s_in, u - S_N + 1)
                bank, q = psum[:, S_BANK + u % S_N, :], slice(i * P, (i + 1) * P)
                if b == 0:
                    r = slice(h * DH, (h + 1) * DH)
                    for n in range(4):
                        mm = pe.matmul(bank[:, n * N_CMP:(n + 1) * N_CMP], m.qT[r, n, q], m.kcT[r, :],
                                       start=True, stop=True)
                elif b < 3:
                    r = slice(h // 4 * DH, (h // 4 + 1) * DH)
                    mm = pe.matmul(bank[:, 0:(i + 1) * P], m.qT[r, h % 4, q], m.kT[r, b - 1, 0:(i + 1) * P],
                                   start=True, stop=True)
                else:
                    mm = pe.matmul(bank[:, 0:(i + 1) * P], m.qmT[:, h, q], m.kmT[:, h, 0:(i + 1) * P],
                                   start=True, stop=True)
                mm.then_inc(s_mm, 1)

            def turn(u):
                i, b, _ = units[u]
                pe.wait_ge(d_ok, u + 1)
                if u >= T_N:
                    copied(pe, u - T_N)
                for n in range(4 if b == 0 else i + 1):
                    if b == 0:
                        mm = pe.transpose(psum[0:N_CMP, T_BANK + u % T_N, n * P:(n + 1) * P],
                                          pr[:, u % RING, n * N_CMP:(n + 1) * N_CMP], m.eye[:, :])
                    else:
                        mm = pe.matmul(psum[:, T_BANK + u % T_N, n * P:(n + 1) * P],
                                       pr[:, u % RING, n * P:(n + 1) * P], scale[:, u % RING, :], start=True, stop=True)
                mm.then_inc(t_mm, 1)

            def values(u):
                i, b, h = units[u]
                copied(pe, u)
                if b == 0:
                    return
                o = outs.index((i, int(b == 3)))
                if o >= O_N:
                    pe.wait_ge(og_ok, o - O_N + 1)
                    pe.wait_ge(sq_ok, o - O_N + 1)
                out = psum[h % 2 * DH:(h % 2 + 1) * DH, O_BANK + o % O_N, h // 2 * P:(h // 2 + 1) * P]
                if b == 1:
                    g = h // 4
                    pe.matmul(out, m.vc[:, g * DH:(g + 1) * DH], cprT[:, u % 2, g, h % 4 * P:(h % 4 + 1) * P],
                              start=True, stop=False)
                for n in range(i + 1):
                    if b < 3:
                        lo = (R_VS, R_VW)[b - 1] + h // 4 * DH
                        v = m.rows[:, n, lo:lo + DH]
                    else:
                        v = m.vm[:, n, h * DH:(h + 1) * DH]
                    mm = pe.matmul(out, v, prT[:, u % RING, n * P:(n + 1) * P],
                                   start=(b == 3 and n == 0), stop=(b != 1 and n == i))
                mm.then_inc(v_mm, 1)

            for s in range(n_units + VALUES):
                if s < n_units:
                    scores(s)
                if TURN <= s < n_units + TURN:
                    turn(s - TURN)
                if s >= VALUES:
                    values(s - VALUES)

        @block.scalar
        def _(act):
            for s in range(n_units + DRAIN + 1):
                if s < n_units:
                    i, b, h = units[s]
                    act.wait_ge(s_in, s + 1)
                    if s >= RING:
                        act.wait_ge(t_mm, s - RING + 1)
                    if b == 0:
                        act.activation(pr[:, s % RING, 0:4 * N_CMP], sc[:, s % RING, 0:4 * N_CMP], ACT.Exp).then_inc(e_ok, 1)
                    else:
                        w = (i + 1) * P
                        act.activation(pr[:, s % RING, 0:w], sc[:, s % RING, 0:w], ACT.Exp, bias=top[:, s, 0:1], scale=-1.0,
                                       accum_out=sums[:, s, 0:1]).then_inc(e_ok, 1)
                if TURN <= s < n_units + TURN and not by_vector(s - TURN):
                    copy_out(act, s - TURN)
                if s > DRAIN and s - DRAIN - 1 in finish:
                    o = finish.index(s - DRAIN - 1)
                    i, c = outs[o]
                    act.wait_ge(og_ok, o + 1)
                    if o >= 2:
                        act.wait_ge(half_ok, o - 1)
                    act.activation(sq[:, o % 2, :], psum[:, O_BANK + o % O_N, :], ACT.Square).then_inc(sq_ok, 1)
                    act.activation(m.o_hi[:, 4 * c:4 * c + 4, i * P:(i + 1) * P],
                                   og[:, o % 2, :].rearrange("p (k n) -> p k n", k=4), ACT.Copy).then_inc(ohi_ok, 1)

        @block.gpsimd
        def _(pool):
            for o, (i, c) in enumerate(outs):
                pool.wait_ge(sq_ok, o + 1)
                if o:
                    pool.wait_ge(ssq_ok, o)
                pool.tensor_tensor(sq2[:, :], sq[:, o % 2, 0:S // 2], sq[:, o % 2, S // 2:S], ALU.add).then_inc(half_ok, 1)
                pool.wait_ge(half_ok, o + 1)
                pool.tensor_tensor(m.ssq[:, c, i * P:(i + 1) * P], sq2[:, 0:P], sq2[:, P:2 * P], ALU.add).then_inc(ssq_ok, 1)
                pool.wait_ge(ohi_ok, o + 1)
                pool.tensor_tensor(m.o_lo[:, 4 * c:4 * c + 4, i * P:(i + 1) * P],
                                   og[:, o % 2, :].rearrange("p (k n) -> p k n", k=4),
                                   m.o_hi[:, 4 * c:4 * c + 4, i * P:(i + 1) * P].bitcast(F32), ALU.subtract
                                   ).then_inc(olo_ok, 1)

        @block.vector
        def _(dve):
            chain = [0]

            def link(ins):
                chain[0] += 1
                ins.then_inc(c_step, 1)
                dve.wait_ge(c_step, chain[0])

            def factor(u):
                i, b, h = units[u]
                dve.wait_ge(e_ok, u + 1)
                gate = m.gate[:, i, :].rearrange("p (h b) -> p b h", b=3)
                if b == 0:
                    p = pr[:, u % RING, 0:4 * N_CMP].rearrange("p (h n) -> p h n", h=4)
                    link(dve.tensor_reduce(sums[:, u, :], p, X, ALU.add))
                    link(dve.reciprocal(fac[:, u, :], sums[:, u, :]))
                    link(dve.tensor_tensor(fac[:, u, :], fac[:, u, :], gate[:, 0, 4 * h:4 * h + 4], ALU.mult))
                    dve.tensor_tensor(p, p, fac[:, u, :].unsqueeze(2).to_broadcast([P, 4, N_CMP]), ALU.mult
                                      ).then_inc(d_ok, 1)
                    return
                link(dve.reciprocal(fac[:, u, 0:1], sums[:, u, 0:1]))
                if u >= RING:
                    dve.wait_ge(t_mm, u - RING + 1)
                dve.tensor_scalar(scale[:, u % RING, :], m.eye[:, :], fac[:, u, 0:1],
                                  gate[:, b, h:h + 1] if b < 3 else None, ALU.mult, *([ALU.mult] if b < 3 else [])
                                  ).then_inc(d_ok, 1)

            gate0 = m.gate[:, 0, :].rearrange("p (h b) -> p b h", b=3)[:, 0, :]
            dve.tensor_scalar(gate0, gate0, m.seen[:, 0:1], None, ALU.mult).then_inc(seen_ok, 1)
            dve.wait_ge(seen_ok, 1)
            for s in range(n_units + DRAIN + 1):
                if s < n_units:
                    i, b, h = units[s]
                    dve.wait_ge(s_mm, s + 1)
                    if s >= RING:
                        dve.wait_ge(e_ok, s - RING + 1)
                    bank, w = psum[:, S_BANK + s % S_N, :], (i + 1) * P
                    j0 = S - w
                    if b == 0:
                        out = sc[:, s % RING, 0:4 * N_CMP].rearrange("p (h n) -> p h n", h=4)
                        c0 = S - P + CMP_LEN - 1 - i * P
                        bias = m.bias[:, 4 * h:4 * h + 4, c0:c0 + (N_CMP - 1) * CMP_STRIDE + 1:CMP_STRIDE]
                        link(dve.tensor_tensor(out, bank[:, 0:4 * N_CMP].rearrange("p (h n) -> p h n", h=4), bias,
                                               ALU.add))
                        link(dve.tensor_reduce(top[:, s, :], out, X, ALU.max))
                        dve.tensor_tensor(out, out, top[:, s, :].unsqueeze(2).to_broadcast([P, 4, N_CMP]),
                                          ALU.subtract).then_inc(s_in, 1)
                    elif b < 3:
                        dve.tensor_tensor_reduce(sc[:, s % RING, 0:w], bank[:, 0:w], m.bias[:, h, j0:S], -1.0, 3.0e38,
                                                 ALU.add, ALU.min, top[:, s, 0:1]).then_inc(s_in, 1)
                    else:
                        dve.tensor_tensor_reduce(sc[:, s % RING, 0:w], bank[:, 0:w], m.mask[:, j0:S], -MLA_SCALE, 3.0e38,
                                                 ALU.add, ALU.min, top[:, s, 0:1]).then_inc(s_in, 1)
                if FACTOR <= s < n_units + FACTOR:
                    factor(s - FACTOR)
                if TURN <= s < n_units + TURN and by_vector(s - TURN):
                    copy_out(dve, s - TURN)
                if s >= DRAIN and s - DRAIN in finish:
                    o = finish.index(s - DRAIN)
                    i, c = outs[o]
                    dve.wait_ge(v_mm, valued(s - DRAIN))
                    if o == 0:
                        dve.wait_ge(m.gain_in, 32)
                    if o >= 2:
                        dve.wait_ge(olo_ok, o - 1)
                    dve.tensor_tensor(og[:, o % 2, :].rearrange("p (k n) -> p k n", k=4),
                                      psum[:, O_BANK + o % O_N, :].rearrange("p (k n) -> p k n", k=4),
                                      m.gain[:, 0, 4 * c:4 * c + 4].unsqueeze(2).to_broadcast([P, 4, P]), ALU.mult
                                      ).then_inc(og_ok, 1)


def output(nc, io, m, psum):
    with ExitStack() as ctx:
        sb = m.scratch().take

        def sem(name):
            return ctx.enter_context(nc.semaphore(name))

        w_hi = sb("wo_hi", [P, KD, D], F32R)
        w_lo = sb("wo_lo", [P, KD, D], F32R)
        ones = sb("ones", [P, 1])
        stat = sb("ostat", [P, 4, 2 * QT])
        stat2 = sb("ostat2", [P, 4, QT])
        scale = sb("oscale", [P, QT, P])
        junk = sb("ojunk", [P, D])

        wh_ok, wl_ok = sem("wh_ok"), sem("wl_ok")
        ones_ok, g_mm, g_var, g_std, g_rs = sem("o_ones"), sem("g_mm"), sem("g_var"), sem("g_std"), sem("g_rs")
        y_mm, y_ok, x2_out = sem("y_mm"), sem("y_ok"), sem("x2_out")
        y_sq, y_var, y_std, y_rs, y_dg, yT_mm, hi_ok, lo_ok = (
            sem("y_sq"), sem("y_var"), sem("y_std"), sem("y_rs"), sem("y_dg"), sem("yT_mm"), sem("hi_ok"), sem("lo_ok"))
        block = ctx.enter_context(nc.Block())
        banks = [(t, b) for t in range(QT) for b in range(2)]

        @block.sync
        def _(sp):
            for k in range(2, KD):
                sp.wait_ge(wl_ok, k - 1)
                sp.dma_start(m.wo_raw[:, k % 2, :], io.w_out[:, k, :]).then_inc(m.wo_in[k % 2], 16)
            for c in range(2):
                sp.dma_start(m.wq_raw[:, c], io.wq[c]).then_inc(m.wq_in[c], 16)
            sp.dma_start(m.keys[:, :, :], io.keysT).then_inc(m.keys_in, 16)
            for t in range(QT):
                sp.wait_ge(y_ok, 2 * QT + 2 * t + 2)
                sp.dma_start(io.x2.rearrange("(t p) d -> t p d", p=P)[t], m.x[:, t, :]).then_inc(x2_out, 16)
            sp.wait_ge(x2_out, 16 * QT)

        @block.gpsimd
        def _(pool):
            pool.memset(ones[:, :], 1.0).then_inc(ones_ok, 1)

        @block.scalar
        def _(act):
            def split(k):
                act.wait_ge(m.wo_in[k % 2], 16 * (k // 2 + 1))
                act.activation(w_hi[:, k, :], m.wo_raw[:, k % 2, :], ACT.Copy).then_inc(wh_ok, 1)

            split(0)
            split(1)
            act.wait_ge(g_var, 1)
            act.activation(stat[:, 2, :], stat[:, 1, :], ACT.Sqrt).then_inc(g_std, 1)
            for k in range(2, KD):
                split(k)
            for t in range(QT):
                act.wait_ge(y_ok, 2 * QT + 2 * t + 2)
                if t:
                    act.wait_ge(y_sq, t)
                act.activation(junk[:, :], m.x[:, t, :], ACT.Square, accum_out=stat2[:, 0, t:t + 1]).then_inc(y_sq, 1)
                act.wait_ge(y_var, t + 1)
                act.activation(stat2[:, 2, t:t + 1], stat2[:, 1, t:t + 1], ACT.Sqrt).then_inc(y_std, 1)
            for k in range(KD):
                act.wait_ge(yT_mm, k + 1)
                act.activation(m.h_hi[:, k, :], psum[:, k, :], ACT.Copy, scale=m.gain[:, 1, k:k + 1]).then_inc(hi_ok, 1)

        @block.vector
        def _(dve):
            def split(k):
                dve.wait_ge(wh_ok, k + 1)
                dve.tensor_tensor(w_lo[:, k, :], m.wo_raw[:, k % 2, :], w_hi[:, k, :].bitcast(F32), ALU.subtract
                                  ).then_inc(wl_ok, 1)

            split(0)
            dve.wait_ge(g_mm, 1)
            dve.tensor_scalar(stat[:, 1, :], psum[:, 7, 0:2 * QT], 1.0 / NSA_W, EPS, ALU.mult, ALU.add).then_inc(g_var, 1)
            split(1)
            dve.wait_ge(g_std, 1)
            dve.reciprocal(stat[:, 3, :], stat[:, 2, :]).then_inc(g_rs, 1)
            for k in range(2, KD):
                split(k)
            dve.wait_ge(g_rs, 1)
            for c in range(2):
                for j, (t, b) in enumerate(banks):
                    dve.wait_ge(y_mm, 2 * QT * c + j + 1)
                    if c:
                        dve.wait_ge(y_ok, j + 1)
                    xs = m.x[:, t, b * S:(b + 1) * S]
                    dve.scalar_tensor_tensor(out=xs, in0=psum[:, j, :], scalar=stat[:, 3, 2 * t + c:2 * t + c + 1],
                                             in1=xs, op0=ALU.mult, op1=ALU.add).then_inc(y_ok, 1)
                    if c and b:
                        dve.wait_ge(y_sq, t + 1)
                        dve.tensor_scalar(stat2[:, 1, t:t + 1], stat2[:, 0, t:t + 1], 1.0 / D, EPS, ALU.mult, ALU.add
                                          ).then_inc(y_var, 1)
                        dve.wait_ge(y_std, t + 1)
                        dve.reciprocal(stat2[:, 3, t:t + 1], stat2[:, 2, t:t + 1]).then_inc(y_rs, 1)
                        dve.wait_ge(y_rs, t + 1)
                        dve.tensor_scalar(scale[:, t, :], m.eye[:, :], stat2[:, 3, t:t + 1], None, ALU.mult
                                          ).then_inc(y_dg, 1)
            for k in range(KD):
                dve.wait_ge(hi_ok, k + 1)
                dve.scalar_tensor_tensor(out=m.h_lo[:, k, :], in0=psum[:, k, :], scalar=m.gain[:, 1, k:k + 1],
                                         in1=m.h_hi[:, k, :].bitcast(F32), op0=ALU.mult, op1=ALU.subtract
                                         ).then_inc(lo_ok, 1)

        @block.tensor
        def _(pe):
            def product(j, k, start, stop):
                t, b = banks[j]
                ts, bs = slice(t * P, (t + 1) * P), slice(b * S, (b + 1) * S)
                for n, (o, w) in enumerate(((m.o_hi, w_hi), (m.o_hi, w_lo), (m.o_lo, w_hi))):
                    mm = pe.matmul(psum[:, j, :], o[:, k, ts], w[:, k, bs],
                                   start=(start and n == 0), stop=(stop and n == 2), skip_group_check=True)
                return mm

            pe.wait_ge(ones_ok, 1)
            for t in range(QT):
                for c in range(2):
                    mm = pe.matmul(psum[:, 7, 2 * t + c:2 * t + c + 1], m.ssq[:, c, t * P:(t + 1) * P], ones[:, :],
                                   start=True, stop=True)
            mm.then_inc(g_mm, 1)
            for k in range(4):
                pe.wait_ge(wl_ok, k + 1)
                for j in range(len(banks)):
                    if k == 0 and j == 7:
                        pe.wait_ge(g_var, 1)
                    mm = product(j, k, k == 0, k == 3)
                    if k == 3:
                        mm.then_inc(y_mm, 1)
            pe.wait_ge(wl_ok, KD)
            for j in range(len(banks)):
                pe.wait_ge(y_ok, j + 1)
                for k in range(4, KD):
                    mm = product(j, k, k == 4, k == KD - 1)
                mm.then_inc(y_mm, 1)
            pe.wait_ge(y_ok, 4 * QT)
            for t in range(QT):
                pe.wait_ge(y_dg, t + 1)
                for k in range(KD):
                    mm = pe.matmul(psum[:, k, t * P:(t + 1) * P], m.x[:, t, k * P:(k + 1) * P], scale[:, t, :],
                                   start=True, stop=True)
                    if t == QT - 1:
                        mm.then_inc(yT_mm, 1)


def product3(pe, bank, w_hi, w_lo, x_hi, x_lo):
    n = 3 * KD
    i = 0
    for k in range(KD):
        for w, x in ((w_hi, x_hi), (w_hi, x_lo), (w_lo, x_hi)):
            mm = pe.matmul(bank, w[:, k, :], x[:, k, :], start=(i == 0), stop=(i == n - 1))
            i += 1
    return mm


def peer_scores(nc, io, m, psum):
    with ExitStack() as ctx:
        sb = m.scratch().take

        def sem(name):
            return ctx.enter_context(nc.semaphore(name))

        raw, keys = m.wq_raw, m.keys
        hi = sb("wq_hi", [P, 2, KD, P], F32R)
        lo = sb("wq_lo", [P, 2, KD, P], F32R)
        qp = sb("qp", [P, 2, S])
        keys_in, raw_in = m.keys_in, m.wq_in
        hi_ok, lo_ok, q_mm, q_ok, s_mm, s_ok = (
            sem("wqhi_ok"), sem("wqlo_ok"), sem("pq_mm"), sem("pq_ok"), sem("ps_mm"), sem("ps_ok"))
        block = ctx.enter_context(nc.Block())
        rounds = PH

        @block.sync
        def _(sp):
            for c in range(2):
                sp.dma_start(m.u_raw[:, c], io.uT[c]).then_inc(m.u_in[c], 16)
            with sp.Fori(1, rounds) as h:
                for c in range(2):
                    sp.wait_ge(lo_ok, 2 * h - 1 + c)
                    sp.dma_start(raw[:, c], io.wq[bass.ds(2 * h + c, 1)].rearrange("o p k n -> p (o k) n")
                                 ).then_inc(raw_in[c], 16)

        @block.scalar
        def _(act):
            def split(h, c):
                act.wait_ge(raw_in[c], 16 * h + 16)
                act.activation(hi[:, c].rearrange("p k n -> p (k n)"), raw[:, c].rearrange("p k n -> p (k n)"),
                               ACT.Copy).then_inc(hi_ok, 1)

            split(0, 0)
            split(0, 1)

            def queries(h, c):
                act.wait_ge(q_mm, 2 * h + 1 + c)
                act.activation(qp[:, c, :], psum[:, c, :], ACT.Copy).then_inc(q_ok, 1)

            with act.Fori(1, rounds) as h:
                for c in range(2):
                    queries(h - 1, c)
                    split(h, c)
            for c in range(2):
                queries(rounds - 1, c)

        @block.vector
        def _(dve):
            def split(h, c):
                dve.wait_ge(hi_ok, 2 * h + 1 + c)
                dve.tensor_tensor(lo[:, c].rearrange("p k n -> p (k n)"), raw[:, c].rearrange("p k n -> p (k n)"),
                                  hi[:, c].rearrange("p k n -> p (k n)").bitcast(F32), ALU.subtract).then_inc(lo_ok, 1)

            def scores(h, c):
                dve.wait_ge(s_mm, 2 * h + 1 + c)
                for t in range(QT):
                    ins = dve.tensor_copy(m.ps[:, bass.ds(t * 2 * PH + 2 * h + c, 1), :].rearrange("p a n -> p (a n)"),
                                          psum[:, 2 + c, t * P:(t + 1) * P])
                ins.then_inc(s_ok, 1)

            split(0, 0)
            split(0, 1)
            with dve.Fori(1, rounds) as h:
                for c in range(2):
                    split(h, c)
                for c in range(2):
                    scores(h - 1, c)
            for c in range(2):
                scores(rounds - 1, c)

        @block.tensor
        def _(pe):
            def turn(h, first):
                for c in range(2):
                    pe.wait_ge(lo_ok, 2 * h + 1 + c)
                    if not first:
                        pe.wait_ge(q_ok, 2 * h - 1 + c)
                    product3(pe, psum[:, c, :], hi[:, c], lo[:, c], m.h_hi, m.h_lo).then_inc(q_mm, 1)
                for c in range(2):
                    pe.wait_ge(q_ok, 2 * h + 1 + c)
                    if not first:
                        pe.wait_ge(s_ok, 2 * h - 1 + c)
                    for t in range(QT):
                        mm = pe.matmul(psum[:, 2 + c, t * P:(t + 1) * P], qp[:, c, t * P:(t + 1) * P], keys[:, c, :],
                                       start=True, stop=True)
                    mm.then_inc(s_mm, 1)

            pe.wait_ge(keys_in, 16)
            turn(0, True)
            with pe.Fori(1, rounds) as h:
                turn(h, False)


N_TILES = NKEYS
ROUNDS = N_TILES // 2
R_ROUNDS = QT * PH
TOK = S // (ROUNDS - R_ROUNDS)
QUAD = 4
CHUNK = P
C_ROUNDS = CHUNK // TOK
STORED = S - CHUNK


def experts(nc, io, m, psum):
    with ExitStack() as ctx:
        sb = m.scratch().take

        def sem(name):
            return ctx.enter_context(nc.semaphore(name))

        raw = m.u_raw
        hi = sb("u_hi", [P, 2, KD, P], F32R)
        lo = sb("u_lo", [P, 2, KD, P], F32R)
        act_out = sb("act_out", [P, 2, S])
        routed = m.routed
        raw_in = m.u_in
        hi_ok, a_mm, a_ok = sem("uhi_ok"), sem("a_mm"), sem("a_ok")
        lo_ok = [sem("ulo_ok0"), sem("ulo_ok1")]
        a_out, w_out = m.a_out, m.w_out
        r_step, routed_ok, g_exp, g_norm, slot_mm, slot_ok = (
            sem("r_step"), sem("routed_ok"), sem("g_exp"), sem("g_norm"), sem("slot_mm"), sem("slot_ok"))
        hot_ok, is1_ok, w_mm, w_ok = sem("hot_ok"), sem("is1_ok"), sem("w_mm"), sem("w_ok")
        iota_ok, w_ahead = sem("iota_ok"), sem("w_ahead")
        block = ctx.enter_context(nc.Block())

        def load(sp, r, c):
            sp.wait_ge(lo_ok[c], r)
            sp.dma_start(raw[:, c], io.uT[bass.ds(2 * r + c, 1)].rearrange("o p k n -> p (o k) n")
                         ).then_inc(raw_in[c], 16)

        def store(sp, r, c):
            sp.wait_ge(a_ok, 2 * r + 1 + c)
            sp.dma_start(io.acts[bass.ds(2 * r + c, 1)].rearrange("o p n -> p (o n)"), act_out[:, c, :]
                         ).then_inc(a_out[c], 16)

        def split(eng, r, c):
            eng.wait_ge(hi_ok, 2 * r + 1 + c)
            eng.tensor_tensor(lo[:, c].rearrange("p k n -> p (k n)"), raw[:, c].rearrange("p k n -> p (k n)"),
                              hi[:, c].rearrange("p k n -> p (k n)").bitcast(F32), ALU.subtract).then_inc(lo_ok[c], 1)

        @block.sync
        def _(sp):
            def turn(r, last=False):
                if not last:
                    for c in range(2):
                        load(sp, r + 1, c)
                for c in range(2):
                    store(sp, r, c)

            slice_keys = NKEYS // C_ROUNDS

            def store_gates(ch, k, signal):
                cols = slice(ch * CHUNK, (ch + 1) * CHUNK)
                sp.dma_start(io.gates[bass.ds(k, slice_keys), :, cols].rearrange("a b t -> b a t"),
                             m.dense[:, ch % 2, bass.ds(k, slice_keys), :]).then_inc(signal, 16)

            with sp.Fori(0, R_ROUNDS) as r:
                turn(r)
            for ch in range(QT):
                first = R_ROUNDS + ch * C_ROUNDS
                start = first
                if ch:
                    sp.wait_ge(w_ok, ch * CHUNK // QUAD)
                if ch == QT - 1:
                    for k in range(2):
                        turn(first + k)
                        store_gates(ch - 1, k * slice_keys, w_ahead)
                    turn(first + 2)
                    store_gates(ch - 1, 2 * slice_keys, w_out[(ch - 1) % 2])
                    sp.wait_ge(w_ahead, 32)
                    for c in range(2):
                        sp.dma_start(m.v_raw[:, c, :], io.v[c]).then_inc(m.v_in[c], 16)
                    start = first + 3
                with sp.Fori(start, first + C_ROUNDS - (ch == QT - 1)) as r:
                    turn(r)
                    if ch:
                        store_gates(ch - 1, (r - first) * slice_keys, w_out[(ch - 1) % 2])
            turn(ROUNDS - 1, last=True)
            store_gates(QT - 2, NKEYS - slice_keys, w_out[(QT - 2) % 2])

        @block.gpsimd
        def _(pool):
            pool.iota(m.iota[:, :], pattern=[[1, P]], base=0, channel_multiplier=0,
                      allow_small_or_imprecise_dtypes=True).then_inc(iota_ok, 1)
            pool.iota(m.iota4[:, :, :], pattern=[[1, P], [0, QUAD]], base=0, channel_multiplier=0,
                      allow_small_or_imprecise_dtypes=True).then_inc(iota_ok, 1)
            ahead = ROUNDS - C_ROUNDS // 2
            with pool.Fori(0, ahead) as r:
                split(pool, r, 1)
            pool.wait_ge(w_ahead, 32)
            pool.wait_ge(w_out[1], 16 * C_ROUNDS)
            for c in range(2):
                pool.wait_ge(a_out[c], 16)
                pool.dma_start(m.acts_in[:, c, :], io.acts[c]).then_inc(m.ag_in[c], 16)
                pool.dma_start(m.gates_in[:, c, :], io.gates[c, :, 0:STORED]).then_inc(m.ag_in[c], 16)
            with pool.Fori(ahead, ROUNDS) as r:
                split(pool, r, 1)

        @block.scalar
        def _(act):
            def split(r, c):
                act.wait_ge(raw_in[c], 16 * r + 16)
                act.activation(hi[:, c].rearrange("p k n -> p (k n)"), raw[:, c].rearrange("p k n -> p (k n)"),
                               ACT.Copy).then_inc(hi_ok, 1)

            def gelu(r, c, first=False):
                act.wait_ge(a_mm, 2 * r + 1 + c)
                if not first:
                    act.wait_ge(a_out[c], 16 * r)
                act.activation(act_out[:, c, :], psum[:, c, :], ACT.Gelu).then_inc(a_ok, 1)

            split(0, 0)
            split(0, 1)
            for c in range(2):
                gelu(0, c, True)
                split(1, c)
            with act.Fori(1, R_ROUNDS) as r:
                for c in range(2):
                    gelu(r, c)
                    split(r + 1, c)
            act.wait_ge(routed_ok, R_ROUNDS)
            act.activation(routed[:, 2], routed[:, 2], ACT.Exp).then_inc(g_exp, 1)

            def turn(r, r0, ch, last=False, between=False):
                if between:
                    for c in range(2):
                        gelu(r, c)
                        split(r + 1, c)
                for c in range(2):
                    if not between:
                        gelu(r, c)
                        if not last:
                            split(r + 1, c)
                    for b in range(2):
                        n = 2 * c + b
                        q = (r - R_ROUNDS) * (TOK // QUAD) + n
                        act.wait_ge(w_mm, q + 1)
                        off = (r - r0) * TOK + n * QUAD
                        act.activation(m.dense[:, ch % 2, :, bass.ds(off, QUAD)].rearrange("p a t -> p t a"),
                                       psum[:, 2 + n % 2, :].rearrange("p (t a) -> p t a", t=QUAD),
                                       ACT.Copy).then_inc(w_ok, 1)

            for ch in range(QT):
                r0 = R_ROUNDS + ch * C_ROUNDS
                if ch >= 2:
                    act.wait_ge(w_out[ch % 2], 16 * C_ROUNDS)
                if ch == 0:
                    turn(r0, r0, ch, between=True)
                with act.Fori(r0 + (ch == 0), r0 + C_ROUNDS - (ch == QT - 1)) as r:
                    turn(r, r0, ch)
                if ch == QT - 1:
                    turn(ROUNDS - 1, r0, ch, last=True)

        @block.vector
        def _(dve):
            STEPS = 14
            low = -3.0e38

            def route(r):
                n = [0]

                def link(ins, before_max=False):
                    n[0] += 1
                    ins.then_inc(r_step, 1)
                    dve.wait_ge(r_step, r * STEPS + n[0])
                    if before_max:
                        dve.memset(m.pause[:, :], 0.0)

                link(dve.tensor_copy(m.cur[:, :, :], m.ps[:, bass.ds(2 * r, 2), :]), True)
                dve.max(m.best[:, 0, 0:8], m.cur[:, 0, :])
                link(dve.max(m.best[:, 1, 0:8], m.cur[:, 1, :]), True)
                for c in range(2):
                    dve.max_index(m.where[:, c, 0:8], m.best[:, c, 0:8], m.cur[:, c, :])
                    ins = dve.match_replace(m.cur2[:, c, :], m.best[:, c, 0:8], m.cur[:, c, :], low)
                link(ins, True)
                dve.max(m.best[:, 0, 8:16], m.cur2[:, 0, :])
                link(dve.max(m.best[:, 1, 8:16], m.cur2[:, 1, :]), True)
                for c in range(2):
                    dve.max_index(m.where[:, c, 8:16], m.best[:, c, 8:16], m.cur2[:, c, :])
                link(dve.tensor_tensor(m.cand[:, :].rearrange("p (a b) -> p a b", a=TOPK),
                                       m.best[:, 0, :].unsqueeze(2).to_broadcast([P, TOPK, TOPK]),
                                       m.best[:, 1, :].unsqueeze(1).to_broadcast([P, TOPK, TOPK]), ALU.add))
                dve.tensor_copy(m.wheref[:, :, :], m.where[:, :, :])
                split(dve, r + 1, 0)
                link(dve.max(m.ctop[:, 0:8], m.cand[:, :]), True)
                dve.max_index(m.cpos[:, 0:8], m.ctop[:, 0:8], m.cand[:, :])
                link(dve.match_replace(m.cand2[:, :], m.ctop[:, 0:8], m.cand[:, :], low), True)
                link(dve.max(m.ctop[:, 8:16], m.cand2[:, :]), True)
                link(dve.max_index(m.cpos[:, 8:16], m.ctop[:, 8:16], m.cand2[:, :]))
                dve.tensor_scalar(m.rc[:, 0, :], m.cpos[:, :], 4, None, ALU.logical_shift_right)
                link(dve.tensor_scalar(m.rc[:, 1, :], m.cpos[:, :], 15, None, ALU.bitwise_and))
                link(dve.tensor_copy(m.rcf[:, :, :], m.rc[:, :, :]))
                for c in range(2):
                    ins = dve.tensor_tensor(m.pick[:, c], m.rcf[:, c, :].unsqueeze(2).to_broadcast([P, TOPK, TOPK]),
                                            m.iota[:, 0:TOPK].unsqueeze(1).to_broadcast([P, TOPK, TOPK]), ALU.is_equal)
                link(ins)
                for c in range(2):
                    ins = dve.tensor_tensor(m.pick[:, c], m.pick[:, c],
                                            m.wheref[:, c, :].unsqueeze(1).to_broadcast([P, TOPK, TOPK]), ALU.mult)
                link(ins)
                for c in range(2):
                    dve.tensor_reduce(routed[:, c, bass.ds(r * TOPK, TOPK)], m.pick[:, c], X, ALU.add)
                dve.tensor_scalar(routed[:, 2, bass.ds(r * TOPK, TOPK)], m.ctop[:, :], m.ctop[:, 0:1], None,
                                  ALU.subtract).then_inc(routed_ok, 1)
                link(dve.tensor_copy(m.cur2[:, 0, 0:1], m.ctop[:, 0:1]))
                return n[0]

            dve.wait_ge(iota_ok, 2)
            split(dve, 0, 0)
            with dve.Fori(0, R_ROUNDS) as r:
                steps = route(r)
            assert steps == STEPS, steps
            dve.wait_ge(g_exp, 1)
            dve.tensor_reduce(m.gsum[:, 0, :], routed[:, 2].rearrange("p (u k) -> p u k", k=TOPK), X, ALU.add
                              ).then_inc(g_norm, 1)
            dve.wait_ge(g_norm, 1)
            dve.reciprocal(m.gsum[:, 1, :], m.gsum[:, 0, :]).then_inc(g_norm, 1)
            dve.wait_ge(g_norm, 2)
            g3 = routed[:, 2].rearrange("p (u k) -> p u k", k=TOPK)
            dve.tensor_tensor(g3, g3, m.gsum[:, 1, :].unsqueeze(2).to_broadcast([P, QT * PH, TOPK]), ALU.mult
                              ).then_inc(g_norm, 1)
            for n in range(3):
                dve.wait_ge(slot_mm, n + 1)
                dve.tensor_copy((m.slot_key[:, 0], m.slot_key[:, 1], m.slot_gate[:, 0])[n], psum[:, 4 + n, :]
                                ).then_inc(slot_ok, 1)
            n_slot = 3
            src = psum[:, 6, :]
            for n in range(1, 3):
                dve.wait_ge(slot_ok, n_slot)
                dve.tensor_tensor(m.slot_rest[:, :], src, m.slot_gate[:, n - 1], ALU.subtract).then_inc(slot_ok, 1)
                dve.wait_ge(slot_ok, n_slot + 1)
                dve.tensor_copy(m.slot_gate[:, n], m.slot_rest[:, :]).then_inc(slot_ok, 1)
                n_slot += 2
                src = m.slot_rest[:, :]
            dve.wait_ge(slot_ok, n_slot)

            def hots(r, n, first=False):
                q = (r - R_ROUNDS) * (TOK // QUAD) + n
                if not first:
                    dve.wait_ge(w_mm, q - 1)

                def row(x):
                    return x[:, bass.ds(q * QUAD, QUAD)].unsqueeze(1).to_broadcast([P, NKEYS, QUAD])

                dve.tensor_tensor(m.is1[:, n % 2], m.iota4[:, :, :], row(m.slot_key[:, 0]), ALU.is_equal
                                  ).then_inc(is1_ok, 1)
                dve.tensor_tensor(m.hot2[:, n % 2], m.iota4[:, :, :], row(m.slot_key[:, 1]), ALU.is_equal)
                dve.wait_ge(is1_ok, q + 1)
                for g in range(3):
                    ins = dve.tensor_tensor(m.hot1[:, n % 2, g], m.is1[:, n % 2], row(m.slot_gate[:, g]), ALU.mult)
                ins.then_inc(hot_ok, 1)

            def turn(r, first=False, last=False):
                for n in range(TOK // QUAD):
                    if not last and n == 2:
                        split(dve, r + 1, 0)
                    hots(r, n, first and n < 2)
    
            turn(R_ROUNDS, first=True)
            with dve.Fori(R_ROUNDS + 1, ROUNDS - 1) as r:
                turn(r)
            turn(ROUNDS - 1, last=True)

        @block.tensor
        def _(pe):
            def tile(r, c, first=False):
                pe.wait_ge(lo_ok[c], r + 1)
                if not first:
                    pe.wait_ge(a_ok, 2 * r - 1 + c)
                product3(pe, psum[:, c, :], hi[:, c], lo[:, c], m.h_hi, m.h_lo).then_inc(a_mm, 1)

            def gates(r, n, first):
                q = (r - R_ROUNDS) * (TOK // QUAD) + n
                if not (first and n < 2):
                    pe.wait_ge(w_ok, q - 1)
                pe.wait_ge(hot_ok, q + 1)
                for j in range(QUAD):
                    for g in range(3):
                        mm = pe.matmul(psum[:, 2 + n % 2, j * P:(j + 1) * P], m.hot2[:, n % 2, :, j],
                                       m.hot1[:, n % 2, g, :, j], start=(g == 0), stop=(g == 2))
                mm.then_inc(w_mm, 1)

            tile(0, 0, True)
            tile(0, 1, True)
            with pe.Fori(1, R_ROUNDS) as r:
                for c in range(2):
                    tile(r, c)

            def turn(r):
                for c in range(2):
                    tile(r, c)
                    gates(r, 2 * c, False)
                    gates(r, 2 * c + 1, False)

            tile(R_ROUNDS, 0)
            pe.wait_ge(g_norm, 3)
            for n in range(3):
                for t in range(QT):
                    mm = pe.transpose(psum[:, 4 + n, t * P:(t + 1) * P], routed[:, n, t * P:(t + 1) * P], m.eye[:, :])
                mm.then_inc(slot_mm, 1)
            tile(R_ROUNDS, 1)
            for n in range(TOK // QUAD):
                gates(R_ROUNDS, n, n < 2)
            with pe.Fori(R_ROUNDS + 1, ROUNDS) as r:
                turn(r)


def combine(nc, io, m, psum):
    with ExitStack() as ctx:
        sb = m.scratch().take

        def sem(name):
            return ctx.enter_context(nc.semaphore(name))

        raw = m.v_raw
        hi = sb("v_hi", [P, 2, D], F32R)
        lo = sb("v_lo", [P, 2, D], F32R)
        acts, gates = m.acts_in, m.gates_in
        wa = sb("wa", [P, 2, S])
        wa_hi = sb("wa_hi", [P, 2, S], F32R)
        wa_lo = sb("wa_lo", [P, 2, S], F32R)
        early = m.early()
        x2 = early.take("x2_back", [P, QT, D])
        fg = early.take("final_gain", [P, D])
        junk = early.take("fjunk", [P, D])
        stat = early.take("fstat", [P, 4, QT])
        v_in, x2_in = m.v_in, sem("x2_in")
        ag_in = m.ag_in
        vhi_ok, vlo_ok, wa_ok, wahi_ok, walo_ok, o_mm = (
            sem("vhi_ok"), sem("vlo_ok"), sem("wa_ok"), sem("wahi_ok"), sem("walo_ok"), sem("o2_mm"))
        f_add, f_sq, f_var, f_std, f_rs, f_sc, f_ok, f_out = (
            sem("f_add"), sem("f_sq"), sem("f_var"), sem("f_std"), sem("f_rs"), sem("f_sc"), sem("f_ok"), sem("f_out"))
        block = ctx.enter_context(nc.Block())

        @block.sync
        def _(sp):
            def load(r, c):
                sp.dma_start(raw[:, c, :], io.v[bass.ds(2 * r + c, 1)].rearrange("o p n -> p (o n)")
                             ).then_inc(v_in[c], 16)

            with sp.Fori(1, ROUNDS) as r:
                for c in range(2):
                    sp.wait_ge(vlo_ok, 2 * r - 1 + c)
                    load(r, c)
            sp.dma_start(x2[:, :, :], io.x2.rearrange("(t p) d -> p t d", p=P)).then_inc(x2_in, 16)
            sp.dma_start(fg[:, :], io.final_g.partition_broadcast(P)).then_inc(x2_in, 16)
            for t in range(QT):
                sp.wait_ge(f_ok, t + 1)
                sp.dma_start(io.out.rearrange("(t p) d -> t p d", p=P)[t], x2[:, t, :]).then_inc(f_out, 16)
            sp.wait_ge(f_out, 16 * QT)

        @block.gpsimd
        def _(pool):
            for c in range(2):
                pool.wait_ge(m.a_out[c], 16 * ROUNDS)
            pool.wait_ge(m.w_out[0], 16 * (2 * C_ROUNDS - 2))
            with pool.Fori(1, ROUNDS) as r:
                for c in range(2):
                    pool.wait_ge(wa_ok, 2 * r - 1 + c)
                    pool.dma_start(acts[:, c, :], io.acts[bass.ds(2 * r + c, 1)].rearrange("o p n -> p (o n)")
                                   ).then_inc(ag_in[c], 16)
                    pool.dma_start(gates[:, c, :],
                                   io.gates[bass.ds(2 * r + c, 1), :, 0:STORED].rearrange("o p n -> p (o n)")
                                   ).then_inc(ag_in[c], 16)

        @block.scalar
        def _(act):
            def split(r, c, first=False):
                act.wait_ge(v_in[c], 16 * r + 16)
                if not first:
                    act.wait_ge(o_mm, 2 * r - 1 + c)
                act.activation(hi[:, c, :], raw[:, c, :], ACT.Copy).then_inc(vhi_ok, 1)
                act.wait_ge(wa_ok, 2 * r + 1 + c)
                act.activation(wa_hi[:, c, :], wa[:, c, :], ACT.Copy).then_inc(wahi_ok, 1)

            split(0, 0, True)
            split(0, 1, True)
            with act.Fori(1, ROUNDS) as r:
                for c in range(2):
                    split(r, c)
            for t in range(QT):
                act.wait_ge(f_add, t + 1)
                if t:
                    act.wait_ge(f_sq, t)
                act.activation(junk[:, :], x2[:, t, :], ACT.Square, accum_out=stat[:, 0, t:t + 1]).then_inc(f_sq, 1)
                act.wait_ge(f_var, t + 1)
                act.activation(stat[:, 2, t:t + 1], stat[:, 1, t:t + 1], ACT.Sqrt).then_inc(f_std, 1)

        @block.vector
        def _(dve):
            def split(r, c, first=False):
                dve.wait_ge(ag_in[c], 32 * r + 32)
                if not first:
                    dve.wait_ge(walo_ok, 2 * r - 1 + c)
                    dve.wait_ge(wahi_ok, 2 * r - 1 + c)
                dve.tensor_tensor(wa[:, c, 0:STORED], acts[:, c, 0:STORED], gates[:, c, :], ALU.mult)
                dve.tensor_tensor(wa[:, c, STORED:S], acts[:, c, STORED:S],
                                  m.dense[:, (QT - 1) % 2, bass.ds(2 * r + c, 1), :].rearrange("p o t -> p (o t)"),
                                  ALU.mult).then_inc(wa_ok, 1)
                dve.wait_ge(vhi_ok, 2 * r + 1 + c)
                dve.tensor_tensor(lo[:, c, :], raw[:, c, :], hi[:, c, :].bitcast(F32), ALU.subtract).then_inc(vlo_ok, 1)
                dve.wait_ge(wahi_ok, 2 * r + 1 + c)
                dve.tensor_tensor(wa_lo[:, c, :], wa[:, c, :], wa_hi[:, c, :].bitcast(F32), ALU.subtract
                                  ).then_inc(walo_ok, 1)

            split(0, 0, True)
            split(0, 1, True)
            with dve.Fori(1, ROUNDS) as r:
                for c in range(2):
                    split(r, c)
            dve.wait_ge(x2_in, 32)
            dve.wait_ge(o_mm, N_TILES)
            for t in range(QT):
                xt = x2[:, t, :].rearrange("p (b n) -> p b n", b=2)
                dve.tensor_tensor(xt, psum[:, 2 * t:2 * t + 2, :], xt, ALU.add).then_inc(f_add, 1)
            for t in range(QT):
                dve.wait_ge(f_sq, t + 1)
                dve.tensor_scalar(stat[:, 1, t:t + 1], stat[:, 0, t:t + 1], 1.0 / D, EPS, ALU.mult, ALU.add
                                  ).then_inc(f_var, 1)
                dve.wait_ge(f_std, t + 1)
                dve.reciprocal(stat[:, 3, t:t + 1], stat[:, 2, t:t + 1]).then_inc(f_rs, 1)
                dve.wait_ge(f_rs, t + 1)
                dve.scalar_tensor_tensor(out=x2[:, t, :], in0=x2[:, t, :], scalar=stat[:, 3, t:t + 1], in1=fg[:, :],
                                         op0=ALU.mult, op1=ALU.mult).then_inc(f_ok, 1)

        @block.tensor
        def _(pe):
            def tile(r, c, first=False, last=False):
                pe.wait_ge(vlo_ok, 2 * r + 1 + c)
                pe.wait_ge(walo_ok, 2 * r + 1 + c)
                for t in range(QT):
                    ts = slice(t * P, (t + 1) * P)
                    for b in range(2):
                        bs = slice(b * S, (b + 1) * S)
                        for n, (w, v) in enumerate(((wa_hi, hi), (wa_hi, lo), (wa_lo, hi))):
                            mm = pe.matmul(psum[:, 2 * t + b, :], w[:, c, ts], v[:, c, bs],
                                           start=(first and n == 0), stop=(last and n == 2), skip_group_check=True)
                mm.then_inc(o_mm, 1)

            tile(0, 0, first=True)
            tile(0, 1)
            with pe.Fori(1, ROUNDS - 1) as r:
                for c in range(2):
                    tile(r, c)
            tile(ROUNDS - 1, 0)
            tile(ROUNDS - 1, 1, last=True)



def hymba_peer_layer(nc, io, until=6):
    KB = 1024
    m = Memory()
    base = (nc.sbuf_base + 63) // 64 * 64
    end = nc.sbuf_usable_end
    shared = base + 1 * KB
    late = shared + 32 * KB
    rows = late + 16 * KB
    rest = rows + 16 * KB

    top = Region(nc, base, shared)
    m.eye = top.take("eye", [P, P])
    m.iota = top.take("iota", [P, P])
    m.early = lambda: Region(nc, shared, late)
    m.late = lambda: Region(nc, late, rows)
    m.x = Region(nc, rows, rest).take("x_rows", [P, QT, D])
    kept = Region(nc, rest, end)
    m.mask = kept.take("mask", [P, S])
    m.seen = kept.take("seen", [P, 1])
    m.bias = kept.take("bias", [P, HEADS, BIAS_W])
    m.rows = kept.take("rows", [P, QT, ROW_W])
    m.kT = kept.take("kT", [P, 2, S])
    m.qT = kept.take("qT", [P, 4, S])
    m.kcT = kept.take("kcT", [P, N_CMP])
    m.vc = kept.take("vc", [N_CMP, GROUPS * DH])
    m.gate = kept.take("gate", [P, QT, 3 * HEADS])
    m.lstat = kept.take("lstat", [P, 3, 2 * QT])
    m.lsum = kept.take("lsum", [P, QT])
    m.inv = kept.take("inv", [P, HALF])
    m.pos = kept.take("pos", [P, QT], I32)
    values_at = kept.at
    m.mla_values = lambda: Region(nc, values_at, values_at + 8 * KB)
    m.vm = kept.take("vm", [P, QT, HEADS * DH])
    attend_free = kept.at
    m.wq_up = kept.take("wq_up", [P, 2, HEADS * QK])
    m.wkv_up = kept.take("wkv_up", [P, HEADS * (NOPE + DH)])
    m.latT = kept.take("latT", [P, 3, S])
    tail = end // 32 * 32 - 29 * KB
    last = Region(nc, tail, end)
    m.o_lo = last.take("o_lo", [P, KD, S], F32R)
    m.ssq = last.take("ssq", [P, 2, S])
    m.wo_raw = last.take("wo_raw", [P, 2, D])
    m.gain = last.take("gain", [P, 2, KD])

    with ExitStack() as own:
        psum = own.enter_context(nc.psum_tensor("psum", [P, 8, S], F32))
        m.wq_in = [own.enter_context(nc.semaphore("wq_in0")), own.enter_context(nc.semaphore("wq_in1"))]
        m.u_in = [own.enter_context(nc.semaphore("u_in0")), own.enter_context(nc.semaphore("u_in1"))]
        m.keys_in = own.enter_context(nc.semaphore("keys_in"))
        m.gain_in = own.enter_context(nc.semaphore("gain_in"))
        m.wo_in = [own.enter_context(nc.semaphore("wo_in0")), own.enter_context(nc.semaphore("wo_in1"))]
        m.scratch = lambda: Region(nc, kept.at, end)
        project(nc, io, m, psum)
        if until < 2:
            return m
        early = m.early()
        m.qmT = early.take("qmT", [QK, HEADS, S])
        m.kmT = early.take("kmT", [QK, HEADS, S])
        latents(nc, io, m, psum)
        m.scratch = lambda: Region(nc, attend_free, tail)
        m.o_hi = m.late().take("o_hi", [P, KD, S], F32R)
        attend(nc, io, m, psum)
        if until < 3:
            return m
        parts = m.early()
        m.h_hi = parts.take("h_hi", [P, KD, S], F32R)
        m.h_lo = parts.take("h_lo", [P, KD, S], F32R)
        after = late + 2 * NKEYS * CHUNK * 4
        first = Region(nc, after, tail)
        m.wq_raw = first.take("wq_raw", [P, 2, KD, P])
        m.keys = first.take("keysT", [P, 2, NKEYS])
        m.scratch = lambda: Region(nc, rest, after)
        output(nc, io, m, psum)
        if until < 4:
            return m
        m.dense = Region(nc, late, after).take("dense", [P, 2, NKEYS, CHUNK])
        before = Region(nc, late, after)
        m.ps = before.take("peer_s", [P, QT * PH * 2, NKEYS])
        m.cur = before.take("cur", [P, 2, NKEYS])
        m.cur2 = before.take("cur2", [P, 2, NKEYS])
        m.best = before.take("best", [P, 2, TOPK])
        m.where = before.take("where", [P, 2, TOPK], U32)
        m.wheref = before.take("wheref", [P, 2, TOPK])
        m.cand = before.take("cand", [P, TOPK * TOPK])
        m.cand2 = before.take("cand2", [P, TOPK * TOPK])
        m.ctop = before.take("ctop", [P, TOPK])
        m.cpos = before.take("cpos", [P, TOPK], U32)
        m.rc = before.take("rc", [P, 2, TOPK], U32)
        m.rcf = before.take("rcf", [P, 2, TOPK])
        m.pause = before.take("pause", [P, 1])
        m.pick = before.take("pick", [P, 2, TOPK, TOPK])
        m.gsum = before.take("gsum", [P, 2, QT * PH])
        u_at = end // 32 * 32 - 8 * KB
        m.u_raw = Region(nc, u_at, end).take("u_raw", [P, 2, KD, P])
        m.scratch = lambda: Region(nc, first.at, u_at)
        peer_scores(nc, io, m, psum)
        if until < 5:
            return m
        slots = Region(nc, after, u_at)
        m.slot_key = slots.take("slot_key", [P, 2, S], BF16)
        m.slot_gate = slots.take("slot_gate", [P, 3, S], BF16)
        m.iota4 = slots.take("iota4", [P, NKEYS, QUAD], BF16)
        turned = Region(nc, slots.at, u_at)
        m.routed = turned.take("routed", [P, 3, S])
        m.slot_rest = turned.take("slot_rest", [P, S])
        m.is1 = slots.take("is1", [P, 2, NKEYS, QUAD], BF16)
        m.hot2 = slots.take("hot2", [P, 2, NKEYS, QUAD], BF16)
        m.hot1 = slots.take("hot1", [P, 2, 3, NKEYS, QUAD], BF16)
        ahead = Region(nc, late, after)
        m.v_raw = ahead.take("v_raw", [P, 2, D])
        m.acts_in = ahead.take("acts_in", [P, 2, S])
        m.gates_in = ahead.take("gates_in", [P, 2, STORED])
        m.a_out = [own.enter_context(nc.semaphore("a_out0")), own.enter_context(nc.semaphore("a_out1"))]
        m.w_out = [own.enter_context(nc.semaphore("w_out0")), own.enter_context(nc.semaphore("w_out1"))]
        m.ag_in = [own.enter_context(nc.semaphore("ag_in0")), own.enter_context(nc.semaphore("ag_in1"))]
        m.v_in = [own.enter_context(nc.semaphore("v_in0")), own.enter_context(nc.semaphore("v_in1"))]
        m.scratch = lambda: Region(nc, slots.at, u_at)
        experts(nc, io, m, psum)
        if until < 6:
            return m
        m.scratch = lambda: Region(nc, after, end)
        combine(nc, io, m, psum)
    return m


def bucket_onehot():
    dist = S - 1 - np.arange(BIAS_L)
    d = np.maximum(dist, 1).astype(np.float32)
    exact = BUCKETS // 2
    large = exact + (np.log(d / exact) / np.float32(np.log(2048 / exact)) * (BUCKETS - exact)).astype(np.int32)
    bucket = np.where(dist < exact, np.maximum(dist, 0), np.minimum(large, BUCKETS - 1))
    bucket = np.where(dist < 0, BUCKETS, bucket)
    return (np.arange(BUCKETS + 1)[:, None] == bucket[None, :]).astype(np.float32)


def layout(inputs):
    c = np.ascontiguousarray
    a = {k: np.asarray(v) for k, v in inputs.items()}

    def tiles(w):
        return c(w.reshape(-1, P, w.shape[1]).transpose(1, 0, 2))

    def column_tiles(w):
        return c(w.reshape(-1, P, w.shape[1] // P, P).transpose(2, 1, 0, 3))

    sizes = [NSA_W] + [GROUPS * DH] * 6 + [3 * HEADS, Q_LORA, KV_LORA, ROPE]
    cuts = np.split(a["w_in"][0], np.cumsum(sizes)[:-1], axis=1)
    q, kc, vc, ks, vs, kw, vw, gates, cq, ckv, kr = cuts
    q = q.reshape(D, GROUPS, HEADS // GROUPS, DH).transpose(0, 2, 1, 3).reshape(D, NSA_W)
    kv_up = a["w_kv_up"][0].reshape(KV_LORA, HEADS, 2, NOPE).transpose(0, 2, 1, 3).reshape(KV_LORA, -1)
    pairs = a["cmp_pos"][0].reshape(LP, P).T
    return {
        "x": c(a["x"].reshape(S, D)),
        "positions": c(a["positions"].reshape(QT, P).T),
        "g1": c(a["norm1_g"][0].reshape(KD, P).T),
        "qkvg": c(np.concatenate([a["q_norm_g"][0], a["kv_norm_g"][0]]).reshape(3, P).T),
        "cmp_posT": c(pairs),
        "w_rows": tiles(np.concatenate([cq, ckv, vs, vw, kr, gates], axis=1)),
        "w_cols": column_tiles(np.concatenate([kc, vc, ks, kw, q], axis=1)),
        "w1k": tiles(a["cmp_k_w1"][0]),
        "w1v": tiles(a["cmp_v_w1"][0]),
        "w2": c(np.stack([tiles(a["cmp_k_w2"][0]), tiles(a["cmp_v_w2"][0])], axis=1)),
        "t5": c(a["t5_bias"]),
        "bucket_onehot": bucket_onehot(),
        "inv_freq": (10000.0 ** (-np.arange(HALF, dtype=np.float32) / HALF)).astype(np.float32),
        "wq_up": tiles(a["w_q_up"][0]),
        "wkv_up": c(kv_up),
        "grp_gain": c(np.concatenate([a["grp_norm_nsa"][0], a["grp_norm_mla"][0]]).reshape(KD, P).T),
        "w_out": tiles(a["w_out"][0]),
        "g2": c(a["norm2_g"][0].reshape(KD, P).T),
        "wq": column_tiles(a["peer_wq"][0]),
        "keysT": c(np.stack([a["peer_keys1"][0].T, a["peer_keys2"][0].T], axis=1)),
        "uT": c(a["peer_u"][0].reshape(NKEYS, P, KD, P).transpose(0, 3, 2, 1)),
        "v": c(a["peer_v"][0].reshape(NKEYS, P, D)),
        "final_g": c(a["final_g"]),
    }


class Dram:

    def __init__(self, nc, arrays):
        def given(name):
            a = arrays[name]
            return nc.dram_tensor(name, a.shape, mybir.dt.from_np(a.dtype), kind="ExternalInput").ap()

        def scratch(name, shape):
            return nc.dram_tensor(name, shape, F32, kind="Internal").ap()

        self.x = given("x")
        self.positions = given("positions")
        self.g1 = given("g1")
        self.qkvg = given("qkvg")
        self.cmp_posT = given("cmp_posT")
        self.w_rows = given("w_rows")
        self.w_cols = given("w_cols")
        self.w1k = given("w1k")
        self.w1v = given("w1v")
        self.w2 = given("w2")
        self.t5 = given("t5")
        self.bucket_onehot = given("bucket_onehot")
        self.inv_freq = given("inv_freq")
        self.wq_up = given("wq_up")
        self.wkv_up = given("wkv_up")
        self.grp_gain = given("grp_gain")
        self.w_out = given("w_out")
        self.g2 = given("g2")
        self.wq = given("wq")
        self.keysT = given("keysT")
        self.uT = given("uT")
        self.v = given("v")
        self.final_g = given("final_g")
        self.bias_rows = scratch("bias_rows", (HEADS, BIAS_L))
        self.bias_rep = scratch("bias_rep", (P, HEADS * BIAS_L))
        self.x2 = scratch("x2", (S, D))
        self.acts = scratch("acts", (NKEYS, P, S))
        self.gates = scratch("gates", (NKEYS, P, S))
        self.out = nc.dram_tensor("out", (S, D), F32, kind="ExternalOutput").ap()


def kernel(**inputs):
    import concourse.bacc as bacc
    from concourse.bass_utils import run_bass_kernel_spmd

    arrays = layout(inputs)
    nc = bacc.Bacc("TRN2", target_bir_lowering=False, num_devices=1)
    hymba_peer_layer(nc, Dram(nc, arrays))
    result = run_bass_kernel_spmd(nc, [arrays], core_ids=[0])
    return result.results[0]["out"].reshape(1, S, D)
```

```python
from contextlib import ExitStack

import numpy as np

import concourse.bass as bass
from concourse import mybir

F32 = mybir.dt.float32
F32R = mybir.dt.float32r
BF16 = mybir.dt.bfloat16
I32 = mybir.dt.int32
U32 = mybir.dt.uint32
ALU = mybir.AluOpType
ACT = mybir.ActivationFunctionType
X = mybir.AxisListType.X

P = 128
D = 1024
S = 512
QT = S // P
KD = D // P
DH = 64
HEADS = 8
GROUPS = 2
NSA_W = HEADS * DH
CMP_LEN, CMP_STRIDE, CMP_HID = 32, 16, 256
N_CMP = (S - CMP_LEN) // CMP_STRIDE + 1
LP = CMP_LEN * DH // P
HT = CMP_HID // P
Q_LORA, KV_LORA, NOPE, ROPE = 256, 128, 64, 32
HALF = ROPE // 2
QK = NOPE + ROPE
MLA_SCALE = QK ** -0.5
NSA_SCALE = DH ** -0.5
EPS = 1e-6
NEG = -1e30
BUCKETS = 32
R_CQ, R_CKV, R_VS, R_VW, R_KR, R_G = 0, 256, 384, 512, 640, 672
ROW_W = 696
C_KC, C_VC, C_KS, C_KW, C_Q = 0, 1, 2, 3, 4
N_COLS = 8
BIAS_L = 1024
BIAS_W = 896
NKEYS = 128
TOPK = 16
PH = 8
TWO_PI_HI = 6.28125
TWO_PI_MID = float(np.float32(0.0019350051879882812))
TWO_PI_LO = float(2 * np.pi - 6.28125 - 0.0019350051879882812)
ROUND = 12582912.0
PI_IN = 3.1415925


class Memory:
    pass


class Region:

    def __init__(self, nc, start, end):
        self.nc, self.at, self.end = nc, start, end

    def take(self, name, shape, dt=F32):
        size = int(np.prod(shape[1:])) * (2 if dt == BF16 else 4)
        tensor = self.nc.alloc_sbuf_tensor_at(name, shape, dt, offset=self.at)
        self.at += (size + 31) // 32 * 32
        assert self.at <= self.end, (name, self.at, self.end)
        return tensor


def product3(pe, bank, w_hi, w_lo, x_hi, x_lo):
    n = 3 * KD
    i = 0
    for k in range(KD):
        for w, x in ((w_hi, x_hi), (w_hi, x_lo), (w_lo, x_hi)):
            mm = pe.matmul(bank, w[:, k, :], x[:, k, :], start=(i == 0), stop=(i == n - 1))
            i += 1
    return mm


def project(nc, io, m, psum):
    with ExitStack() as ctx:
        sb = m.scratch().take

        def sem(name):
            return ctx.enter_context(nc.semaphore(name))

        early = m.early()
        h_hi = early.take("hn_hi", [P, KD, S], F32R)
        h_lo = early.take("hn_lo", [P, KD, S], F32R)
        early = m.early()
        part = early.take("part", [P, 4, QT, HEADS, HALF])
        junk = early.take("junk", [P, 2, D])
        late = m.late()
        onehot = late.take("onehot", [BUCKETS + 1, BIAS_L])
        brow = late.take("brow", [HEADS, BIAS_L])
        blk = late.take("blk", [P, 2, LP, GROUPS, N_CMP])
        qf = m.late().take("qf", [P, QT, HEADS, QK])
        w_raw = sb("w_raw", [P, 2, D])
        w_hi = sb("w_hi", [P, 2, D], F32R)
        w_lo = sb("w_lo", [P, 2, D], F32R)
        cT = sb("cT", [P, 2, S])
        pairs = m.mla_values().take("pairs", [P, 2, GROUPS, S])
        b_hi = sb("b_hi", [P, 2, LP, GROUPS, N_CMP], F32R)
        b_lo = sb("b_lo", [P, 2, LP, GROUPS, N_CMP], F32R)
        w2 = sb("w2", [P, 2, HT, DH])
        hid = sb("hid", [P, 2, HT, GROUPS * N_CMP])
        posT = sb("posT", [P, LP])
        g1 = sb("g1", [P, KD])
        qkvg = sb("qkvg", [P, 3])
        t5x = sb("t5x", [BUCKETS + 1, HEADS])
        stat = sb("stat", [P, 5, 4])
        scale = sb("xscale", [P, QT, P])
        both = sb("kf", [P, QT * HEADS * QK])
        kf = both[:, :].rearrange("p (t h d) -> p t h d", t=QT, h=HEADS)
        lat = both[:, 0:QT * 384].rearrange("p (t n) -> p t n", t=QT)
        posf = sb("posf", [P, QT])
        ang = sb("ang", [P, QT, HALF])
        turns = sb("turns", [P, 2, QT * HALF])
        red = sb("red", [P, 2, QT * HALF])
        trig = sb("trig", [P, 2, QT, HALF])
        kpart = sb("kpart", [P, 4, QT, HALF])
        krot = sb("krot", [P, QT, ROPE])
        spare = sb("spare", [P, 256])

        x_in = [sem(f"x_in{t}") for t in range(QT)]
        w_in = [sem("w_in0"), sem("w_in1")]
        small_in, w2_in, t5_in, up_in, pos_in = sem("small_in"), sem("w2_in"), sem("t5_in"), sem("up_in"), sem("pos_in")
        x_sq, x_var, x_std, x_rs, x_dg = sem("x_sq"), sem("x_var"), sem("x_std"), sem("x_rs"), sem("x_dg")
        xT_mm, hhi_ok, h_ok = sem("xT_mm"), sem("hhi_ok"), sem("h_ok")
        whi_ok, wlo_ok = sem("whi_ok"), sem("wlo_ok")
        tile_mm = sem("tile_mm")
        rows_mm, rows_a, rows_v = sem("rows_mm"), sem("rows_a"), sem("rows_v")
        cols_a, cols_v = sem("cols_a"), sem("cols_v")
        pair_ok, blk_ok, bhi_ok, blo_ok, hid_ok, cmp_mm, cmp_ok = (
            sem("pair_ok"), sem("blk_ok"), sem("bhi_ok"), sem("blo_ok"), sem("hid_ok"), sem("cmp_mm"), sem("cmp_ok"))
        lat_sq, lat_var, lat_std, lat_rs, lat_ok, latT_mm, latT_ok = (
            sem("lat_sq"), sem("lat_var"), sem("lat_std"), sem("lat_rs"), sem("lat_ok"), sem("latT_mm"), sem("latT_ok"))
        b_mm, b_row, b_out, b_rep, b_tile = sem("b_mm"), sem("b_row"), sem("b_out"), sem("b_rep"), sem("b_tile")
        neg_ok, eye_ok, ones_ok = sem("neg_ok"), sem("eye_ok"), sem("ones_ok")
        step, red_ok, trig_ok, gate_e = sem("rope_step"), sem("red_ok"), sem("trig_ok"), sem("gate_e")
        up_mm, upq_ok, upk_ok = sem("up_mm"), sem("upq_ok"), sem("upk_ok")
        q_rot, k_rot, qkT_mm, qkT_a, qkT_v = sem("q_rot"), sem("k_rot"), sem("qkT_mm"), sem("qkT_a"), sem("qkT_v")
        block = ctx.enter_context(nc.Block())
        R0, C0, H0, N_STREAM = 0, KD, KD + N_COLS, KD + N_COLS + 8
        UP_BANKS = 6

        def rows_done(eng, t):
            if t < QT - 1:
                eng.wait_ge(rows_mm, t + 1)
            else:
                eng.wait_ge(tile_mm, C0)

        def turned(u):
            return m.kmT[:, u, :] if u < HEADS else m.qmT[:, u - HEADS, :]

        @block.sync
        def _(sp):
            for t in range(QT):
                sp.dma_start(m.x[:, t, :], io.x.rearrange("(t p) d -> t p d", p=P)[t]).then_inc(x_in[t], 16)
            sp.dma_start(g1[:, :], io.g1).then_inc(small_in, 16)
            sp.dma_start(qkvg[:, :], io.qkvg).then_inc(small_in, 16)
            sp.dma_start(posT[:, :], io.cmp_posT).then_inc(small_in, 16)
            for i in range(N_STREAM):
                if i >= 2:
                    sp.wait_ge(wlo_ok, i - 1)
                dst = w_raw[:, i % 2, :]
                if i < C0:
                    sp.dma_start(dst[:, 0:ROW_W], io.w_rows[:, i, :]).then_inc(w_in[i % 2], 16)
                else:
                    src = io.w_cols[i - C0] if i < H0 else io.w1[i - H0]
                    sp.dma_start(dst, src.rearrange("p k n -> p (k n)")).then_inc(w_in[i % 2], 16)

        @block.gpsimd
        def _(pool):
            pool.memset(m.eye[:, :], 0.0).then_inc(eye_ok, 1)
            pool.wait_ge(eye_ok, 1)
            pool.affine_select(out=m.eye[:, :], in_=m.eye[:, :], compare_op=ALU.not_equal, fill=1.0,
                               base=0, pattern=[[-1, P]], channel_multiplier=1).then_inc(eye_ok, 1)
            pool.memset(m.mask[:, :], 0.0).then_inc(ones_ok, 1)
            pool.memset(m.seen[:, :], 1.0).then_inc(ones_ok, 1)
            pool.wait_ge(ones_ok, 2)
            pool.affine_select(out=m.mask[:, S - P:S], in_=m.mask[:, S - P:S], compare_op=ALU.is_ge, fill=NEG,
                               base=0, pattern=[[-1, P]], channel_multiplier=1)
            pool.affine_select(out=m.seen[:, :], in_=m.seen[:, :], compare_op=ALU.is_ge, fill=0.0,
                               base=-(CMP_LEN - 1), pattern=[[0, 1]], channel_multiplier=1).then_inc(ones_ok, 1)
            pool.wait_ge(b_row, 2)
            pool.dma_start(io.bias_rows, brow[:, :]).then_inc(b_out, 16)
            pool.wait_ge(b_out, 16)
            pool.dma_start(io.bias_rep.rearrange("p (h n) -> p h n", h=HEADS),
                           io.bias_rows.partition_broadcast(P)).then_inc(b_rep, 16)
            pool.wait_ge(b_rep, 16)
            skew = bass.AP(tensor=io.bias_rep.tensor, offset=P - 1,
                           ap=[[HEADS * BIAS_L - 1, P], [BIAS_L, HEADS], [1, BIAS_W]])
            for c in range(2):
                pool.wait_ge(cols_a if c == 0 else cols_v, 1)
                for g in range(GROUPS):
                    src = cT[g * DH:(g + 1) * DH, c, :]
                    pool.dma_start(pairs[0:DH, c, g, :], src).then_inc(pair_ok, 16)
                    pool.dma_start(pairs[DH:P, c, g, 0:S - 1], src[:, 1:S]).then_inc(pair_ok, 16)
            pool.dma_start(m.bias[:, :, :], skew).then_inc(b_tile, 16)
            pool.wait_ge(b_tile, 16)
            pool.wait_ge(pair_ok, 128)
            pool.wait_ge(ones_ok, 3)

        @block.scalar
        def _(act):
            act.dma_start(t5x[0:BUCKETS, :], io.t5).then_inc(t5_in, 16)
            act.dma_start(onehot[:, :], io.bucket_onehot).then_inc(t5_in, 16)
            act.dma_start(m.pos[:, :], io.positions).then_inc(pos_in, 16)
            act.dma_start(m.inv[:, :], io.inv_freq.partition_broadcast(P)).then_inc(pos_in, 16)
            act.dma_start(w2[:, :, :, :], io.w2).then_inc(w2_in, 16)

            def split(i):
                w = ROW_W if i < C0 else D
                act.wait_ge(w_in[i % 2], 16 * (i // 2 + 1))
                if i >= 2:
                    act.wait_ge(tile_mm, i - 1)
                act.activation(w_hi[:, i % 2, 0:w], w_raw[:, i % 2, 0:w], ACT.Copy).then_inc(whi_ok, 1)

            for t in range(QT):
                act.wait_ge(x_in[t], 16)
                if t >= 2:
                    act.wait_ge(x_sq, t - 1)
                act.activation(junk[:, t % 2, :], m.x[:, t, :], ACT.Square, accum_out=stat[:, 0, t:t + 1]).then_inc(x_sq, 1)
                act.wait_ge(x_var, t + 1)
                act.activation(stat[:, 2, t:t + 1], stat[:, 1, t:t + 1], ACT.Sqrt).then_inc(x_std, 1)
            act.dma_start(m.wq_up[:, :, :], io.wq_up).then_inc(up_in, 16)
            act.dma_start(m.wkv_up[:, :], io.wkv_up).then_inc(up_in, 16)
            split(0)
            split(1)
            act.wait_ge(small_in, 48)
            for k in range(KD):
                act.wait_ge(xT_mm, k + 1)
                act.activation(h_hi[:, k, :], psum[:, k, :], ACT.Copy, scale=g1[:, k:k + 1]).then_inc(hhi_ok, 1)
            for i in range(2, C0 + 1):
                split(i)
            for t in range(QT):
                rows_done(act, t)
                act.activation(m.rows[:, t, 0:S], psum[:, 2 * t, :], ACT.Copy).then_inc(rows_a, 1)
            split(C0 + 1)
            for j in range(N_COLS):
                if j % 2 == 0:
                    act.wait_ge(tile_mm, C0 + j + 1)
                    if j < C_Q:
                        dst = cT[:, 0, :] if j == C_KC else m.kT[:, 0, :]
                        act.activation(dst, psum[:, j, :], ACT.Copy).then_inc(cols_a, 1)
                    else:
                        act.activation(m.qT[:, j - C_Q, :], psum[:, j, :], ACT.Copy, scale=NSA_SCALE).then_inc(cols_a, 1)
                split(C0 + 2 + j)
                if j == 1:
                    for c, (lo, hi) in enumerate(((R_CQ, R_CKV), (R_CKV, R_VS))):
                        for t in range(QT):
                            if c + t:
                                act.wait_ge(lat_sq, c * QT + t)
                            act.wait_ge(rows_a, t + 1)
                            act.activation(spare[:, 0:hi - lo], m.rows[:, t, lo:hi], ACT.Square,
                                           accum_out=stat[:, 4, t:t + 1] if c == 0 else m.lsum[:, t:t + 1]
                                           ).then_inc(lat_sq, 1)
                if j == 2:
                    act.wait_ge(lat_var, 2)
                    act.activation(m.lstat[:, 1, :], m.lstat[:, 0, :], ACT.Sqrt).then_inc(lat_std, 1)
                if j == 3:
                    act.wait_ge(red_ok, 1)
                    act.activation(trig[:, :, :, :].rearrange("p c t d -> p (c t d)"),
                                   red[:, :, :].rearrange("p c n -> p (c n)"), ACT.Sin).then_inc(trig_ok, 1)
                if j == 4:
                    act.wait_ge(rows_v, QT)
                    act.activation(m.gate[:, :, :], m.rows[:, :, R_G:ROW_W], ACT.Exp, scale=-1.0).then_inc(gate_e, 1)
                if j == 6:
                    for c in range(2):
                        act.wait_ge(blk_ok, GROUPS * (c + 1))
                        act.activation(b_hi[:, c].rearrange("p l g n -> p (l g n)"),
                                       blk[:, c].rearrange("p l g n -> p (l g n)"), ACT.Copy).then_inc(bhi_ok, 1)
            for c in range(3):
                act.wait_ge(latT_mm, c + 1)
                act.activation(m.latT[:, c, :], psum[:, c, :], ACT.Copy, scale=qkvg[:, c:c + 1]).then_inc(latT_ok, 1)
            act.wait_ge(blo_ok, 2)
            act.wait_ge(b_out, 16)
            for t in range(QT):
                act.wait_ge(up_mm, t + 1)
                for b in range(2):
                    act.activation(qf[:, t, 4 * b:4 * b + 4, :].rearrange("p h d -> p (h d)"),
                                   psum[:, (4 * t + b) % UP_BANKS, 0:4 * QK], ACT.Copy).then_inc(upq_ok, 1)
                for i in (H0 + 2 * t + 2, H0 + 2 * t + 3):
                    if i < N_STREAM:
                        split(i)
            for c in range(2):
                act.wait_ge(tile_mm, H0 + 4 * (c + 1))
                act.activation(hid[:, c, :, :], psum[:, 6 + c, 0:HT * GROUPS * N_CMP].rearrange(
                    "p (h n) -> p h n", h=HT), ACT.Gelu).then_inc(hid_ok, 1)
            for u in range(0, 2 * HEADS, 2):
                act.wait_ge(qkT_mm, u + 1)
                act.activation(turned(u), psum[0:QK, u % UP_BANKS, :], ACT.Copy).then_inc(qkT_a, 1)

        @block.vector
        def _(dve):
            chain = [0]

            def link(ins):
                chain[0] += 1
                ins.then_inc(step, 1)
                dve.wait_ge(step, chain[0])

            def split(i):
                w = ROW_W if i < C0 else D
                dve.wait_ge(whi_ok, i + 1)
                dve.tensor_tensor(w_lo[:, i % 2, 0:w], w_raw[:, i % 2, 0:w], w_hi[:, i % 2, 0:w].bitcast(F32),
                                  ALU.subtract).then_inc(wlo_ok, 1)

            dve.memset(t5x[BUCKETS:BUCKETS + 1, :], NEG).then_inc(neg_ok, 1)
            for t in range(QT):
                if t == 1:
                    dve.wait_ge(b_mm, 1)
                    for b in range(2):
                        dve.tensor_copy(brow[:, b * S:(b + 1) * S], psum[0:HEADS, 6 + b, :]).then_inc(b_row, 1)
                dve.wait_ge(x_sq, t + 1)
                dve.tensor_scalar(stat[:, 1, t:t + 1], stat[:, 0, t:t + 1], 1.0 / D, EPS, ALU.mult, ALU.add).then_inc(x_var, 1)
                dve.wait_ge(x_std, t + 1)
                dve.reciprocal(stat[:, 3, t:t + 1], stat[:, 2, t:t + 1]).then_inc(x_rs, 1)
                dve.wait_ge(x_rs, t + 1)
                dve.wait_ge(eye_ok, 2)
                dve.tensor_scalar(scale[:, t, :], m.eye[:, :], stat[:, 3, t:t + 1], None, ALU.mult).then_inc(x_dg, 1)
            split(0)
            split(1)
            dve.wait_ge(small_in, 48)
            for k in range(KD):
                dve.wait_ge(hhi_ok, k + 1)
                dve.scalar_tensor_tensor(out=h_lo[:, k, :], in0=psum[:, k, :], scalar=g1[:, k:k + 1],
                                         in1=h_hi[:, k, :].bitcast(F32), op0=ALU.mult, op1=ALU.subtract).then_inc(h_ok, 1)
            for i in range(2, C0 + 1):
                split(i)
            for t in range(QT):
                rows_done(dve, t)
                dve.tensor_copy(m.rows[:, t, S:ROW_W], psum[:, 2 * t + 1, 0:ROW_W - S]).then_inc(rows_v, 1)
            split(C0 + 1)

            def angles():
                dve.wait_ge(pos_in, 32)
                link(dve.tensor_copy(posf[:, :], m.pos[:, :]))
                link(dve.tensor_tensor(ang[:, :, :], posf[:, :].unsqueeze(2).to_broadcast([P, QT, HALF]),
                                       m.inv[:, :].unsqueeze(1).to_broadcast([P, QT, HALF]), ALU.mult))
                a = ang[:, :, :].rearrange("p t d -> p (t d)")
                dve.tensor_scalar(turns[:, 0, :], a, 1 / (2 * np.pi), None, ALU.mult).then_inc(step, 1)
                chain[0] += 1
                link(dve.tensor_scalar(turns[:, 1, :], a, 1 / (2 * np.pi), 0.25, ALU.mult, ALU.add))
                link(dve.tensor_scalar(turns[:, :, :], turns[:, :, :], ROUND, None, ALU.add))
                link(dve.tensor_scalar(turns[:, :, :], turns[:, :, :], ROUND, None, ALU.subtract))
                src = ang[:, :, :].rearrange("p t d -> p (t d)").unsqueeze(1).to_broadcast([P, 2, QT * HALF])
                for c in (TWO_PI_HI, TWO_PI_MID, TWO_PI_LO):
                    link(dve.scalar_tensor_tensor(out=red[:, :, :], in0=turns[:, :, :], scalar=-c, in1=src,
                                                  op0=ALU.mult, op1=ALU.add))
                    src = red[:, :, :]
                link(dve.tensor_scalar(red[:, 1, :], red[:, 1, :], float(np.pi / 2), None, ALU.add))
                dve.tensor_scalar(red[:, :, :], red[:, :, :], PI_IN, -PI_IN, ALU.min, ALU.max).then_inc(red_ok, 1)

            def norms():
                dve.wait_ge(lat_std, 1)
                dve.reciprocal(m.lstat[:, 2, :], m.lstat[:, 1, :]).then_inc(lat_rs, 1)
                dve.wait_ge(lat_rs, 1)
                for t in range(QT):
                    dve.tensor_scalar(lat[:, t, 0:256], m.rows[:, t, R_CQ:R_CKV], m.lstat[:, 2, t:t + 1], None, ALU.mult)
                    dve.tensor_scalar(lat[:, t, 256:384], m.rows[:, t, R_CKV:R_VS], m.lstat[:, 2, QT + t:QT + t + 1],
                                      None, ALU.mult).then_inc(lat_ok, 1)

            def rotate_keys():
                dve.wait_ge(trig_ok, 1)
                k1, k2 = m.rows[:, :, R_KR:R_KR + HALF], m.rows[:, :, R_KR + HALF:R_G]
                sin, cos = trig[:, 0], trig[:, 1]
                for n, (xx, tt) in enumerate(((k1, cos), (k2, sin), (k1, sin), (k2, cos))):
                    dve.tensor_tensor(kpart[:, n], xx, tt, ALU.mult).then_inc(step, 1)
                    chain[0] += 1
                dve.wait_ge(step, chain[0])
                dve.tensor_tensor(krot[:, :, 0:HALF], kpart[:, 0], kpart[:, 1], ALU.subtract)
                link(dve.tensor_tensor(krot[:, :, HALF:ROPE], kpart[:, 2], kpart[:, 3], ALU.add))

            def rotate_queries(t):
                dve.wait_ge(upq_ok, 2 * t + 2)
                q1, q2 = qf[:, t, :, NOPE:NOPE + HALF], qf[:, t, :, NOPE + HALF:QK]
                sin_t = trig[:, 0, t, :].unsqueeze(1).to_broadcast([P, HEADS, HALF])
                cos_t = trig[:, 1, t, :].unsqueeze(1).to_broadcast([P, HEADS, HALF])
                for n, (xx, tt) in enumerate(((q1, cos_t), (q2, sin_t), (q1, sin_t), (q2, cos_t))):
                    dve.tensor_tensor(part[:, n, t], xx, tt, ALU.mult).then_inc(step, 1)
                    chain[0] += 1
                dve.wait_ge(step, chain[0])
                dve.tensor_tensor(qf[:, t, :, NOPE:NOPE + HALF], part[:, 0, t], part[:, 1, t], ALU.subtract
                                  ).then_inc(q_rot, 1)
                dve.tensor_tensor(qf[:, t, :, NOPE + HALF:QK], part[:, 2, t], part[:, 3, t], ALU.add).then_inc(q_rot, 1)

            def blocks():
                dve.wait_ge(pair_ok, 128)
                for c in range(2):
                    for g in range(GROUPS):
                        raw = pairs[:, c, g, :]
                        raw = bass.AP(tensor=raw.tensor, offset=raw.offset,
                                      ap=[raw.ap[0], [2, LP], [CMP_STRIDE, N_CMP]])
                        dve.tensor_tensor(blk[:, c, :, g, :], raw, posT[:, :].unsqueeze(2).to_broadcast([P, LP, N_CMP]),
                                          ALU.add).then_inc(blk_ok, 1)

            for j in range(N_COLS):
                if j % 2 == 1:
                    dve.wait_ge(tile_mm, C0 + j + 1)
                    if j < C_Q:
                        dst = cT[:, 1, :] if j == C_VC else m.kT[:, 1, :]
                        dve.tensor_copy(dst, psum[:, j, :]).then_inc(cols_v, 1)
                    else:
                        dve.tensor_scalar(m.qT[:, j - C_Q, :], psum[:, j, :], NSA_SCALE, None, ALU.mult).then_inc(cols_v, 1)
                split(C0 + 2 + j)
                if j == 0:
                    angles()
                if j == 1:
                    dve.wait_ge(lat_sq, 2 * QT)
                    dve.tensor_scalar(m.lstat[:, 0, 0:QT], stat[:, 4, :], 1.0 / Q_LORA, EPS, ALU.mult, ALU.add
                                      ).then_inc(lat_var, 1)
                    dve.tensor_scalar(m.lstat[:, 0, QT:], m.lsum[:, :], 1.0 / KV_LORA, EPS, ALU.mult, ALU.add
                                      ).then_inc(lat_var, 1)
                if j == 2:
                    norms()
                if j == 3:
                    rotate_keys()
                if j == 4:
                    dve.wait_ge(gate_e, 1)
                    link(dve.tensor_scalar(m.gate[:, :, :], m.gate[:, :, :], 1.0, None, ALU.add))
                    dve.reciprocal(m.gate[:, :, :], m.gate[:, :, :])
                if j == 5:
                    blocks()
                if j == 6:
                    for c in range(2):
                        dve.wait_ge(bhi_ok, c + 1)
                        dve.tensor_tensor(b_lo[:, c].rearrange("p l g n -> p (l g n)"),
                                          blk[:, c].rearrange("p l g n -> p (l g n)"),
                                          b_hi[:, c].rearrange("p l g n -> p (l g n)").bitcast(F32), ALU.subtract
                                          ).then_inc(blo_ok, 1)
            dve.wait_ge(latT_mm, 3)
            for t in range(QT):
                dve.tensor_copy(kf[:, t, :, NOPE:QK], krot[:, t, :].unsqueeze(1).to_broadcast([P, HEADS, ROPE])
                                ).then_inc(k_rot, 1)
            for t in range(QT):
                dve.wait_ge(up_mm, t + 1)
                dve.tensor_copy(kf[:, t, :, 0:NOPE],
                                psum[:, (4 * t + 2) % UP_BANKS, :].rearrange("p (h d) -> p h d", h=HEADS)
                                ).then_inc(upk_ok, 1)
                dve.tensor_copy(m.vm[:, t, :], psum[:, (4 * t + 3) % UP_BANKS, :]).then_inc(upk_ok, 1)
                for i in (H0 + 2 * t + 2, H0 + 2 * t + 3):
                    if i < N_STREAM:
                        split(i)
                rotate_queries(t)
            for u in range(1, HEADS, 2):
                dve.wait_ge(qkT_mm, u + 1)
                dve.tensor_copy(turned(u), psum[0:QK, u % UP_BANKS, :]).then_inc(qkT_v, 1)
            dve.wait_ge(cmp_mm, 1)
            dve.tensor_copy(m.kcT[0:DH, :], psum[0:DH, 6, 0:N_CMP]).then_inc(cmp_ok, 1)
            dve.tensor_copy(m.kcT[DH:P, :], psum[DH:P, 6, 0:N_CMP]).then_inc(cmp_ok, 1)
            dve.wait_ge(cmp_mm, 2)
            dve.tensor_copy(m.vc[:, :], psum[0:N_CMP, 7, 0:GROUPS * DH]).then_inc(cmp_ok, 1)
            for u in range(HEADS + 1, 2 * HEADS, 2):
                dve.wait_ge(qkT_mm, u + 1)
                dve.tensor_copy(turned(u), psum[0:QK, u % UP_BANKS, :]).then_inc(qkT_v, 1)

        @block.tensor
        def _(pe):
            pe.wait_ge(t5_in, 32)
            pe.wait_ge(neg_ok, 1)
            for b in range(2):
                mm = pe.matmul(psum[0:HEADS, 6 + b, :], t5x[:, :], onehot[:, b * S:(b + 1) * S], start=True, stop=True)
            mm.then_inc(b_mm, 1)
            for t in range(QT):
                pe.wait_ge(x_dg, t + 1)
                for k in range(KD):
                    if t == 0 and k == 6:
                        pe.wait_ge(b_row, 2)
                    mm = pe.matmul(psum[:, k, t * P:(t + 1) * P], m.x[:, t, k * P:(k + 1) * P], scale[:, t, :],
                                   start=True, stop=True)
                    if t == QT - 1:
                        mm.then_inc(xT_mm, 1)
            pe.wait_ge(h_ok, KD)
            for k in range(KD):
                pe.wait_ge(wlo_ok, k + 1)
                for t in range(QT):
                    ts = slice(t * P, (t + 1) * P)
                    for b, (lo, hi) in enumerate(((0, S), (S, ROW_W))):
                        for n, (h, w) in enumerate(((h_hi, w_hi), (h_hi, w_lo), (h_lo, w_hi))):
                            mm = pe.matmul(psum[:, 2 * t + b, 0:hi - lo], h[:, k, ts], w[:, k % 2, lo:hi],
                                           start=(k == 0 and n == 0), stop=(k == KD - 1 and n == 2),
                                           skip_group_check=True)
                    if k == KD - 1 and t < QT - 1:
                        mm.then_inc(rows_mm, 1)
                mm.then_inc(tile_mm, 1)
            for j in range(N_COLS):
                i = C0 + j
                pe.wait_ge(wlo_ok, i + 1)
                pe.wait_ge(rows_a, j // 2 + 1)
                pe.wait_ge(rows_v, j // 2 + 1)
                hi = w_hi[:, i % 2, :].rearrange("p (k n) -> p k n", k=KD)
                lo = w_lo[:, i % 2, :].rearrange("p (k n) -> p k n", k=KD)
                product3(pe, psum[:, j, :], hi, lo, h_hi, h_lo).then_inc(tile_mm, 1)
            pe.wait_ge(lat_ok, QT)
            pe.wait_ge(cols_a, 2)
            pe.wait_ge(cols_v, 1)
            for c in range(3):
                for t in range(QT):
                    mm = pe.transpose(psum[:, c, t * P:(t + 1) * P], lat[:, t, c * P:(c + 1) * P], m.eye[:, :])
                mm.then_inc(latT_mm, 1)
            pe.wait_ge(up_in, 32)
            pe.wait_ge(latT_ok, 3)
            pe.wait_ge(cols_a, 4)
            pe.wait_ge(cols_v, 4)

            def up_copied(v):
                t, n = v // 4, v % 4
                if n < 2:
                    pe.wait_ge(upq_ok, 2 * t + n + 1)
                else:
                    pe.wait_ge(upk_ok, 2 * t + n - 1)

            for t in range(QT):
                for n in range(4):
                    v = 4 * t + n
                    if v >= UP_BANKS:
                        up_copied(v - UP_BANKS)
                    bank = psum[:, v % UP_BANKS, :]
                    if n < 2:
                        for c in range(2):
                            pe.matmul(bank[:, 0:4 * QK], m.latT[:, c, t * P:(t + 1) * P],
                                      m.wq_up[:, c, n * 4 * QK:(n + 1) * 4 * QK], start=(c == 0), stop=(c == 1))
                    else:
                        mm = pe.matmul(bank, m.latT[:, 2, t * P:(t + 1) * P],
                                       m.wkv_up[:, (n - 2) * 512:(n - 1) * 512], start=True, stop=True)
                mm.then_inc(up_mm, 1)
                for half in range(2):
                    i = H0 + 2 * t + half
                    c, h = t // 2, t % 2
                    pe.wait_ge(wlo_ok, i + 1)
                    pe.wait_ge(blo_ok, c + 1)
                    for n in range(KD):
                        l = half * KD + n
                        for o, (w, x) in enumerate(((w_hi, b_hi), (w_hi, b_lo), (w_lo, b_hi))):
                            mm = pe.matmul(psum[:, 6 + c, h * GROUPS * N_CMP:(h + 1) * GROUPS * N_CMP],
                                           w[:, i % 2, n * P:(n + 1) * P], x[:, c, l, :, :].rearrange("p g n -> p (g n)"),
                                           start=(l == 0 and o == 0), stop=(l == LP - 1 and o == 2))
                    mm.then_inc(tile_mm, 1)
            pe.wait_ge(upq_ok, 2 * QT)
            pe.wait_ge(upk_ok, 2 * QT)
            pe.wait_ge(k_rot, QT)

            def turn(u):
                if u >= UP_BANKS:
                    pe.wait_ge(qkT_a if u % 2 == 0 else qkT_v, (u - UP_BANKS) // 2 + 1)
                for t in range(QT):
                    mm = pe.transpose(psum[0:QK, u % UP_BANKS, t * P:(t + 1) * P],
                                      (kf if u < HEADS else qf)[:, t, u % HEADS, :], m.eye[:, :])
                mm.then_inc(qkT_mm, 1)

            for u in range(HEADS):
                turn(u)
            pe.wait_ge(w2_in, 16)
            pe.wait_ge(hid_ok, 2)
            for g in range(GROUPS):
                for h in range(HT):
                    mm = pe.matmul(psum[g * DH:(g + 1) * DH, 6, 0:N_CMP], w2[:, 0, h, :],
                                   hid[:, 0, h, g * N_CMP:(g + 1) * N_CMP], start=(h == 0), stop=(h == HT - 1))
            mm.then_inc(cmp_mm, 1)
            for g in range(GROUPS):
                for h in range(HT):
                    mm = pe.matmul(psum[0:N_CMP, 7, g * DH:(g + 1) * DH], hid[:, 1, h, g * N_CMP:(g + 1) * N_CMP],
                                   w2[:, 1, h, :], start=(h == 0), stop=(h == HT - 1))
            mm.then_inc(cmp_mm, 1)
            pe.wait_ge(q_rot, 2 * QT)
            for u in range(HEADS, 2 * HEADS):
                turn(u)


def attend(nc, io, m, psum):
    kinds = [(0, g) for g in range(GROUPS)]
    kinds += [(b, h) for h in range(HEADS) for b in (1, 2)]
    kinds += [(3, h) for h in range(HEADS)]
    pairs = [(i, QT - 1 - i) for i in range(QT // 2)]
    units = [(i, b, h) for pair in pairs for b, h in kinds for i in pair]
    n_units = len(units)
    RING = 4
    outs = [(i, c) for pair in pairs for c in range(2) for i in pair]
    finish = [max(u for u, (ui, b, _) in enumerate(units) if ui == i and (b == 3) == (c == 1)) for i, c in outs]
    with ExitStack() as ctx:
        sb = m.scratch().take

        def sem(name):
            return ctx.enter_context(nc.semaphore(name))

        sc = sb("sc", [P, RING, S])
        pr = sb("pr", [P, RING, S])
        prT = sb("prT", [P, RING, S])
        cprT = sb("cprT", [N_CMP, 2, GROUPS, S])
        top = sb("top", [P, n_units, 4])
        sums = sb("sums", [P, n_units, 4])
        fac = sb("fac", [P, n_units, 4])
        scale = sb("scale", [P, RING, P])
        og = sb("og", [P, 2, S])
        sq = sb("sq", [P, 2, S])
        sq2 = sb("sq2", [P, S // 2])

        s_mm, s_in, e_ok, c_step, d_ok = sem("s_mm"), sem("s_in"), sem("e_ok"), sem("c_step"), sem("d_ok")
        t_mm, t_v, t_a, v_mm = sem("t_mm"), sem("t_v"), sem("t_a"), sem("v_mm")
        og_ok, sq_ok, half_ok, ssq_ok, ohi_ok, olo_ok = (
            sem("og_ok"), sem("sq_ok"), sem("half_ok"), sem("ssq_ok"), sem("ohi_ok"), sem("olo_ok"))
        seen_ok = sem("seen_ok")
        block = ctx.enter_context(nc.Block())
        S_BANK, T_BANK, O_BANK = 0, 3, 5
        S_N, T_N, O_N = 3, 2, 3
        FACTOR, TURN, VALUES, DRAIN = 1, 2, 4, 5

        def valued(u):
            return sum(b != 0 for _, b, _ in units[:u + 1])

        def by_vector(u):
            return u % 4 in (0, 3)

        def copied(eng, u):
            n = sum(by_vector(v) == by_vector(u) for v in range(u + 1))
            eng.wait_ge(t_v if by_vector(u) else t_a, n)

        def copy_out(eng, u):
            i, b, g = units[u]
            eng.wait_ge(t_mm, u + 1)
            if b == 0:
                rows, w, dst = N_CMP, S, cprT[:, u % 2, g, :]
                if u >= n_units // 2:
                    eng.wait_ge(v_mm, valued(finish[1]))
            else:
                rows, w = P, (i + 1) * P
                dst = prT[:, u % RING, 0:w]
                if u >= RING and units[u - RING][1]:
                    eng.wait_ge(v_mm, valued(u - RING))
            src = psum[0:rows, T_BANK + u % T_N, 0:w]
            if by_vector(u):
                nc.vector.tensor_copy(dst, src).then_inc(t_v, 1)
            else:
                nc.scalar.activation(dst, src, ACT.Copy).then_inc(t_a, 1)

        @block.sync
        def _(sp):
            sp.dma_start(m.gain[:, 0, :], io.grp_gain).then_inc(m.gain_in, 16)
            sp.dma_start(m.gain[:, 1, :], io.g2).then_inc(m.gain_in, 16)
            for k in range(2):
                sp.dma_start(m.wo_raw[:, k, :], io.w_out[:, k, :]).then_inc(m.wo_in[k], 16)

        @block.tensor
        def _(pe):
            def scores(u):
                i, b, h = units[u]
                if u >= S_N:
                    pe.wait_ge(s_in, u - S_N + 1)
                bank, q = psum[:, S_BANK + u % S_N, :], slice(i * P, (i + 1) * P)
                if b == 0:
                    r = slice(h * DH, (h + 1) * DH)
                    for n in range(4):
                        mm = pe.matmul(bank[:, n * N_CMP:(n + 1) * N_CMP], m.qT[r, n, q], m.kcT[r, :],
                                       start=True, stop=True)
                elif b < 3:
                    r = slice(h // 4 * DH, (h // 4 + 1) * DH)
                    mm = pe.matmul(bank[:, 0:(i + 1) * P], m.qT[r, h % 4, q], m.kT[r, b - 1, 0:(i + 1) * P],
                                   start=True, stop=True)
                else:
                    mm = pe.matmul(bank[:, 0:(i + 1) * P], m.qmT[:, h, q], m.kmT[:, h, 0:(i + 1) * P],
                                   start=True, stop=True)
                mm.then_inc(s_mm, 1)

            def turn(u):
                i, b, _ = units[u]
                pe.wait_ge(d_ok, u + 1)
                if u >= T_N:
                    copied(pe, u - T_N)
                for n in range(4 if b == 0 else i + 1):
                    if b == 0:
                        mm = pe.transpose(psum[0:N_CMP, T_BANK + u % T_N, n * P:(n + 1) * P],
                                          pr[:, u % RING, n * N_CMP:(n + 1) * N_CMP], m.eye[:, :])
                    else:
                        mm = pe.matmul(psum[:, T_BANK + u % T_N, n * P:(n + 1) * P],
                                       pr[:, u % RING, n * P:(n + 1) * P], scale[:, u % RING, :], start=True, stop=True)
                mm.then_inc(t_mm, 1)

            def values(u):
                i, b, h = units[u]
                copied(pe, u)
                if b == 0:
                    return
                o = outs.index((i, int(b == 3)))
                if o >= O_N:
                    pe.wait_ge(og_ok, o - O_N + 1)
                    pe.wait_ge(sq_ok, o - O_N + 1)
                out = psum[h % 2 * DH:(h % 2 + 1) * DH, O_BANK + o % O_N, h // 2 * P:(h // 2 + 1) * P]
                if b == 1:
                    g = h // 4
                    pe.matmul(out, m.vc[:, g * DH:(g + 1) * DH], cprT[:, u % 2, g, h % 4 * P:(h % 4 + 1) * P],
                              start=True, stop=False)
                for n in range(i + 1):
                    if b < 3:
                        lo = (R_VS, R_VW)[b - 1] + h // 4 * DH
                        v = m.rows[:, n, lo:lo + DH]
                    else:
                        v = m.vm[:, n, h * DH:(h + 1) * DH]
                    mm = pe.matmul(out, v, prT[:, u % RING, n * P:(n + 1) * P],
                                   start=(b == 3 and n == 0), stop=(b != 1 and n == i))
                mm.then_inc(v_mm, 1)

            for s in range(n_units + VALUES):
                if s < n_units:
                    scores(s)
                if TURN <= s < n_units + TURN:
                    turn(s - TURN)
                if s >= VALUES:
                    values(s - VALUES)

        @block.scalar
        def _(act):
            for s in range(n_units + DRAIN + 1):
                if s < n_units:
                    i, b, h = units[s]
                    act.wait_ge(s_in, s + 1)
                    if s >= RING:
                        act.wait_ge(t_mm, s - RING + 1)
                    if b == 0:
                        act.activation(pr[:, s % RING, 0:4 * N_CMP], sc[:, s % RING, 0:4 * N_CMP], ACT.Exp).then_inc(e_ok, 1)
                    else:
                        w = (i + 1) * P
                        act.activation(pr[:, s % RING, 0:w], sc[:, s % RING, 0:w], ACT.Exp, bias=top[:, s, 0:1], scale=-1.0,
                                       accum_out=sums[:, s, 0:1]).then_inc(e_ok, 1)
                if TURN <= s < n_units + TURN and not by_vector(s - TURN):
                    copy_out(act, s - TURN)
                if s > DRAIN and s - DRAIN - 1 in finish:
                    o = finish.index(s - DRAIN - 1)
                    i, c = outs[o]
                    act.wait_ge(og_ok, o + 1)
                    if o >= 2:
                        act.wait_ge(half_ok, o - 1)
                    act.activation(sq[:, o % 2, :], psum[:, O_BANK + o % O_N, :], ACT.Square).then_inc(sq_ok, 1)
                    act.activation(m.o_hi[:, 4 * c:4 * c + 4, i * P:(i + 1) * P],
                                   og[:, o % 2, :].rearrange("p (k n) -> p k n", k=4), ACT.Copy).then_inc(ohi_ok, 1)

        @block.gpsimd
        def _(pool):
            for o, (i, c) in enumerate(outs):
                pool.wait_ge(sq_ok, o + 1)
                if o:
                    pool.wait_ge(ssq_ok, o)
                pool.tensor_tensor(sq2[:, :], sq[:, o % 2, 0:S // 2], sq[:, o % 2, S // 2:S], ALU.add).then_inc(half_ok, 1)
                pool.wait_ge(half_ok, o + 1)
                pool.tensor_tensor(m.ssq[:, c, i * P:(i + 1) * P], sq2[:, 0:P], sq2[:, P:2 * P], ALU.add).then_inc(ssq_ok, 1)
                pool.wait_ge(ohi_ok, o + 1)
                pool.tensor_tensor(m.o_lo[:, 4 * c:4 * c + 4, i * P:(i + 1) * P],
                                   og[:, o % 2, :].rearrange("p (k n) -> p k n", k=4),
                                   m.o_hi[:, 4 * c:4 * c + 4, i * P:(i + 1) * P].bitcast(F32), ALU.subtract
                                   ).then_inc(olo_ok, 1)

        @block.vector
        def _(dve):
            chain = [0]

            def link(ins):
                chain[0] += 1
                ins.then_inc(c_step, 1)
                dve.wait_ge(c_step, chain[0])

            def factor(u):
                i, b, h = units[u]
                dve.wait_ge(e_ok, u + 1)
                gate = m.gate[:, i, :].rearrange("p (h b) -> p b h", b=3)
                if b == 0:
                    p = pr[:, u % RING, 0:4 * N_CMP].rearrange("p (h n) -> p h n", h=4)
                    link(dve.tensor_reduce(sums[:, u, :], p, X, ALU.add))
                    link(dve.reciprocal(fac[:, u, :], sums[:, u, :]))
                    link(dve.tensor_tensor(fac[:, u, :], fac[:, u, :], gate[:, 0, 4 * h:4 * h + 4], ALU.mult))
                    dve.tensor_tensor(p, p, fac[:, u, :].unsqueeze(2).to_broadcast([P, 4, N_CMP]), ALU.mult
                                      ).then_inc(d_ok, 1)
                    return
                link(dve.reciprocal(fac[:, u, 0:1], sums[:, u, 0:1]))
                if u >= RING:
                    dve.wait_ge(t_mm, u - RING + 1)
                dve.tensor_scalar(scale[:, u % RING, :], m.eye[:, :], fac[:, u, 0:1],
                                  gate[:, b, h:h + 1] if b < 3 else None, ALU.mult, *([ALU.mult] if b < 3 else [])
                                  ).then_inc(d_ok, 1)

            gate0 = m.gate[:, 0, :].rearrange("p (h b) -> p b h", b=3)[:, 0, :]
            dve.tensor_scalar(gate0, gate0, m.seen[:, 0:1], None, ALU.mult).then_inc(seen_ok, 1)
            dve.wait_ge(seen_ok, 1)
            for s in range(n_units + DRAIN + 1):
                if s < n_units:
                    i, b, h = units[s]
                    dve.wait_ge(s_mm, s + 1)
                    if s >= RING:
                        dve.wait_ge(e_ok, s - RING + 1)
                    bank, w = psum[:, S_BANK + s % S_N, :], (i + 1) * P
                    j0 = S - w
                    if b == 0:
                        out = sc[:, s % RING, 0:4 * N_CMP].rearrange("p (h n) -> p h n", h=4)
                        c0 = S - P + CMP_LEN - 1 - i * P
                        bias = m.bias[:, 4 * h:4 * h + 4, c0:c0 + (N_CMP - 1) * CMP_STRIDE + 1:CMP_STRIDE]
                        link(dve.tensor_tensor(out, bank[:, 0:4 * N_CMP].rearrange("p (h n) -> p h n", h=4), bias,
                                               ALU.add))
                        link(dve.tensor_reduce(top[:, s, :], out, X, ALU.max))
                        dve.tensor_tensor(out, out, top[:, s, :].unsqueeze(2).to_broadcast([P, 4, N_CMP]),
                                          ALU.subtract).then_inc(s_in, 1)
                    elif b < 3:
                        dve.tensor_tensor_reduce(sc[:, s % RING, 0:w], bank[:, 0:w], m.bias[:, h, j0:S], -1.0, 3.0e38,
                                                 ALU.add, ALU.min, top[:, s, 0:1]).then_inc(s_in, 1)
                    else:
                        dve.tensor_tensor_reduce(sc[:, s % RING, 0:w], bank[:, 0:w], m.mask[:, j0:S], -MLA_SCALE, 3.0e38,
                                                 ALU.add, ALU.min, top[:, s, 0:1]).then_inc(s_in, 1)
                if FACTOR <= s < n_units + FACTOR:
                    factor(s - FACTOR)
                if TURN <= s < n_units + TURN and by_vector(s - TURN):
                    copy_out(dve, s - TURN)
                if s >= DRAIN and s - DRAIN in finish:
                    o = finish.index(s - DRAIN)
                    i, c = outs[o]
                    dve.wait_ge(v_mm, valued(s - DRAIN))
                    if o == 0:
                        dve.wait_ge(m.gain_in, 32)
                    if o >= 2:
                        dve.wait_ge(olo_ok, o - 1)
                    dve.tensor_tensor(og[:, o % 2, :].rearrange("p (k n) -> p k n", k=4),
                                      psum[:, O_BANK + o % O_N, :].rearrange("p (k n) -> p k n", k=4),
                                      m.gain[:, 0, 4 * c:4 * c + 4].unsqueeze(2).to_broadcast([P, 4, P]), ALU.mult
                                      ).then_inc(og_ok, 1)


def output(nc, io, m, psum):
    with ExitStack() as ctx:
        sb = m.scratch().take

        def sem(name):
            return ctx.enter_context(nc.semaphore(name))

        w_hi = sb("wo_hi", [P, KD, D], F32R)
        w_lo = sb("wo_lo", [P, KD, D], F32R)
        ones = sb("ones", [P, 1])
        stat = sb("ostat", [P, 4, 2 * QT])
        stat2 = sb("ostat2", [P, 4, QT])
        scale = sb("oscale", [P, QT, P])
        junk = sb("ojunk", [P, D])

        wh_ok, wl_ok = sem("wh_ok"), sem("wl_ok")
        ones_ok, g_mm, g_var, g_std, g_rs = sem("o_ones"), sem("g_mm"), sem("g_var"), sem("g_std"), sem("g_rs")
        y_mm, y_ok, x2_out = sem("y_mm"), sem("y_ok"), sem("x2_out")
        y_sq, y_var, y_std, y_rs, y_dg, yT_mm, hi_ok, lo_ok = (
            sem("y_sq"), sem("y_var"), sem("y_std"), sem("y_rs"), sem("y_dg"), sem("yT_mm"), sem("hi_ok"), sem("lo_ok"))
        block = ctx.enter_context(nc.Block())
        banks = [(t, b) for t in range(QT) for b in range(2)]

        @block.sync
        def _(sp):
            for k in range(2, KD):
                sp.wait_ge(wl_ok, k - 1)
                sp.dma_start(m.wo_raw[:, k % 2, :], io.w_out[:, k, :]).then_inc(m.wo_in[k % 2], 16)
            for c in range(2):
                sp.dma_start(m.wq_raw[:, c], io.wq[c]).then_inc(m.wq_in[c], 16)
            sp.dma_start(m.keys[:, :, :], io.keysT).then_inc(m.keys_in, 16)
            for t in range(QT):
                sp.wait_ge(y_ok, 2 * QT + 2 * t + 2)
                sp.dma_start(io.x2.rearrange("(t p) d -> t p d", p=P)[t], m.x[:, t, :]).then_inc(x2_out, 16)
            sp.wait_ge(x2_out, 16 * QT)

        @block.gpsimd
        def _(pool):
            pool.memset(ones[:, :], 1.0).then_inc(ones_ok, 1)

        @block.scalar
        def _(act):
            def split(k):
                act.wait_ge(m.wo_in[k % 2], 16 * (k // 2 + 1))
                act.activation(w_hi[:, k, :], m.wo_raw[:, k % 2, :], ACT.Copy).then_inc(wh_ok, 1)

            split(0)
            split(1)
            act.wait_ge(g_var, 1)
            act.activation(stat[:, 2, :], stat[:, 1, :], ACT.Sqrt).then_inc(g_std, 1)
            for k in range(2, KD):
                split(k)
            for t in range(QT):
                act.wait_ge(y_ok, 2 * QT + 2 * t + 2)
                if t:
                    act.wait_ge(y_sq, t)
                act.activation(junk[:, :], m.x[:, t, :], ACT.Square, accum_out=stat2[:, 0, t:t + 1]).then_inc(y_sq, 1)
                act.wait_ge(y_var, t + 1)
                act.activation(stat2[:, 2, t:t + 1], stat2[:, 1, t:t + 1], ACT.Sqrt).then_inc(y_std, 1)
            for k in range(KD):
                act.wait_ge(yT_mm, k + 1)
                act.activation(m.h_hi[:, k, :], psum[:, k, :], ACT.Copy, scale=m.gain[:, 1, k:k + 1]).then_inc(hi_ok, 1)

        @block.vector
        def _(dve):
            def split(k):
                dve.wait_ge(wh_ok, k + 1)
                dve.tensor_tensor(w_lo[:, k, :], m.wo_raw[:, k % 2, :], w_hi[:, k, :].bitcast(F32), ALU.subtract
                                  ).then_inc(wl_ok, 1)

            split(0)
            dve.wait_ge(g_mm, 1)
            dve.tensor_scalar(stat[:, 1, :], psum[:, 7, 0:2 * QT], 1.0 / NSA_W, EPS, ALU.mult, ALU.add).then_inc(g_var, 1)
            split(1)
            dve.wait_ge(g_std, 1)
            dve.reciprocal(stat[:, 3, :], stat[:, 2, :]).then_inc(g_rs, 1)
            for k in range(2, KD):
                split(k)
            dve.wait_ge(g_rs, 1)
            for c in range(2):
                for j, (t, b) in enumerate(banks):
                    dve.wait_ge(y_mm, 2 * QT * c + j + 1)
                    if c:
                        dve.wait_ge(y_ok, j + 1)
                    xs = m.x[:, t, b * S:(b + 1) * S]
                    dve.scalar_tensor_tensor(out=xs, in0=psum[:, j, :], scalar=stat[:, 3, 2 * t + c:2 * t + c + 1],
                                             in1=xs, op0=ALU.mult, op1=ALU.add).then_inc(y_ok, 1)
                    if c and b:
                        dve.wait_ge(y_sq, t + 1)
                        dve.tensor_scalar(stat2[:, 1, t:t + 1], stat2[:, 0, t:t + 1], 1.0 / D, EPS, ALU.mult, ALU.add
                                          ).then_inc(y_var, 1)
                        dve.wait_ge(y_std, t + 1)
                        dve.reciprocal(stat2[:, 3, t:t + 1], stat2[:, 2, t:t + 1]).then_inc(y_rs, 1)
                        dve.wait_ge(y_rs, t + 1)
                        dve.tensor_scalar(scale[:, t, :], m.eye[:, :], stat2[:, 3, t:t + 1], None, ALU.mult
                                          ).then_inc(y_dg, 1)
            for k in range(KD):
                dve.wait_ge(hi_ok, k + 1)
                dve.scalar_tensor_tensor(out=m.h_lo[:, k, :], in0=psum[:, k, :], scalar=m.gain[:, 1, k:k + 1],
                                         in1=m.h_hi[:, k, :].bitcast(F32), op0=ALU.mult, op1=ALU.subtract
                                         ).then_inc(lo_ok, 1)

        @block.tensor
        def _(pe):
            def product(j, k, start, stop):
                t, b = banks[j]
                ts, bs = slice(t * P, (t + 1) * P), slice(b * S, (b + 1) * S)
                for n, (o, w) in enumerate(((m.o_hi, w_hi), (m.o_hi, w_lo), (m.o_lo, w_hi))):
                    mm = pe.matmul(psum[:, j, :], o[:, k, ts], w[:, k, bs],
                                   start=(start and n == 0), stop=(stop and n == 2), skip_group_check=True)
                return mm

            pe.wait_ge(ones_ok, 1)
            for t in range(QT):
                for c in range(2):
                    mm = pe.matmul(psum[:, 7, 2 * t + c:2 * t + c + 1], m.ssq[:, c, t * P:(t + 1) * P], ones[:, :],
                                   start=True, stop=True)
            mm.then_inc(g_mm, 1)
            for k in range(4):
                pe.wait_ge(wl_ok, k + 1)
                for j in range(len(banks)):
                    if k == 0 and j == 7:
                        pe.wait_ge(g_var, 1)
                    mm = product(j, k, k == 0, k == 3)
                    if k == 3:
                        mm.then_inc(y_mm, 1)
            pe.wait_ge(wl_ok, KD)
            for j in range(len(banks)):
                pe.wait_ge(y_ok, j + 1)
                for k in range(4, KD):
                    mm = product(j, k, k == 4, k == KD - 1)
                mm.then_inc(y_mm, 1)
            pe.wait_ge(y_ok, 4 * QT)
            for t in range(QT):
                pe.wait_ge(y_dg, t + 1)
                for k in range(KD):
                    mm = pe.matmul(psum[:, k, t * P:(t + 1) * P], m.x[:, t, k * P:(k + 1) * P], scale[:, t, :],
                                   start=True, stop=True)
                    if t == QT - 1:
                        mm.then_inc(yT_mm, 1)


def peer_scores(nc, io, m, psum):
    with ExitStack() as ctx:
        sb = m.scratch().take

        def sem(name):
            return ctx.enter_context(nc.semaphore(name))

        raw, keys = m.wq_raw, m.keys
        hi = sb("wq_hi", [P, 2, KD, P], F32R)
        lo = sb("wq_lo", [P, 2, KD, P], F32R)
        qp = sb("qp", [P, 2, S])
        keys_in, raw_in = m.keys_in, m.wq_in
        hi_ok, lo_ok, q_mm, q_ok, s_mm, s_ok = (
            sem("wqhi_ok"), sem("wqlo_ok"), sem("pq_mm"), sem("pq_ok"), sem("ps_mm"), sem("ps_ok"))
        block = ctx.enter_context(nc.Block())
        rounds = PH

        @block.sync
        def _(sp):
            for c in range(2):
                sp.dma_start(m.u_raw[:, c], io.uT[c]).then_inc(m.u_in[c], 16)
            with sp.Fori(1, rounds) as h:
                for c in range(2):
                    sp.wait_ge(lo_ok, 2 * h - 1 + c)
                    sp.dma_start(raw[:, c], io.wq[bass.ds(2 * h + c, 1)].rearrange("o p k n -> p (o k) n")
                                 ).then_inc(raw_in[c], 16)

        @block.scalar
        def _(act):
            def split(h, c):
                act.wait_ge(raw_in[c], 16 * h + 16)
                act.activation(hi[:, c].rearrange("p k n -> p (k n)"), raw[:, c].rearrange("p k n -> p (k n)"),
                               ACT.Copy).then_inc(hi_ok, 1)

            split(0, 0)
            split(0, 1)

            def queries(h, c):
                act.wait_ge(q_mm, 2 * h + 1 + c)
                act.activation(qp[:, c, :], psum[:, c, :], ACT.Copy).then_inc(q_ok, 1)

            with act.Fori(1, rounds) as h:
                for c in range(2):
                    queries(h - 1, c)
                    split(h, c)
            for c in range(2):
                queries(rounds - 1, c)

        @block.vector
        def _(dve):
            def split(h, c):
                dve.wait_ge(hi_ok, 2 * h + 1 + c)
                dve.tensor_tensor(lo[:, c].rearrange("p k n -> p (k n)"), raw[:, c].rearrange("p k n -> p (k n)"),
                                  hi[:, c].rearrange("p k n -> p (k n)").bitcast(F32), ALU.subtract).then_inc(lo_ok, 1)

            def scores(h, c):
                dve.wait_ge(s_mm, 2 * h + 1 + c)
                for t in range(QT):
                    ins = dve.tensor_copy(m.ps[:, bass.ds(t * 2 * PH + 2 * h + c, 1), :].rearrange("p a n -> p (a n)"),
                                          psum[:, 2 + c, t * P:(t + 1) * P])
                ins.then_inc(s_ok, 1)

            split(0, 0)
            split(0, 1)
            with dve.Fori(1, rounds) as h:
                for c in range(2):
                    split(h, c)
                for c in range(2):
                    scores(h - 1, c)
            for c in range(2):
                scores(rounds - 1, c)

        @block.tensor
        def _(pe):
            def turn(h, first):
                for c in range(2):
                    pe.wait_ge(lo_ok, 2 * h + 1 + c)
                    if not first:
                        pe.wait_ge(q_ok, 2 * h - 1 + c)
                    product3(pe, psum[:, c, :], hi[:, c], lo[:, c], m.h_hi, m.h_lo).then_inc(q_mm, 1)
                for c in range(2):
                    pe.wait_ge(q_ok, 2 * h + 1 + c)
                    if not first:
                        pe.wait_ge(s_ok, 2 * h - 1 + c)
                    for t in range(QT):
                        mm = pe.matmul(psum[:, 2 + c, t * P:(t + 1) * P], qp[:, c, t * P:(t + 1) * P], keys[:, c, :],
                                       start=True, stop=True)
                    mm.then_inc(s_mm, 1)

            pe.wait_ge(keys_in, 16)
            turn(0, True)
            with pe.Fori(1, rounds) as h:
                turn(h, False)


N_TILES = NKEYS
ROUNDS = N_TILES // 2
R_ROUNDS = QT * PH
TOK = S // (ROUNDS - R_ROUNDS)
QUAD = 4
CHUNK = P
C_ROUNDS = CHUNK // TOK
STORED = S - CHUNK


def experts(nc, io, m, psum):
    with ExitStack() as ctx:
        sb = m.scratch().take

        def sem(name):
            return ctx.enter_context(nc.semaphore(name))

        raw = m.u_raw
        hi = sb("u_hi", [P, 2, KD, P], F32R)
        lo = sb("u_lo", [P, 2, KD, P], F32R)
        act_out = sb("act_out", [P, 2, S])
        routed = m.routed
        raw_in = m.u_in
        hi_ok, a_mm, a_ok = sem("uhi_ok"), sem("a_mm"), sem("a_ok")
        lo_ok = [sem("ulo_ok0"), sem("ulo_ok1")]
        a_out, w_out = m.a_out, m.w_out
        r_step, routed_ok, g_exp, g_norm, slot_mm, slot_ok = (
            sem("r_step"), sem("routed_ok"), sem("g_exp"), sem("g_norm"), sem("slot_mm"), sem("slot_ok"))
        hot_ok, is1_ok, w_mm, w_ok = sem("hot_ok"), sem("is1_ok"), sem("w_mm"), sem("w_ok")
        iota_ok, w_ahead = sem("iota_ok"), sem("w_ahead")
        block = ctx.enter_context(nc.Block())

        def load(sp, r, c):
            sp.wait_ge(lo_ok[c], r)
            sp.dma_start(raw[:, c], io.uT[bass.ds(2 * r + c, 1)].rearrange("o p k n -> p (o k) n")
                         ).then_inc(raw_in[c], 16)

        def store(sp, r, c):
            sp.wait_ge(a_ok, 2 * r + 1 + c)
            sp.dma_start(io.acts[bass.ds(2 * r + c, 1)].rearrange("o p n -> p (o n)"), act_out[:, c, :]
                         ).then_inc(a_out[c], 16)

        def split(eng, r, c):
            eng.wait_ge(hi_ok, 2 * r + 1 + c)
            eng.tensor_tensor(lo[:, c].rearrange("p k n -> p (k n)"), raw[:, c].rearrange("p k n -> p (k n)"),
                              hi[:, c].rearrange("p k n -> p (k n)").bitcast(F32), ALU.subtract).then_inc(lo_ok[c], 1)

        @block.sync
        def _(sp):
            def turn(r, last=False):
                if not last:
                    for c in range(2):
                        load(sp, r + 1, c)
                for c in range(2):
                    store(sp, r, c)

            slice_keys = NKEYS // C_ROUNDS

            def store_gates(ch, k, signal):
                cols = slice(ch * CHUNK, (ch + 1) * CHUNK)
                sp.dma_start(io.gates[bass.ds(k, slice_keys), :, cols].rearrange("a b t -> b a t"),
                             m.dense[:, ch % 2, bass.ds(k, slice_keys), :]).then_inc(signal, 16)

            with sp.Fori(0, R_ROUNDS) as r:
                turn(r)
            for ch in range(QT):
                first = R_ROUNDS + ch * C_ROUNDS
                start = first
                if ch:
                    sp.wait_ge(w_ok, ch * CHUNK // QUAD)
                if ch == QT - 1:
                    for k in range(2):
                        turn(first + k)
                        store_gates(ch - 1, k * slice_keys, w_ahead)
                    turn(first + 2)
                    store_gates(ch - 1, 2 * slice_keys, w_out[(ch - 1) % 2])
                    sp.wait_ge(w_ahead, 32)
                    for c in range(2):
                        sp.dma_start(m.v_raw[:, c, :], io.v[c]).then_inc(m.v_in[c], 16)
                    start = first + 3
                with sp.Fori(start, first + C_ROUNDS - (ch == QT - 1)) as r:
                    turn(r)
                    if ch:
                        store_gates(ch - 1, (r - first) * slice_keys, w_out[(ch - 1) % 2])
            turn(ROUNDS - 1, last=True)
            store_gates(QT - 2, NKEYS - slice_keys, w_out[(QT - 2) % 2])

        @block.gpsimd
        def _(pool):
            pool.iota(m.iota[:, :], pattern=[[1, P]], base=0, channel_multiplier=0,
                      allow_small_or_imprecise_dtypes=True).then_inc(iota_ok, 1)
            pool.iota(m.iota4[:, :, :], pattern=[[1, P], [0, QUAD]], base=0, channel_multiplier=0,
                      allow_small_or_imprecise_dtypes=True).then_inc(iota_ok, 1)
            ahead = ROUNDS - C_ROUNDS // 2
            with pool.Fori(0, ahead) as r:
                split(pool, r, 1)
            pool.wait_ge(w_ahead, 32)
            pool.wait_ge(w_out[1], 16 * C_ROUNDS)
            for c in range(2):
                pool.wait_ge(a_out[c], 16)
                pool.dma_start(m.acts_in[:, c, :], io.acts[c]).then_inc(m.ag_in[c], 16)
                pool.dma_start(m.gates_in[:, c, :], io.gates[c, :, 0:STORED]).then_inc(m.ag_in[c], 16)
            with pool.Fori(ahead, ROUNDS) as r:
                split(pool, r, 1)

        @block.scalar
        def _(act):
            def split(r, c):
                act.wait_ge(raw_in[c], 16 * r + 16)
                act.activation(hi[:, c].rearrange("p k n -> p (k n)"), raw[:, c].rearrange("p k n -> p (k n)"),
                               ACT.Copy).then_inc(hi_ok, 1)

            def gelu(r, c, first=False):
                act.wait_ge(a_mm, 2 * r + 1 + c)
                if not first:
                    act.wait_ge(a_out[c], 16 * r)
                act.activation(act_out[:, c, :], psum[:, c, :], ACT.Gelu).then_inc(a_ok, 1)

            split(0, 0)
            split(0, 1)
            for c in range(2):
                gelu(0, c, True)
                split(1, c)
            with act.Fori(1, R_ROUNDS) as r:
                for c in range(2):
                    gelu(r, c)
                    split(r + 1, c)
            act.wait_ge(routed_ok, R_ROUNDS)
            act.activation(routed[:, 2], routed[:, 2], ACT.Exp).then_inc(g_exp, 1)

            def turn(r, r0, ch, last=False, between=False):
                if between:
                    for c in range(2):
                        gelu(r, c)
                        split(r + 1, c)
                for c in range(2):
                    if not between:
                        gelu(r, c)
                        if not last:
                            split(r + 1, c)
                    for b in range(2):
                        n = 2 * c + b
                        q = (r - R_ROUNDS) * (TOK // QUAD) + n
                        act.wait_ge(w_mm, q + 1)
                        off = (r - r0) * TOK + n * QUAD
                        act.activation(m.dense[:, ch % 2, :, bass.ds(off, QUAD)].rearrange("p a t -> p t a"),
                                       psum[:, 2 + n % 2, :].rearrange("p (t a) -> p t a", t=QUAD),
                                       ACT.Copy).then_inc(w_ok, 1)

            for ch in range(QT):
                r0 = R_ROUNDS + ch * C_ROUNDS
                if ch >= 2:
                    act.wait_ge(w_out[ch % 2], 16 * C_ROUNDS)
                if ch == 0:
                    turn(r0, r0, ch, between=True)
                with act.Fori(r0 + (ch == 0), r0 + C_ROUNDS - (ch == QT - 1)) as r:
                    turn(r, r0, ch)
                if ch == QT - 1:
                    turn(ROUNDS - 1, r0, ch, last=True)

        @block.vector
        def _(dve):
            STEPS = 14
            low = -3.0e38

            def route(r):
                n = [0]

                def link(ins, before_max=False):
                    n[0] += 1
                    ins.then_inc(r_step, 1)
                    dve.wait_ge(r_step, r * STEPS + n[0])
                    if before_max:
                        dve.memset(m.pause[:, :], 0.0)

                link(dve.tensor_copy(m.cur[:, :, :], m.ps[:, bass.ds(2 * r, 2), :]), True)
                dve.max(m.best[:, 0, 0:8], m.cur[:, 0, :])
                link(dve.max(m.best[:, 1, 0:8], m.cur[:, 1, :]), True)
                for c in range(2):
                    dve.max_index(m.where[:, c, 0:8], m.best[:, c, 0:8], m.cur[:, c, :])
                    ins = dve.match_replace(m.cur2[:, c, :], m.best[:, c, 0:8], m.cur[:, c, :], low)
                link(ins, True)
                dve.max(m.best[:, 0, 8:16], m.cur2[:, 0, :])
                link(dve.max(m.best[:, 1, 8:16], m.cur2[:, 1, :]), True)
                for c in range(2):
                    dve.max_index(m.where[:, c, 8:16], m.best[:, c, 8:16], m.cur2[:, c, :])
                link(dve.tensor_tensor(m.cand[:, :].rearrange("p (a b) -> p a b", a=TOPK),
                                       m.best[:, 0, :].unsqueeze(2).to_broadcast([P, TOPK, TOPK]),
                                       m.best[:, 1, :].unsqueeze(1).to_broadcast([P, TOPK, TOPK]), ALU.add))
                dve.tensor_copy(m.wheref[:, :, :], m.where[:, :, :])
                split(dve, r + 1, 0)
                link(dve.max(m.ctop[:, 0:8], m.cand[:, :]), True)
                dve.max_index(m.cpos[:, 0:8], m.ctop[:, 0:8], m.cand[:, :])
                link(dve.match_replace(m.cand2[:, :], m.ctop[:, 0:8], m.cand[:, :], low), True)
                link(dve.max(m.ctop[:, 8:16], m.cand2[:, :]), True)
                link(dve.max_index(m.cpos[:, 8:16], m.ctop[:, 8:16], m.cand2[:, :]))
                dve.tensor_scalar(m.rc[:, 0, :], m.cpos[:, :], 4, None, ALU.logical_shift_right)
                link(dve.tensor_scalar(m.rc[:, 1, :], m.cpos[:, :], 15, None, ALU.bitwise_and))
                link(dve.tensor_copy(m.rcf[:, :, :], m.rc[:, :, :]))
                for c in range(2):
                    ins = dve.tensor_tensor(m.pick[:, c], m.rcf[:, c, :].unsqueeze(2).to_broadcast([P, TOPK, TOPK]),
                                            m.iota[:, 0:TOPK].unsqueeze(1).to_broadcast([P, TOPK, TOPK]), ALU.is_equal)
                link(ins)
                for c in range(2):
                    ins = dve.tensor_tensor(m.pick[:, c], m.pick[:, c],
                                            m.wheref[:, c, :].unsqueeze(1).to_broadcast([P, TOPK, TOPK]), ALU.mult)
                link(ins)
                for c in range(2):
                    dve.tensor_reduce(routed[:, c, bass.ds(r * TOPK, TOPK)], m.pick[:, c], X, ALU.add)
                dve.tensor_scalar(routed[:, 2, bass.ds(r * TOPK, TOPK)], m.ctop[:, :], m.ctop[:, 0:1], None,
                                  ALU.subtract).then_inc(routed_ok, 1)
                link(dve.tensor_copy(m.cur2[:, 0, 0:1], m.ctop[:, 0:1]))
                return n[0]

            dve.wait_ge(iota_ok, 2)
            split(dve, 0, 0)
            with dve.Fori(0, R_ROUNDS) as r:
                steps = route(r)
            assert steps == STEPS, steps
            dve.wait_ge(g_exp, 1)
            dve.tensor_reduce(m.gsum[:, 0, :], routed[:, 2].rearrange("p (u k) -> p u k", k=TOPK), X, ALU.add
                              ).then_inc(g_norm, 1)
            dve.wait_ge(g_norm, 1)
            dve.reciprocal(m.gsum[:, 1, :], m.gsum[:, 0, :]).then_inc(g_norm, 1)
            dve.wait_ge(g_norm, 2)
            g3 = routed[:, 2].rearrange("p (u k) -> p u k", k=TOPK)
            dve.tensor_tensor(g3, g3, m.gsum[:, 1, :].unsqueeze(2).to_broadcast([P, QT * PH, TOPK]), ALU.mult
                              ).then_inc(g_norm, 1)
            for n in range(3):
                dve.wait_ge(slot_mm, n + 1)
                dve.tensor_copy((m.slot_key[:, 0], m.slot_key[:, 1], m.slot_gate[:, 0])[n], psum[:, 4 + n, :]
                                ).then_inc(slot_ok, 1)
            n_slot = 3
            src = psum[:, 6, :]
            for n in range(1, 3):
                dve.wait_ge(slot_ok, n_slot)
                dve.tensor_tensor(m.slot_rest[:, :], src, m.slot_gate[:, n - 1], ALU.subtract).then_inc(slot_ok, 1)
                dve.wait_ge(slot_ok, n_slot + 1)
                dve.tensor_copy(m.slot_gate[:, n], m.slot_rest[:, :]).then_inc(slot_ok, 1)
                n_slot += 2
                src = m.slot_rest[:, :]
            dve.wait_ge(slot_ok, n_slot)

            def hots(r, n, first=False):
                q = (r - R_ROUNDS) * (TOK // QUAD) + n
                if not first:
                    dve.wait_ge(w_mm, q - 1)

                def row(x):
                    return x[:, bass.ds(q * QUAD, QUAD)].unsqueeze(1).to_broadcast([P, NKEYS, QUAD])

                dve.tensor_tensor(m.is1[:, n % 2], m.iota4[:, :, :], row(m.slot_key[:, 0]), ALU.is_equal
                                  ).then_inc(is1_ok, 1)
                dve.tensor_tensor(m.hot2[:, n % 2], m.iota4[:, :, :], row(m.slot_key[:, 1]), ALU.is_equal)
                dve.wait_ge(is1_ok, q + 1)
                for g in range(3):
                    ins = dve.tensor_tensor(m.hot1[:, n % 2, g], m.is1[:, n % 2], row(m.slot_gate[:, g]), ALU.mult)
                ins.then_inc(hot_ok, 1)

            def turn(r, first=False, last=False):
                for n in range(TOK // QUAD):
                    if not last and n == 2:
                        split(dve, r + 1, 0)
                    hots(r, n, first and n < 2)
    
            turn(R_ROUNDS, first=True)
            with dve.Fori(R_ROUNDS + 1, ROUNDS - 1) as r:
                turn(r)
            turn(ROUNDS - 1, last=True)

        @block.tensor
        def _(pe):
            def tile(r, c, first=False):
                pe.wait_ge(lo_ok[c], r + 1)
                if not first:
                    pe.wait_ge(a_ok, 2 * r - 1 + c)
                product3(pe, psum[:, c, :], hi[:, c], lo[:, c], m.h_hi, m.h_lo).then_inc(a_mm, 1)

            def gates(r, n, first):
                q = (r - R_ROUNDS) * (TOK // QUAD) + n
                if not (first and n < 2):
                    pe.wait_ge(w_ok, q - 1)
                pe.wait_ge(hot_ok, q + 1)
                for j in range(QUAD):
                    for g in range(3):
                        mm = pe.matmul(psum[:, 2 + n % 2, j * P:(j + 1) * P], m.hot2[:, n % 2, :, j],
                                       m.hot1[:, n % 2, g, :, j], start=(g == 0), stop=(g == 2))
                mm.then_inc(w_mm, 1)

            tile(0, 0, True)
            tile(0, 1, True)
            with pe.Fori(1, R_ROUNDS) as r:
                for c in range(2):
                    tile(r, c)

            def turn(r):
                for c in range(2):
                    tile(r, c)
                    gates(r, 2 * c, False)
                    gates(r, 2 * c + 1, False)

            tile(R_ROUNDS, 0)
            pe.wait_ge(g_norm, 3)
            for n in range(3):
                for t in range(QT):
                    mm = pe.transpose(psum[:, 4 + n, t * P:(t + 1) * P], routed[:, n, t * P:(t + 1) * P], m.eye[:, :])
                mm.then_inc(slot_mm, 1)
            tile(R_ROUNDS, 1)
            for n in range(TOK // QUAD):
                gates(R_ROUNDS, n, n < 2)
            with pe.Fori(R_ROUNDS + 1, ROUNDS) as r:
                turn(r)


def combine(nc, io, m, psum):
    with ExitStack() as ctx:
        sb = m.scratch().take

        def sem(name):
            return ctx.enter_context(nc.semaphore(name))

        raw = m.v_raw
        hi = sb("v_hi", [P, 2, D], F32R)
        lo = sb("v_lo", [P, 2, D], F32R)
        acts, gates = m.acts_in, m.gates_in
        wa = sb("wa", [P, 2, S])
        wa_hi = sb("wa_hi", [P, 2, S], F32R)
        wa_lo = sb("wa_lo", [P, 2, S], F32R)
        early = m.early()
        x2 = early.take("x2_back", [P, QT, D])
        fg = early.take("final_gain", [P, D])
        junk = early.take("fjunk", [P, D])
        stat = early.take("fstat", [P, 4, QT])
        v_in, x2_in = m.v_in, sem("x2_in")
        ag_in = m.ag_in
        vhi_ok, vlo_ok, wa_ok, wahi_ok, walo_ok, o_mm = (
            sem("vhi_ok"), sem("vlo_ok"), sem("wa_ok"), sem("wahi_ok"), sem("walo_ok"), sem("o2_mm"))
        t_mm, f_add, f_sq, f_var, f_std, f_rs, f_ok, f_out = (
            sem("tile_mm"), sem("f_add"), sem("f_sq"), sem("f_var"), sem("f_std"), sem("f_rs"), sem("f_ok"), sem("f_out"))
        block = ctx.enter_context(nc.Block())

        @block.sync
        def _(sp):
            def load(r, c):
                sp.dma_start(raw[:, c, :], io.v[bass.ds(2 * r + c, 1)].rearrange("o p n -> p (o n)")
                             ).then_inc(v_in[c], 16)

            with sp.Fori(1, ROUNDS) as r:
                for c in range(2):
                    sp.wait_ge(vlo_ok, 2 * r - 1 + c)
                    load(r, c)
            sp.dma_start(x2[:, :, :], io.x2.rearrange("(t p) d -> p t d", p=P)).then_inc(x2_in, 16)
            sp.dma_start(fg[:, :], io.final_g.partition_broadcast(P)).then_inc(x2_in, 16)
            for t in range(QT):
                sp.wait_ge(f_ok, t + 1)
                sp.dma_start(io.out.rearrange("(t p) d -> t p d", p=P)[t], x2[:, t, :]).then_inc(f_out, 16)
            sp.wait_ge(f_out, 16 * QT)

        @block.gpsimd
        def _(pool):
            for c in range(2):
                pool.wait_ge(m.a_out[c], 16 * ROUNDS)
            pool.wait_ge(m.w_out[0], 16 * (2 * C_ROUNDS - 2))
            with pool.Fori(1, ROUNDS) as r:
                for c in range(2):
                    pool.wait_ge(wa_ok, 2 * r - 1 + c)
                    pool.dma_start(acts[:, c, :], io.acts[bass.ds(2 * r + c, 1)].rearrange("o p n -> p (o n)")
                                   ).then_inc(ag_in[c], 16)
                    pool.dma_start(gates[:, c, :],
                                   io.gates[bass.ds(2 * r + c, 1), :, 0:STORED].rearrange("o p n -> p (o n)")
                                   ).then_inc(ag_in[c], 16)

        @block.scalar
        def _(act):
            def split(r, c, first=False):
                act.wait_ge(v_in[c], 16 * r + 16)
                if not first:
                    act.wait_ge(o_mm, 2 * r - 1 + c)
                act.activation(hi[:, c, :], raw[:, c, :], ACT.Copy).then_inc(vhi_ok, 1)
                act.wait_ge(wa_ok, 2 * r + 1 + c)
                act.activation(wa_hi[:, c, :], wa[:, c, :], ACT.Copy).then_inc(wahi_ok, 1)

            split(0, 0, True)
            split(0, 1, True)
            with act.Fori(1, ROUNDS) as r:
                for c in range(2):
                    split(r, c)
            for t in range(QT):
                act.wait_ge(f_add, t + 1)
                if t:
                    act.wait_ge(f_sq, t)
                act.activation(junk[:, :], x2[:, t, :], ACT.Square, accum_out=stat[:, 0, t:t + 1]).then_inc(f_sq, 1)
                act.wait_ge(f_var, t + 1)
                act.activation(stat[:, 2, t:t + 1], stat[:, 1, t:t + 1], ACT.Sqrt).then_inc(f_std, 1)

        @block.vector
        def _(dve):
            def split(r, c, first=False):
                dve.wait_ge(ag_in[c], 32 * r + 32)
                if not first:
                    dve.wait_ge(walo_ok, 2 * r - 1 + c)
                    dve.wait_ge(wahi_ok, 2 * r - 1 + c)
                dve.tensor_tensor(wa[:, c, 0:STORED], acts[:, c, 0:STORED], gates[:, c, :], ALU.mult)
                dve.tensor_tensor(wa[:, c, STORED:S], acts[:, c, STORED:S],
                                  m.dense[:, (QT - 1) % 2, bass.ds(2 * r + c, 1), :].rearrange("p o t -> p (o t)"),
                                  ALU.mult).then_inc(wa_ok, 1)
                dve.wait_ge(vhi_ok, 2 * r + 1 + c)
                dve.tensor_tensor(lo[:, c, :], raw[:, c, :], hi[:, c, :].bitcast(F32), ALU.subtract).then_inc(vlo_ok, 1)
                dve.wait_ge(wahi_ok, 2 * r + 1 + c)
                dve.tensor_tensor(wa_lo[:, c, :], wa[:, c, :], wa_hi[:, c, :].bitcast(F32), ALU.subtract
                                  ).then_inc(walo_ok, 1)

            split(0, 0, True)
            split(0, 1, True)
            with dve.Fori(1, ROUNDS) as r:
                for c in range(2):
                    split(r, c)
            dve.wait_ge(x2_in, 32)

            def add(t):
                dve.wait_ge(t_mm, t + 1)
                xt = x2[:, t, :].rearrange("p (b n) -> p b n", b=2)
                dve.tensor_tensor(xt, psum[:, 2 * t:2 * t + 2, :], xt, ALU.add).then_inc(f_add, 1)

            add(0)
            for t in range(QT):
                if t + 1 < QT:
                    add(t + 1)
                dve.wait_ge(f_sq, t + 1)
                dve.tensor_scalar(stat[:, 1, t:t + 1], stat[:, 0, t:t + 1], 1.0 / D, EPS, ALU.mult, ALU.add
                                  ).then_inc(f_var, 1)
                dve.wait_ge(f_std, t + 1)
                dve.reciprocal(stat[:, 3, t:t + 1], stat[:, 2, t:t + 1]).then_inc(f_rs, 1)
                dve.wait_ge(f_rs, t + 1)
                dve.scalar_tensor_tensor(out=x2[:, t, :], in0=x2[:, t, :], scalar=stat[:, 3, t:t + 1], in1=fg[:, :],
                                         op0=ALU.mult, op1=ALU.mult).then_inc(f_ok, 1)

        @block.tensor
        def _(pe):
            def tile(r, c, first=False, last=False):
                pe.wait_ge(vlo_ok, 2 * r + 1 + c)
                pe.wait_ge(walo_ok, 2 * r + 1 + c)
                for t in range(QT):
                    ts = slice(t * P, (t + 1) * P)
                    for b in range(2):
                        bs = slice(b * S, (b + 1) * S)
                        for n, (w, v) in enumerate(((wa_hi, hi), (wa_hi, lo), (wa_lo, hi))):
                            mm = pe.matmul(psum[:, 2 * t + b, :], w[:, c, ts], v[:, c, bs],
                                           start=(first and n == 0), stop=(last and n == 2), skip_group_check=True)
                    if last:
                        mm.then_inc(t_mm, 1)
                if not last:
                    mm.then_inc(o_mm, 1)

            tile(0, 0, first=True)
            tile(0, 1)
            with pe.Fori(1, ROUNDS - 1) as r:
                for c in range(2):
                    tile(r, c)
            tile(ROUNDS - 1, 0)
            tile(ROUNDS - 1, 1, last=True)



def hymba_peer_layer(nc, io):
    KB = 1024
    m = Memory()
    base = (nc.sbuf_base + 63) // 64 * 64
    end = nc.sbuf_usable_end
    shared = base + 1 * KB
    late = shared + 32 * KB
    rows = late + 16 * KB
    rest = rows + 16 * KB

    top = Region(nc, base, shared)
    m.eye = top.take("eye", [P, P])
    m.iota = top.take("iota", [P, P])
    m.early = lambda: Region(nc, shared, late)
    m.late = lambda: Region(nc, late, rows)
    m.x = Region(nc, rows, rest).take("x_rows", [P, QT, D])
    kept = Region(nc, rest, end)
    m.mask = kept.take("mask", [P, S])
    m.seen = kept.take("seen", [P, 1])
    m.bias = kept.take("bias", [P, HEADS, BIAS_W])
    m.rows = kept.take("rows", [P, QT, ROW_W])
    m.kT = kept.take("kT", [P, 2, S])
    m.qT = kept.take("qT", [P, 4, S])
    m.kcT = kept.take("kcT", [P, N_CMP])
    m.vc = kept.take("vc", [N_CMP, GROUPS * DH])
    m.gate = kept.take("gate", [P, QT, 3 * HEADS])
    m.lstat = kept.take("lstat", [P, 3, 2 * QT])
    m.lsum = kept.take("lsum", [P, QT])
    m.inv = kept.take("inv", [P, HALF])
    m.pos = kept.take("pos", [P, QT], I32)
    values_at = kept.at
    m.mla_values = lambda: Region(nc, values_at, values_at + 8 * KB)
    m.vm = kept.take("vm", [P, QT, HEADS * DH])
    attend_free = kept.at
    m.wq_up = kept.take("wq_up", [P, 2, HEADS * QK])
    m.wkv_up = kept.take("wkv_up", [P, HEADS * (NOPE + DH)])
    m.latT = kept.take("latT", [P, 3, S])
    tail = end // 32 * 32 - 29 * KB
    last = Region(nc, tail, end)
    m.o_lo = last.take("o_lo", [P, KD, S], F32R)
    m.ssq = last.take("ssq", [P, 2, S])
    m.wo_raw = last.take("wo_raw", [P, 2, D])
    m.gain = last.take("gain", [P, 2, KD])

    with ExitStack() as own:
        psum = own.enter_context(nc.psum_tensor("psum", [P, 8, S], F32))
        m.wq_in = [own.enter_context(nc.semaphore("wq_in0")), own.enter_context(nc.semaphore("wq_in1"))]
        m.u_in = [own.enter_context(nc.semaphore("u_in0")), own.enter_context(nc.semaphore("u_in1"))]
        m.keys_in = own.enter_context(nc.semaphore("keys_in"))
        m.gain_in = own.enter_context(nc.semaphore("gain_in"))
        m.wo_in = [own.enter_context(nc.semaphore("wo_in0")), own.enter_context(nc.semaphore("wo_in1"))]
        m.scratch = lambda: Region(nc, kept.at, end)
        early = m.early()
        m.qmT = early.take("qmT", [QK, HEADS, S])
        m.kmT = early.take("kmT", [QK, HEADS, S])
        project(nc, io, m, psum)
        m.scratch = lambda: Region(nc, attend_free, tail)
        m.o_hi = m.late().take("o_hi", [P, KD, S], F32R)
        attend(nc, io, m, psum)
        parts = m.early()
        m.h_hi = parts.take("h_hi", [P, KD, S], F32R)
        m.h_lo = parts.take("h_lo", [P, KD, S], F32R)
        after = late + 2 * NKEYS * CHUNK * 4
        first = Region(nc, after, tail)
        m.wq_raw = first.take("wq_raw", [P, 2, KD, P])
        m.keys = first.take("keysT", [P, 2, NKEYS])
        m.scratch = lambda: Region(nc, rest, after)
        output(nc, io, m, psum)
        m.dense = Region(nc, late, after).take("dense", [P, 2, NKEYS, CHUNK])
        before = Region(nc, late, after)
        m.ps = before.take("peer_s", [P, QT * PH * 2, NKEYS])
        m.cur = before.take("cur", [P, 2, NKEYS])
        m.cur2 = before.take("cur2", [P, 2, NKEYS])
        m.best = before.take("best", [P, 2, TOPK])
        m.where = before.take("where", [P, 2, TOPK], U32)
        m.wheref = before.take("wheref", [P, 2, TOPK])
        m.cand = before.take("cand", [P, TOPK * TOPK])
        m.cand2 = before.take("cand2", [P, TOPK * TOPK])
        m.ctop = before.take("ctop", [P, TOPK])
        m.cpos = before.take("cpos", [P, TOPK], U32)
        m.rc = before.take("rc", [P, 2, TOPK], U32)
        m.rcf = before.take("rcf", [P, 2, TOPK])
        m.pause = before.take("pause", [P, 1])
        m.pick = before.take("pick", [P, 2, TOPK, TOPK])
        m.gsum = before.take("gsum", [P, 2, QT * PH])
        u_at = end // 32 * 32 - 8 * KB
        m.u_raw = Region(nc, u_at, end).take("u_raw", [P, 2, KD, P])
        m.scratch = lambda: Region(nc, first.at, u_at)
        peer_scores(nc, io, m, psum)
        slots = Region(nc, after, u_at)
        m.slot_key = slots.take("slot_key", [P, 2, S], BF16)
        m.slot_gate = slots.take("slot_gate", [P, 3, S], BF16)
        m.iota4 = slots.take("iota4", [P, NKEYS, QUAD], BF16)
        turned = Region(nc, slots.at, u_at)
        m.routed = turned.take("routed", [P, 3, S])
        m.slot_rest = turned.take("slot_rest", [P, S])
        m.is1 = slots.take("is1", [P, 2, NKEYS, QUAD], BF16)
        m.hot2 = slots.take("hot2", [P, 2, NKEYS, QUAD], BF16)
        m.hot1 = slots.take("hot1", [P, 2, 3, NKEYS, QUAD], BF16)
        ahead = Region(nc, late, after)
        m.v_raw = ahead.take("v_raw", [P, 2, D])
        m.acts_in = ahead.take("acts_in", [P, 2, S])
        m.gates_in = ahead.take("gates_in", [P, 2, STORED])
        m.a_out = [own.enter_context(nc.semaphore("a_out0")), own.enter_context(nc.semaphore("a_out1"))]
        m.w_out = [own.enter_context(nc.semaphore("w_out0")), own.enter_context(nc.semaphore("w_out1"))]
        m.ag_in = [own.enter_context(nc.semaphore("ag_in0")), own.enter_context(nc.semaphore("ag_in1"))]
        m.v_in = [own.enter_context(nc.semaphore("v_in0")), own.enter_context(nc.semaphore("v_in1"))]
        m.scratch = lambda: Region(nc, slots.at, u_at)
        experts(nc, io, m, psum)
        m.scratch = lambda: Region(nc, after, end)
        combine(nc, io, m, psum)


def bucket_onehot():
    dist = S - 1 - np.arange(BIAS_L)
    d = np.maximum(dist, 1).astype(np.float32)
    exact = BUCKETS // 2
    large = exact + (np.log(d / exact) / np.float32(np.log(2048 / exact)) * (BUCKETS - exact)).astype(np.int32)
    bucket = np.where(dist < exact, np.maximum(dist, 0), np.minimum(large, BUCKETS - 1))
    bucket = np.where(dist < 0, BUCKETS, bucket)
    return (np.arange(BUCKETS + 1)[:, None] == bucket[None, :]).astype(np.float32)


def layout(inputs):
    c = np.ascontiguousarray
    a = {k: np.asarray(v) for k, v in inputs.items()}

    def tiles(w):
        return c(w.reshape(-1, P, w.shape[1]).transpose(1, 0, 2))

    def column_tiles(w):
        return c(w.reshape(-1, P, w.shape[1] // P, P).transpose(2, 1, 0, 3))

    def hidden_tiles(w):
        t = column_tiles(w).reshape(HT, P, 2, LP // 2, P).transpose(0, 2, 1, 3, 4)
        return t.reshape(2 * HT, P, LP // 2, P)

    sizes = [NSA_W] + [GROUPS * DH] * 6 + [3 * HEADS, Q_LORA, KV_LORA, ROPE]
    cuts = np.split(a["w_in"][0], np.cumsum(sizes)[:-1], axis=1)
    q, kc, vc, ks, vs, kw, vw, gates, cq, ckv, kr = cuts
    q = q.reshape(D, GROUPS, HEADS // GROUPS, DH).transpose(0, 2, 1, 3).reshape(D, NSA_W)
    kv_up = a["w_kv_up"][0].reshape(KV_LORA, HEADS, 2, NOPE).transpose(0, 2, 1, 3).reshape(KV_LORA, -1)
    pairs = a["cmp_pos"][0].reshape(LP, P).T
    return {
        "x": c(a["x"].reshape(S, D)),
        "positions": c(a["positions"].reshape(QT, P).T),
        "g1": c(a["norm1_g"][0].reshape(KD, P).T),
        "qkvg": c(np.concatenate([a["q_norm_g"][0], a["kv_norm_g"][0]]).reshape(3, P).T),
        "cmp_posT": c(pairs),
        "w_rows": tiles(np.concatenate([cq, ckv, vs, vw, kr, gates], axis=1)),
        "w_cols": column_tiles(np.concatenate([kc, vc, ks, kw, q], axis=1)),
        "w1": c(np.concatenate([hidden_tiles(a["cmp_k_w1"][0]), hidden_tiles(a["cmp_v_w1"][0])])),
        "w2": c(np.stack([tiles(a["cmp_k_w2"][0]), tiles(a["cmp_v_w2"][0])], axis=1)),
        "t5": c(a["t5_bias"]),
        "bucket_onehot": bucket_onehot(),
        "inv_freq": (10000.0 ** (-np.arange(HALF, dtype=np.float32) / HALF)).astype(np.float32),
        "wq_up": tiles(a["w_q_up"][0]),
        "wkv_up": c(kv_up),
        "grp_gain": c(np.concatenate([a["grp_norm_nsa"][0], a["grp_norm_mla"][0]]).reshape(KD, P).T),
        "w_out": tiles(a["w_out"][0]),
        "g2": c(a["norm2_g"][0].reshape(KD, P).T),
        "wq": column_tiles(a["peer_wq"][0]),
        "keysT": c(np.stack([a["peer_keys1"][0].T, a["peer_keys2"][0].T], axis=1)),
        "uT": c(a["peer_u"][0].reshape(NKEYS, P, KD, P).transpose(0, 3, 2, 1)),
        "v": c(a["peer_v"][0].reshape(NKEYS, P, D)),
        "final_g": c(a["final_g"]),
    }


class Dram:

    def __init__(self, nc, arrays):
        def given(name):
            a = arrays[name]
            return nc.dram_tensor(name, a.shape, mybir.dt.from_np(a.dtype), kind="ExternalInput").ap()

        def scratch(name, shape):
            return nc.dram_tensor(name, shape, F32, kind="Internal").ap()

        self.x = given("x")
        self.positions = given("positions")
        self.g1 = given("g1")
        self.qkvg = given("qkvg")
        self.cmp_posT = given("cmp_posT")
        self.w_rows = given("w_rows")
        self.w_cols = given("w_cols")
        self.w1 = given("w1")
        self.w2 = given("w2")
        self.t5 = given("t5")
        self.bucket_onehot = given("bucket_onehot")
        self.inv_freq = given("inv_freq")
        self.wq_up = given("wq_up")
        self.wkv_up = given("wkv_up")
        self.grp_gain = given("grp_gain")
        self.w_out = given("w_out")
        self.g2 = given("g2")
        self.wq = given("wq")
        self.keysT = given("keysT")
        self.uT = given("uT")
        self.v = given("v")
        self.final_g = given("final_g")
        self.bias_rows = scratch("bias_rows", (HEADS, BIAS_L))
        self.bias_rep = scratch("bias_rep", (P, HEADS * BIAS_L))
        self.x2 = scratch("x2", (S, D))
        self.acts = scratch("acts", (NKEYS, P, S))
        self.gates = scratch("gates", (NKEYS, P, S))
        self.out = nc.dram_tensor("out", (S, D), F32, kind="ExternalOutput").ap()


def kernel(**inputs):
    import concourse.bacc as bacc
    from concourse.bass_utils import run_bass_kernel_spmd

    arrays = layout(inputs)
    nc = bacc.Bacc("TRN2", target_bir_lowering=False, num_devices=1)
    hymba_peer_layer(nc, Dram(nc, arrays))
    result = run_bass_kernel_spmd(nc, [arrays], core_ids=[0])
    return result.results[0]["out"].reshape(1, S, D)
```
